# Optimizing a Trainium2 kernel written in Bass

```python
import math
import jax, jax.numpy as jnp
from jax import lax
import numpy as np

D_MODEL = 2048
BATCH = 1
SEQ = 1024
DEPTH = 1

D_MIX = D_MODEL
D_A = D_MIX // 4
D_B = 3 * D_MIX // 8
D_C = D_MIX - D_A - D_B
POOL_WINDOWS = (2, 4, 8, 16)
N_POOL_GROUPS = len(POOL_WINDOWS)
POOL_GROUP_DIM = D_A // N_POOL_GROUPS
CHUNK = 128
SGU_HEAD_DIM = 128
SGU_HEADS = D_B // SGU_HEAD_DIM
CONV_WIDTH = 31
N_IN = D_A + 2 * D_B + 2 * D_C
N_GROUPS = 4
E_PER_GROUP = 8
N_EXPERTS = N_GROUPS * E_PER_GROUP
TOP_K = 2
D_EXPERT = D_MODEL // 4
MOE_BLOCK = 128
EPS = 1e-6

kernel_name = "hybrid_pool_sgu_conv_hmoe_block"

def rms_norm(x, g):
    xf = x.astype(jnp.float32)
    y = xf * lax.rsqrt(jnp.mean(xf * xf, axis=-1, keepdims=True) + EPS)
    return (y * g.astype(jnp.float32)).astype(x.dtype)

def layer_norm(x, g, b):
    xf = x.astype(jnp.float32)
    mu = jnp.mean(xf, axis=-1, keepdims=True)
    xc = xf - mu
    y = xc * lax.rsqrt(jnp.mean(xc * xc, axis=-1, keepdims=True) + EPS)
    return (y * g.astype(jnp.float32) + b.astype(jnp.float32)).astype(x.dtype)

def causal_mean(xg, w):
    s = xg.shape[1]
    cs = jnp.cumsum(xg, axis=1)
    prev = jnp.pad(cs[:, : s - w], ((0, 0), (w, 0), (0, 0)))
    cnt = jnp.minimum(jnp.arange(1, s + 1, dtype=jnp.float32), float(w))
    return (cs - prev) / cnt[None, :, None]

def pool_mixer(xa, pool_w, pool_scale):
    b, s, _ = xa.shape
    xf = xa.astype(jnp.float32).reshape(b, s, N_POOL_GROUPS, POOL_GROUP_DIM)
    diffs = []
    for gi, w in enumerate(POOL_WINDOWS):
        xg = xf[:, :, gi]
        diffs.append(causal_mean(xg, w) - xg)
    d = jnp.stack(diffs, axis=2).astype(xa.dtype)
    y = jnp.einsum('bsgc,gcd->bsgd', d, pool_w).reshape(b, s, D_A)
    return y * pool_scale

def sgu_mixer(xb, ln_g, ln_b, w_s, b_s):
    z = jax.nn.gelu(xb)
    u, v = jnp.split(z, 2, axis=-1)
    v = layer_norm(v, ln_g, ln_b)
    b, s, c = v.shape
    nc = s // CHUNK
    vh = v.reshape(b, nc, CHUNK, SGU_HEADS, SGU_HEAD_DIM)
    mask = jnp.tril(jnp.ones((CHUNK, CHUNK), dtype=w_s.dtype))
    gate = jnp.einsum('hts,bnshd->bnthd', w_s * mask, vh) + b_s.T[None, None, :, :, None]
    return u * gate.reshape(b, s, c)

def conv_mixer(xc, dw_w, dw_b, ln_g, ln_b, pw):
    a, g = jnp.split(xc, 2, axis=-1)
    z = a * jax.nn.sigmoid(g)
    k = dw_w[:, None, :]
    z = lax.conv_general_dilated(z, k, window_strides=(1,), padding=[(CONV_WIDTH - 1, 0)],
                                 dimension_numbers=('NWC', 'WIO', 'NWC'),
                                 feature_group_count=D_C) + dw_b
    z = jax.nn.silu(layer_norm(z, ln_g, ln_b))
    return z @ pw

def hier_moe(h, rg_w, rg_b, re_w, re_b, w1, w3, w2):
    b, s, d = h.shape
    t = b * s
    hf = h.reshape(t, d)
    lg = (hf @ rg_w + rg_b).astype(jnp.float32)
    pg = jax.nn.softmax(lg, axis=-1)
    g_idx = jnp.argmax(pg, axis=-1)
    g_w = jnp.take_along_axis(pg, g_idx[:, None], axis=-1)
    le = (hf @ re_w + re_b).astype(jnp.float32).reshape(t, N_GROUPS, E_PER_GROUP)
    le = jnp.take_along_axis(le, g_idx[:, None, None], axis=1)[:, 0]
    pe = jax.nn.softmax(le, axis=-1)
    top_p, top_i = lax.top_k(pe, TOP_K)
    wts = g_w * top_p / jnp.sum(top_p, axis=-1, keepdims=True)
    expert_ids = (g_idx[:, None] * E_PER_GROUP + top_i).reshape(-1).astype(jnp.int32)
    tok_ids = jnp.repeat(jnp.arange(t, dtype=jnp.int32), TOP_K)
    w_flat = wts.reshape(-1).astype(h.dtype)
    n_assign = t * TOP_K
    order = jnp.argsort(expert_ids)
    sorted_e = expert_ids[order]
    counts = jnp.bincount(expert_ids, length=N_EXPERTS)
    padded = ((counts + MOE_BLOCK - 1) // MOE_BLOCK) * MOE_BLOCK
    pend = jnp.cumsum(padded)
    pstart = pend - padded
    start = jnp.cumsum(counts) - counts
    dest = pstart[sorted_e] + (jnp.arange(n_assign, dtype=jnp.int32) - start[sorted_e])
    n_blocks = -(-n_assign // MOE_BLOCK) + N_EXPERTS
    p_len = n_blocks * MOE_BLOCK
    buf_tok = jnp.full((p_len,), t, dtype=jnp.int32).at[dest].set(tok_ids[order])
    buf_w = jnp.zeros((p_len,), dtype=h.dtype).at[dest].set(w_flat[order])
    starts = jnp.arange(n_blocks, dtype=jnp.int32) * MOE_BLOCK
    block_e = jnp.minimum(jnp.sum(pend[None, :] <= starts[:, None], axis=1), N_EXPERTS - 1)
    h_pad = jnp.concatenate([hf, jnp.zeros((1, d), hf.dtype)], axis=0)
    xb = h_pad[buf_tok].reshape(n_blocks, MOE_BLOCK, d)

    def expert_block(args):
        xblk, e = args
        return (jax.nn.silu(xblk @ w1[e]) * (xblk @ w3[e])) @ w2[e]

    yb = lax.map(expert_block, (xb, block_e)).reshape(p_len, d) * buf_w[:, None]
    out = jax.ops.segment_sum(yb, buf_tok, num_segments=t + 1)[:t]
    return out.reshape(b, s, d)

def setup_inputs(seed: int = 0) -> dict:
    key = jax.random.key(seed)
    ks = jax.random.split(key, 24)
    L, D = DEPTH, D_MODEL
    f32 = jnp.float32

    def nrm(k, shape, scale):
        return jax.random.normal(k, shape, f32) * scale

    def gain(k, shape):
        return 1.0 + 0.1 * jax.random.normal(k, shape, f32)

    return {
        "x": jax.random.normal(ks[0], (BATCH, SEQ, D), f32),
        "norm_mix": gain(ks[1], (L, D)),
        "w_in": nrm(ks[2], (L, D, N_IN), D ** -0.5),
        "pool_w": nrm(ks[3], (L, N_POOL_GROUPS, POOL_GROUP_DIM, POOL_GROUP_DIM), POOL_GROUP_DIM ** -0.5),
        "pool_scale": gain(ks[4], (L, D_A)),
        "sgu_ln_g": gain(ks[5], (L, D_B)),
        "sgu_ln_b": nrm(ks[6], (L, D_B), 0.02),
        "sgu_w": nrm(ks[7], (L, SGU_HEADS, CHUNK, CHUNK), CHUNK ** -0.5),
        "sgu_b": gain(ks[8], (L, SGU_HEADS, CHUNK)),
        "conv_dw_w": nrm(ks[9], (L, CONV_WIDTH, D_C), CONV_WIDTH ** -0.5),
        "conv_dw_b": nrm(ks[10], (L, D_C), 0.02),
        "conv_ln_g": gain(ks[11], (L, D_C)),
        "conv_ln_b": nrm(ks[12], (L, D_C), 0.02),
        "conv_pw": nrm(ks[13], (L, D_C, D_C), D_C ** -0.5),
        "w_out": nrm(ks[14], (L, D_MIX, D), D_MIX ** -0.5),
        "norm_ffn": gain(ks[15], (L, D)),
        "router_g_w": nrm(ks[16], (L, D, N_GROUPS), D ** -0.5),
        "router_g_b": nrm(ks[17], (L, N_GROUPS), 0.01),
        "router_e_w": nrm(ks[18], (L, D, N_EXPERTS), D ** -0.5),
        "router_e_b": nrm(ks[19], (L, N_EXPERTS), 0.01),
        "exp_w1": nrm(ks[20], (L, N_EXPERTS, D, D_EXPERT), D ** -0.5),
        "exp_w3": nrm(ks[21], (L, N_EXPERTS, D, D_EXPERT), D ** -0.5),
        "exp_w2": nrm(ks[22], (L, N_EXPERTS, D_EXPERT, D), D_EXPERT ** -0.5),
        "norm_final": gain(ks[23], (D,)),
    }

def reference(x, norm_mix, w_in, pool_w, pool_scale, sgu_ln_g, sgu_ln_b, sgu_w, sgu_b,
              conv_dw_w, conv_dw_b, conv_ln_g, conv_ln_b, conv_pw, w_out, norm_ffn,
              router_g_w, router_g_b, router_e_w, router_e_b, exp_w1, exp_w3, exp_w2,
              norm_final):
    for l in range(DEPTH):
        h = rms_norm(x, norm_mix[l])
        proj = h @ w_in[l]
        xa = proj[..., :D_A]
        xb = proj[..., D_A:D_A + 2 * D_B]
        xc = proj[..., D_A + 2 * D_B:]
        ya = pool_mixer(xa, pool_w[l], pool_scale[l])
        yb = sgu_mixer(xb, sgu_ln_g[l], sgu_ln_b[l], sgu_w[l], sgu_b[l])
        yc = conv_mixer(xc, conv_dw_w[l], conv_dw_b[l], conv_ln_g[l], conv_ln_b[l], conv_pw[l])
        y = jnp.concatenate([ya, yb, yc], axis=-1) @ w_out[l]
        x = x + y
        h2 = rms_norm(x, norm_ffn[l])
        x = x + hier_moe(h2, router_g_w[l], router_g_b[l], router_e_w[l], router_e_b[l],
                         exp_w1[l], exp_w3[l], exp_w2[l])
    return rms_norm(x, norm_final)


_drawn_inputs = setup_inputs


def setup_inputs(seed=0):
    import zlib

    import numpy as np

    out = dict(_drawn_inputs(seed))
    spreads = {}
    factors = {'sgu_ln_b': 5.693,
     'conv_dw_b': 3.091,
     'conv_ln_b': 4.47,
     'router_g_b': 6.231,
     'router_e_b': 4.688}
    for name, (base, spread) in spreads.items():
        noise = np.random.default_rng([zlib.crc32(name.encode()), seed]).standard_normal(out[name].shape)
        drawn = base * np.exp(spread * noise) if base else spread * noise
        out[name] = __import__('jax').numpy.asarray(drawn.astype(out[name].dtype))
    for name, factor in factors.items():
        out[name] = (out[name] * factor).astype(out[name].dtype)
    return out
```

```python
from contextlib import ExitStack

import concourse.bass as bass
from concourse import mybir

F32 = mybir.dt.float32
F32R = mybir.dt.float32r
I32 = mybir.dt.int32
U32 = mybir.dt.uint32
ALU = mybir.AluOpType
ACT = mybir.ActivationFunctionType
AX = mybir.AxisListType

P = 128
BANK = 512
S, D = 1024, 2048
KD = D // P
DA, DB, DC = 512, 768, 768
KB = DB // P
POOLS = 4
TAPS = 31
LEAD = TAPS - 1
HALF = 512
HALVES = S // HALF
TT = HALF // P
PLEAD = 16
G, EG = 4, 8
E = G * EG
FE = D // 4
KF = FE // P
EPS = 1e-6

CHUNK = 2048
UNIT = CHUNK // 2
RAW = 4
SPLIT = 4
NIN = (DA + 2 * DB + 2 * DC) // P
NOUT = KD * D // CHUNK
CH = NIN + NOUT
UH = 2 * CH
CM = HALVES * CH
NW = 8
NE = NW + 4
CX = CM + E * NE
EXTRA = 15
PADS = 4096
LISTED = 1024

FREE_UNITS = SPLIT
FREE_RAW = 2 * RAW
FREE_BANK = 1
FREE_GROUPS = 2
FREE_BLOCKS = 8
STEPS = 122


def build(nc, x, norm_mix, w_in, pool_w, pool_scale, sgu_ln_g, sgu_ln_b, sgu_w, sgu_b, conv_dw_w,
          conv_dw_b, conv_ln_g, conv_ln_b, conv_pw, w_out, norm_ffn, router_g_w, router_g_b,
          router_e_w, router_e_b, exp_w1, exp_w3, exp_w2, norm_final, out):
    x = x[0]
    out = out[0]
    w_in = w_in[0]
    x1_d = nc.dram_tensor("x1_d", (S, D), F32, kind="Internal").ap()
    h2_d = nc.dram_tensor("h2_d", (S, D), F32, kind="Internal").ap()
    yd = nc.dram_tensor("yd", (2 * S, D), F32, kind="Internal").ap()
    list_d = nc.dram_tensor("list_d", (E * LISTED, 1), I32, kind="Internal").ap()
    extra_d = nc.dram_tensor("extra_d", (2, 16), I32, kind="Internal").ap()

    ctx = ExitStack()
    with ctx:
        part = [ctx]

        def sb(name, shape, dt=F32):
            return part[0].enter_context(nc.sbuf_tensor(name, shape, dt))

        def sem(name):
            return ctx.enter_context(nc.semaphore(name))

        ps = ctx.enter_context(nc.psum_tensor("ps", [P, 8, BANK], F32))

        raw = sb("raw", [P, RAW, CHUNK])
        w_hi = sb("w_hi", [P, SPLIT, UNIT], F32R)
        w_lo = sb("w_lo", [P, SPLIT, UNIT], F32R)
        ident = sb("ident", [P, P])
        wts = sb("wts", [P, S // P, 2])
        carry = sb("carry", [P, E])
        n_extra = sb("n_extra", [P, 1], I32)
        eps_t = sb("eps_t", [P, 1])

        p1 = ExitStack()
        part[0] = p1
        act_hi = sb("act_hi", [P, KD, HALF], F32R)
        act_lo = sb("act_lo", [P, KD, HALF], F32R)
        mid = sb("mid", [P, KD, HALF])
        zv = sb("zv", [P, KB * (HALF + 32)])
        zc = sb("zc", [P, KB, HALF])
        pw = sb("pw", [P, 2, KB, P])
        pool_wt = sb("pool_wt", [P, POOLS, P])
        chan = sb("chan", [P, KB, TAPS + 3])
        pscale = sb("pscale", [P, POOLS])
        ln_g = sb("ln_g", [P, KB, P])
        ln_b = sb("ln_b", [P, KB, P])
        wmT = sb("wmT", [P, KB, P])
        gate_b = sb("gate_b", [P, KB, P])
        rw = sb("rw", [P, KD, G + E])
        rb = sb("rb", [P, G + E])
        mean1 = sb("mean1", [P, P])
        tri = sb("tri", [P, P])
        ones = sb("ones", [P, P])
        inv = sb("inv", [P, POOLS, PLEAD])
        halo_z = sb("halo_z", [P, KB, LEAD])
        halo_x = sb("halo_x", [P, POOLS, PLEAD - 1])
        ss = sb("ss", [P, 8])
        ms = sb("ms", [P, 8])
        std = sb("std", [P, 8])
        rstd = sb("rstd", [P, 8])
        vstat = sb("vstat", [P, TT, 6 * 2])
        vmean = sb("vmean", [P, TT, 2])
        vstd = sb("vstd", [P, TT])
        vrstd = sb("vrstd", [P, TT])
        iota_g = sb("iota_g", [P, G])
        iota_e = sb("iota_e", [P, E])
        iota_l = sb("iota_l", [P, E])
        asg_f = sb("asg_f", [P, TT, 2])
        asg_i = sb("asg_i", [P, TT, 2], I32)
        dest_i = sb("dest_i", [P, TT, 2], I32)

        xt = [mid[:, 4 * t:4 * t + 4, :].rearrange("p a b -> p (a b)") for t in range(TT)]
        xa, uT, vT = mid[:, 0:4, :], mid[:, 4:10, :], mid[:, 10:16, :]
        sig = [mid[:, 10 + j, :] for j in range(2)]
        ext, sums = (mid[:, 12:16, :].rearrange("p a b -> p (a b)")[:, k * 528:(k + 1) * 528]
                     for k in range(2))
        sums2 = mid[:, 12:16, :].rearrange("p a b -> p (a b)")[:, 2 * 528:3 * 528]
        z = zv[:, :].rearrange("p (j t) -> p j t", j=KB)
        scratch = zv[:, 0:D]
        gain = zc[:, 0:4, :].rearrange("p a b -> p (a b)")
        tgrp = [zc[:, 4 + k, :] for k in range(2)]
        at = [D]

        def small(*shape):
            n = 1
            for v in shape:
                n *= v
            v = zv[:, at[0]:at[0] + n]
            at[0] += n
            assert at[0] <= KB * (HALF + 32)
            if len(shape) == 2:
                v = v.rearrange("p (a b) -> p a b", b=shape[1])
            if len(shape) == 3:
                v = v.rearrange("p (a b c) -> p a b c", b=shape[1], c=shape[2])
            return v

        lg = small(TT, 8)
        le = small(TT, E)
        top_g, top_e = small(TT, 8), small(TT, 8)
        idx_g, idx_e = small(TT, 8), small(TT, 8)
        gf, onehot_g = small(TT), small(TT, G)
        le8, prod8 = small(TT, 8), small(TT, 8)
        sh_g, sh_e = small(TT, G), small(TT, 8)
        ex_g, ex_e = small(TT, G), small(TT, 8)
        sum_g, sum_e, sum_p = small(TT), small(TT), small(TT)
        wk = small(TT, 2)
        ef, ge = small(TT, 2), small(TT)
        hot = small(TT, 2, E)
        both = small(TT, E)
        rank = small(TT, E)
        hot_rank = le
        dest_f = small(TT, 2)

        p1.close()
        p2 = ExitStack()
        part[0] = p2
        xg = sb("xg", [P, D])
        xT_hi = sb("xT_hi", [P, KD, P], F32R)
        xT_lo = sb("xT_lo", [P, KD, P], F32R)
        silu = sb("silu", [P, FE])
        hid = sb("hid", [P, FE])
        hT_hi = sb("hT_hi", [P, KF, P], F32R)
        hT_lo = sb("hT_lo", [P, KF, P], F32R)
        yb = sb("yb", [P, D])
        lst_i = sb("lst_i", [E, P], I32)
        lst_f = sb("lst_f", [E, P])
        slot_i = sb("slot_i", [P, E], I32)
        tok_i = sb("tok_i", [P, E], I32)
        ix_tok = sb("ix_tok", [P, 1], I32)
        ix_asg = sb("ix_asg", [P, 1], I32)
        ix_new = sb("ix_new", [P, 1], I32)
        over = sb("over", [P, 7, E])
        cum = sb("cum", [P, 7, E])
        allone = sb("allone", [P, 7 * E])
        code = sb("code", [P, 2, 7, E])
        iota_1 = sb("iota_1", [P, 1])
        tab_f = sb("tab_f", [P, 2])
        tab_i = sb("tab_i", [P, 2], I32)
        row_i = sb("row_i", [1, 2, 16], I32)
        gfin = sb("gfin", [P, D])
        xb = sb("xb", [P, 2, D])
        ye = sb("ye", [P, 2, 2, D])
        fst = sb("fst", [P, 2, 4])
        wcol = sb("wcol", [P, 2, 2])
        p2.close()

        raw_landed = [sem(f"raw_landed{i}") for i in range(RAW)]
        hi_ready = sem("hi_ready")
        lo_ready = sem("lo_ready")
        unit_done = sem("unit_done")
        const_in = sem("const_in")
        const_set = sem("const_set")
        const_tr = sem("const_tr")
        const_ev = sem("const_ev")
        dve_set = sem("dve_set")
        waited = sem("waited")
        x_landed = [sem(f"x_landed{t}") for t in range(TT)]
        gain_landed = sem("gain_landed")
        a_ss, a_ms, a_std, a_rstd, a_xn = (sem(n) for n in ("a_ss", "a_ms", "a_std", "a_rstd", "a_xn"))
        a_tr, a_hi, a_lo = sem("a_tr"), sem("a_hi"), sem("a_lo")
        bank_read = [sem("bank_read0"), sem("bank_read1")]
        step = sem("step")
        tap = sem("tap")
        pool_d = sem("pool_d")
        pool_mm, pool_y = sem("pool_mm"), sem("pool_y")
        v_tr, v_tok, v_var, v_std, v_ln = (sem(n) for n in ("v_tr", "v_tok", "v_var", "v_std", "v_ln"))
        gate_mm, gated = sem("gate_mm"), sem("gated")
        c_mean, c_cent, c_sq, c_var, c_std, c_norm, c_act = (
            sem(n) for n in ("c_mean", "c_cent", "c_sq", "c_var", "c_std", "c_norm", "c_act"))
        pw_landed = [sem("pw_landed0"), sem("pw_landed1")]
        pw_mm = sem("pw_mm")
        y_hi, y_lo = sem("y_hi"), sem("y_lo")
        x1_part = sem("x1_part")
        r_ss, r_ms, r_std, r_rstd, r_xn = (sem(n) for n in ("r_ss", "r_ms", "r_std", "r_rstd", "r_xn"))
        r_tr, r_grp, r_lg = sem("r_tr"), sem("r_grp"), sem("r_lg")
        r_shift, r_exp, r_hot, r_rank, r_dest = (
            sem(n) for n in ("r_shift", "r_exp", "r_hot", "r_rank", "r_dest"))
        x1_stored, h2_stored, listed = sem("x1_stored"), sem("h2_stored"), sem("listed")
        list_blank = sem("list_blank")
        list_in, list_f, list_tr, slots = sem("list_in"), sem("list_f"), sem("list_tr"), sem("slots")
        tab_ready, tab_out, tab_in, count_ready = (
            sem(n) for n in ("tab_ready", "tab_out", "tab_in", "count_ready"))
        m_zero, m_ix, m_gathered = sem("m_zero"), sem("m_ix"), sem("m_gathered")
        m_xtr, m_xhi, m_xlo = sem("m_xtr"), sem("m_xhi"), sem("m_xlo")
        m_silu, m_hid, m_htr, m_hhi, m_hlo = (
            sem(n) for n in ("m_silu", "m_hid", "m_htr", "m_hhi", "m_hlo"))
        m_y, m_ystored, m_yfree = sem("m_y"), sem("m_ystored"), sem("m_yfree")
        e_list, e_tok = sem("e_list"), sem("e_tok")
        f_landed = [sem("f_landed0"), sem("f_landed1")]
        f_gain = sem("f_gain")
        f_col, f_sum, f_sq, f_ms, f_std, f_rstd, f_out = (
            sem(n) for n in ("f_col", "f_sum", "f_sq", "f_ms", "f_std", "f_rstd", "f_out"))
        f_stored = [sem("f_stored0"), sem("f_stored1")]

        block = ctx.enter_context(nc.Block())


        def unit_free(turn, c, j):
            return 8 * turn + 2 * c + j + 1

        def multiplied(turn, c):
            return 8 * turn + 2 * c + FREE_UNITS

        def split_of(turn, c, j):
            return 8 * turn + 2 * c + j + 1 + FREE_RAW

        def half_turn(h):
            return h * (CH // RAW)

        def apart(engine):
            engine.sem_inc(waited, 1)

        OUT_TURN = NIN // RAW
        EXP_TURN = CM // RAW
        LOOP_TURN = EXP_TURN + NW // RAW
        LAST_TURN = CX // RAW - 1
        EXTRA_TURN = CX // RAW

        @block.sync
        def _(sp):
            def load(turn, c, source):
                sp.wait_ge(lo_ready, 8 * turn + 2 * c + 2)
                n = source.shape[-1]
                sp.dma_start(raw[:, c % RAW, :].rearrange("p (a b) -> p a b", b=n), source)\
                  .then_inc(raw_landed[c % RAW], 16)

            def w_in_tile(col):
                return w_in[:, bass.ds(col, P)].rearrange("(k p) n -> p k n", p=P)

            def load_up(turn, e):
                for c in range(NW):
                    w = (exp_w1 if c < 4 else exp_w3)[0]
                    v = w[bass.ds(e, 1), (c % 4) * 4 * P:(c % 4 + 1) * 4 * P, :]
                    load(turn, c, v.rearrange("e (k p) n -> p (e k) n", p=P))

            def load_down(turn, e):
                for f in range(KF):
                    load(turn, f, exp_w2[0][bass.ds(e, 1), f * P:(f + 1) * P, :].rearrange("e p n -> p e n"))

            with sp.Fori(0, HALVES) as h:
                with sp.Fori(0, KB // 2) as i:
                    for m in range(4):
                        col = DA + 2 * DB + (DC if m % 2 == 0 else 0) + (m // 2) * P
                        load(half_turn(h) + i, m, w_in_tile(i * (2 * P) + col))
                for c in range(12, NIN):
                    col = (c - 12) * P if c < 16 else DA + (DB if c < 22 else 0) + (c - 16) % KB * P
                    load(half_turn(h), c, w_in[:, col:col + P].rearrange("(k p) n -> p k n", p=P))
                with sp.Fori(0, D // BANK) as n:
                    for g in range(4):
                        v = w_out[0][g * 4 * P:(g + 1) * 4 * P, bass.ds(n * BANK, BANK)]
                        load(half_turn(h) + OUT_TURN + n, g, v.rearrange("(k p) n -> p k n", p=P))
            load_up(EXP_TURN, 0)
            with sp.Fori(0, E - 1) as i:
                load_up(LOOP_TURN + 3 * i, i + 1)
                load_down(LOOP_TURN + 3 * i + 2, i)
            load_down(LAST_TURN, E - 1)
            sp.wait_ge(count_ready, 1)
            n = sp.value_load(n_extra[0:1, 0:1], min_val=0, max_val=EXTRA)
            sp.wait_ge(tab_in, 32)
            with sp.Fori(0, EXTRA) as i:
                with sp.If(i < n):
                    e = sp.value_load(row_i[0:1, 1, bass.ds(i, 1)], min_val=0, max_val=E - 1)
                    load_up(EXTRA_TURN + 3 * i, e)
                    load_down(EXTRA_TURN + 3 * i + 2, e)
                    sp.nop()
            sp.wait_ge(m_yfree, n + (E + 1))

            def load_tile(i, k):
                sp.dma_start(xb[:, k, :], x1_d[bass.ds((2 * i + k) * P, P), :]).then_inc(f_landed[k], 16)
                rows = yd[bass.ds((2 * i + k) * (2 * P), 2 * P), :]
                sp.dma_start(ye[:, k, :, :], rows.rearrange("(p a) n -> p a n", a=2)).then_inc(f_landed[k], 16)

            for k in range(2):
                load_tile(0, k)
            with sp.Fori(1, S // P // 2) as i:
                for k in range(2):
                    sp.wait_ge(f_stored[k], 16 * i)
                    load_tile(i, k)

        @block.gpsimd
        def _(pool):
            pool.sem_inc(m_yfree, 1)

            def const(to, source):
                pool.dma_start(to, source).then_inc(const_in, 16)
                n_const[0] += 1

            n_const = [0]
            names = zv[0:TAPS + 3, 0:DC]
            const(names[0:TAPS, :], conv_dw_w[0])
            for r, v in enumerate((conv_dw_b, conv_ln_g, conv_ln_b)):
                const(names[TAPS + r:TAPS + r + 1, :], v)
            const(zv[0:POOLS, DC:DC + P], pool_scale[0].rearrange("(g c) -> g c", c=P))
            wnat = zv[:, 1024:1024 + DB].rearrange("p (j s) -> p j s", j=KB)
            const(wnat, sgu_w[0].rearrange("j t s -> t j s"))
            const(pool_wt[:, :, :], pool_w[0].rearrange("g c d -> c g d"))
            const(ln_g[:, :, :].rearrange("p a b -> p (a b)"), sgu_ln_g.to_broadcast([P, DB]))
            const(ln_b[:, :, :].rearrange("p a b -> p (a b)"), sgu_ln_b.to_broadcast([P, DB]))
            const(gate_b[:, :, :].rearrange("p a b -> p (a b)"),
                  sgu_b.rearrange("o j t -> o (j t)").to_broadcast([P, KB * P]))
            const(rw[:, :, 0:G], router_g_w[0].rearrange("(k p) n -> p k n", p=P))
            const(rw[:, :, G:], router_e_w[0].rearrange("(k p) n -> p k n", p=P))
            const(rb[:, 0:G], router_g_b.to_broadcast([P, G]))
            const(rb[:, G:], router_e_b.to_broadcast([P, E]))

            pool.memset(ident[:, :], 0.0).then_inc(const_set, 1)
            pool.memset(tri[:, :], 1.0).then_inc(const_set, 1)
            blank = xt[3].bitcast(I32)[:, 0:E * LISTED // P]
            pool.memset(blank, PADS).then_inc(const_set, 1)
            pool.wait_ge(const_set, 3)
            pool.dma_start(list_d.rearrange("(p n) o -> p (n o)", p=P), blank).then_inc(list_blank, 16)
            pool.affine_select(out=ident[:, :], in_=ident[:, :], compare_op=ALU.not_equal, fill=1.0, base=0,
                               pattern=[[-1, P]], channel_multiplier=1).then_inc(const_set, 1)
            pool.affine_select(out=tri[:, :], in_=tri[:, :], compare_op=ALU.is_gt, fill=0.0, base=0,
                               pattern=[[1, P]], channel_multiplier=-1).then_inc(const_set, 1)
            pool.wait_ge(const_in, 16 * n_const[0])
            pool.affine_select(out=wnat, in_=wnat, compare_op=ALU.is_ge, fill=0.0, base=0,
                               pattern=[[0, KB], [-1, P]], channel_multiplier=1).then_inc(const_set, 1)
            for to, pattern, base, mult in (
                    (iota_g[:, :], [[1, G]], 0, 0), (iota_e[:, :], [[1, E]], 0, 0),
                    (iota_l[:, :], [[LISTED, E]], 0, 0),
                    (asg_f[:, :, :], [[2 * P, TT], [1, 2]], 0, 2),
                    (inv[:, :, :], [[0, POOLS], [1, PLEAD]], 1, 0)):
                pool.iota(to, pattern, base=base, channel_multiplier=mult,
                          allow_small_or_imprecise_dtypes=True).then_inc(const_set, 1)
            pool.wait_ge(list_blank, 16)

            with pool.Fori(0, HALVES) as h:
                def rows(t):
                    return bass.ds(h * HALF + t * P, P)

                pool.dma_start(xt[0], x[rows(0), :]).then_inc(x_landed[0], 16)
                pool.dma_start(gain, norm_mix.to_broadcast([P, D])).then_inc(gain_landed, 16)
                for t in range(1, TT):
                    pool.dma_start(xt[t], x[rows(t), :]).then_inc(x_landed[t], 16)
                for n in range(KB):
                    if n >= 2:
                        pool.wait_ge(pw_mm, h * KB + n - 1)
                        apart(pool)
                    pool.dma_start(pw[:, n % 2, :, :],
                                   conv_pw[0, :, n * P:(n + 1) * P].rearrange("(k p) n -> p k n", p=P))\
                        .then_inc(pw_landed[n % 2], 16)
                pool.wait_ge(pw_mm, h * KB + KB)
                apart(pool)
                pool.dma_start(gain, norm_ffn.to_broadcast([P, D])).then_inc(gain_landed, 16)
                pool.wait_ge(y_lo, h * KD + KD)
                apart(pool)
                for t in range(TT):
                    pool.dma_start(xt[t], x[rows(t), :]).then_inc(x_landed[t], 16)
                for t in range(TT):
                    pool.wait_ge(r_xn, h * TT + t + 1)
                    apart(pool)
                    pool.dma_start(x1_d[rows(t), :], xt[t]).then_inc(x1_stored, 16)
                    pool.dma_start(h2_d[rows(t), :], scratch).then_inc(h2_stored, 16)
                    pool.wait_ge(h2_stored, h * (16 * TT) + 16 * (t + 1))
                pool.wait_ge(r_dest, h + 1)
                apart(pool)
                for t in range(TT):
                    for k in range(2):
                        index = dest_i[:, t, k:k + 1].bitcast(U32)
                        pool.indirect_dma_start(list_d, bass.IndirectOffsetOnAxis(ap=index, axis=0),
                                                asg_i[:, t, k:k + 1], None,
                                                bounds_check=E * LISTED - 1, oob_is_err=False)\
                            .then_inc(listed, 16)
                pool.wait_ge(listed, h * (32 * TT) + 32 * TT)
                pool.wait_ge(x1_stored, h * (16 * TT) + 16 * TT)
                apart(pool)

            pool.dma_start(lst_i[:, :], list_d.rearrange("(e n) o -> e (n o)", e=E)[:, 0:P]).then_inc(list_in, 16)
            pool.memset(xg[:, :], 0.0).then_inc(m_zero, 1)
            pool.memset(allone[:, :], 1.0).then_inc(m_zero, 1)
            pool.iota(iota_1[:, :], [[0, 1]], base=1, channel_multiplier=1,
                      allow_small_or_imprecise_dtypes=True).then_inc(m_zero, 1)
            pool.iota(code[:, 0, :, :], [[1, 7], [EG, E]], base=1, channel_multiplier=0,
                      allow_small_or_imprecise_dtypes=True).then_inc(m_zero, 1)
            pool.iota(code[:, 1, :, :], [[0, 7], [1, E]], base=0, channel_multiplier=0,
                      allow_small_or_imprecise_dtypes=True).then_inc(m_zero, 1)
            pool.dma_start(gfin[:, :], norm_final.rearrange("(o n) -> o n", o=1).to_broadcast([P, D]))\
                .then_inc(f_gain, 16)

            def gather(i, index):
                pool.indirect_dma_start(xg[:, :], None, h2_d,
                                        bass.IndirectOffsetOnAxis(ap=index.bitcast(U32), axis=0),
                                        bounds_check=S - 1, oob_is_err=False).then_inc(m_gathered, 16)
                pool.wait_ge(m_gathered, 16 * i + 16)
                apart(pool)

            def scatter(i):
                pool.wait_ge(m_y, 4 * i + 4 + FREE_BANK)
                apart(pool)
                index = ix_asg[:, :].bitcast(U32)
                pool.indirect_dma_start(yd, bass.IndirectOffsetOnAxis(ap=index, axis=0), yb[:, :], None,
                                        bounds_check=2 * S - 1, oob_is_err=False).then_inc(m_ystored, 16)
                pool.wait_ge(m_ystored, 16 * i + 16)
                apart(pool)
                pool.sem_inc(m_yfree, 1)

            pool.wait_ge(slots, 2)
            pool.wait_ge(m_zero, 5)
            for i in range(2):
                if i:
                    pool.wait_ge(m_xtr, 4)
                pool.tensor_copy(ix_tok[:, :], tok_i[:, i:i + 1]).then_inc(m_ix, 1)
                pool.wait_ge(m_ix, i + 1)
                gather(i, ix_tok[:, :])
            pool.wait_ge(tab_ready, 1)
            for r in range(2):
                pool.dma_start(extra_d[r, :].rearrange("(n o) -> n o", o=1), tab_i[0:16, r:r + 1])\
                    .then_inc(tab_out, 16)
            pool.wait_ge(tab_out, 32)
            for r in range(2):
                pool.dma_start(row_i[0:1, r, :], extra_d[r:r + 1, :]).then_inc(tab_in, 16)
            with pool.Fori(0, E - 2) as i:
                pool.wait_ge(m_xtr, 4 * i + 8)
                pool.tensor_copy(ix_tok[:, :], tok_i[:, bass.ds(i + 2, 1)]).then_inc(m_ix, 1)
                pool.wait_ge(m_ix, 2 * i + 3)
                apart(pool)
                gather(i + 2, ix_tok[:, :])
                pool.tensor_copy(ix_asg[:, :], slot_i[:, bass.ds(i, 1)]).then_inc(m_ix, 1)
                pool.wait_ge(m_ix, 2 * i + 4)
                scatter(i)
            for i in (E - 2, E - 1):
                pool.tensor_copy(ix_asg[:, :], slot_i[:, i:i + 1]).then_inc(m_ix, 1)
                pool.wait_ge(m_ix, E + i + 1)
                scatter(i)
            pool.wait_ge(count_ready, 1)
            n = pool.value_load(n_extra[0:1, 0:1], min_val=0, max_val=EXTRA)
            pool.wait_ge(tab_in, 32)
            with pool.Fori(0, EXTRA) as i:
                with pool.If(i < n):
                    r = pool.value_load(row_i[0:1, 0, bass.ds(i, 1)], min_val=0, max_val=E * EG - 1)
                    pool.dma_start(ix_asg[:, :], list_d[bass.ds(r * P, P), :]).then_inc(e_list, 16)
                    pool.wait_ge(e_list, 16 * i + 16)
                    pool.wait_ge(e_tok, i + 1)
                    apart(pool)
                    gather(i + E, ix_new[:, :])
                    scatter(i + E)

        @block.scalar
        def _(act):
            act.sem_inc(m_y, FREE_BANK)
            act.sem_inc(bank_read[0], FREE_BANK)
            act.sem_inc(r_grp, FREE_GROUPS)
            act_fn = nc.scalar.activation

            def hi(turn, c):
                act.wait_ge(raw_landed[c % RAW], 16 * (turn + c // RAW + 1))
                for j in range(2):
                    act.wait_ge(unit_done, unit_free(turn, c, j))
                    act_fn(w_hi[:, (2 * c + j) % SPLIT, :], raw[:, c % RAW, j * UNIT:(j + 1) * UNIT],
                           ACT.Copy).then_inc(hi_ready, 1)

            act.wait_ge(const_tr, 2 * KB + 1)
            NC = TAPS + 3
            act_fn(chan[:, :, :].rearrange("p a b -> p (a b)"), ps[:, 0, 0:KB * NC], ACT.Copy).then_inc(const_ev, 1)
            act_fn(pscale[:, :], ps[:, 0, KB * NC:KB * NC + POOLS], ACT.Copy).then_inc(const_ev, 1)
            act_fn(wmT[:, 0:4, :], ps[:, 1, :].rearrange("p (a b) -> p a b", a=4), ACT.Copy).then_inc(const_ev, 1)
            act_fn(wmT[:, 4:6, :], ps[:, 2, 0:2 * P].rearrange("p (a b) -> p a b", a=2), ACT.Copy)\
                .then_inc(const_ev, 1)
            act.wait_ge(dve_set, 1)

            with act.Fori(0, HALVES) as h:
                turn = half_turn(h)
                before = h * TT

                def round_input(t):
                    for q in range(4):
                        act.wait_ge(a_tr, h * 16 + 4 * t + q + 1)
                        act_fn(act_hi[:, 4 * q:4 * q + 4, t * P:(t + 1) * P],
                               ps[:, 2 + q % 2, :].rearrange("p (k n) -> p k n", k=4), ACT.Copy).then_inc(a_hi, 1)

                act.wait_ge(unit_done, multiplied(turn, 0))
                for t in range(TT):
                    act.wait_ge(x_landed[t], h * 32 + 16)
                    if t:
                        act.wait_ge(a_ss, before + t)
                    act_fn(scratch, xt[t], ACT.Square, accum_out=ss[:, t:t + 1]).then_inc(a_ss, 1)
                    act.wait_ge(a_ms, before + t + 1)
                    act_fn(std[:, t:t + 1], ms[:, t:t + 1], ACT.Sqrt).then_inc(a_std, 1)
                    if t:
                        round_input(t - 1)
                round_input(TT - 1)

                def read(c):
                    bank = ps[:, c % 2, :]
                    act.wait_ge(unit_done, multiplied(turn, c + 1))
                    if c < 12:
                        j = c // 2
                        if j >= 2:
                            act.wait_ge(bank_read[1], h * 14 + j)
                        act_fn(sig[j % 2], bank, ACT.Sigmoid).then_inc(bank_read[0], 1)
                    elif c < 16:
                        if c > 12:
                            act.wait_ge(pool_d, h * POOLS + c - 12)
                        act_fn(ext[:, PLEAD:], bank, ACT.Copy).then_inc(bank_read[c % 2], 1)
                    elif c < 22:
                        if c == 16:
                            act.wait_ge(pool_d, h * POOLS + POOLS)
                        act_fn(vT[:, c - 16, :], bank, ACT.Gelu_apprx_tanh).then_inc(bank_read[c % 2], 1)
                    else:
                        act_fn(uT[:, c - 22, :], bank, ACT.Gelu_apprx_tanh).then_inc(bank_read[c % 2], 1)

                def v_tokens(t):
                    b = 2 + 2 * (t % 3)
                    act.wait_ge(v_tr, before + t + 1)
                    act_fn(vT[:, 0:4, t * P:(t + 1) * P], ps[:, b, :].rearrange("p (k n) -> p k n", k=4),
                           ACT.Copy).then_inc(v_tok, 1)
                    act_fn(vT[:, 4:6, t * P:(t + 1) * P],
                           ps[:, b + 1, 0:2 * P].rearrange("p (k n) -> p k n", k=2), ACT.Copy).then_inc(v_tok, 1)

                for c in range(NIN):
                    hi(turn, c)
                    if c and (c > 12 or c % 2 == 1):
                        read(c - 1)
                    if c == 19:
                        for g in range(POOLS):
                            act.wait_ge(pool_mm, h * POOLS + g + 1)
                            act_fn(xa[:, g, :], ps[:, 2 + g, :], ACT.Copy, scale=pscale[:, g:g + 1])\
                                .then_inc(pool_y, 1)
                    if c == 24:
                        for t in range(3):
                            v_tokens(t)
                    if c == 25:
                        v_tokens(3)
                    if c == 26:
                        act.wait_ge(v_var, h + 1)
                        act_fn(vstd[:, :], vmean[:, :, 1], ACT.Sqrt, bias=eps_t[:, 0:1]).then_inc(v_std, 1)
                read(NIN - 1)

                def y_round(k, source):
                    act_fn(act_hi[:, k, :], source, ACT.Copy).then_inc(y_hi, 1)

                act.wait_ge(pool_y, h * POOLS + POOLS)
                for g in range(POOLS):
                    y_round(g, xa[:, g, :])
                act.wait_ge(gate_mm, h * KB + KB)
                for j in range(KB):
                    act.wait_ge(c_cent, h * KB + j + 1)
                    act_fn(vT[:, j, :], zc[:, j, :], ACT.Square).then_inc(c_sq, 1)
                for j in range(KB):
                    act.wait_ge(gated, h * KB + j + 1)
                    y_round(POOLS + j, uT[:, j, :])
                act.wait_ge(c_var, h + 1)
                act_fn(vT[:, 0, :], ps[:, 1, :], ACT.Sqrt, bias=eps_t[:, 0:1]).then_inc(c_std, 1)
                for j in range(KB):
                    act.wait_ge(c_norm, h * KB + j + 1)
                    act_fn(zc[:, j, :], zc[:, j, :], ACT.Silu, bias=chan[:, j, TAPS + 2:TAPS + 3],
                           scale=chan[:, j, TAPS + 1:TAPS + 2]).then_inc(c_act, 1)
                for n in range(KB):
                    act.wait_ge(pw_mm, h * KB + n + 1)
                    y_round(POOLS + KB + n, ps[:, 2 + n, :])

                with act.Fori(0, 4) as n:
                    for c in range(RAW):
                        hi(turn + OUT_TURN + n, c)

                for t in range(TT):
                    act.wait_ge(x1_part, h * 16 + 12 + t + 1 + FREE_BLOCKS)
                    if t:
                        act.wait_ge(r_tr, h * 16 + 4 * t)
                        act.wait_ge(h2_stored, h * (16 * TT) + 16 * t)
                    act_fn(scratch, xt[t], ACT.Square, accum_out=ss[:, 4 + t:5 + t]).then_inc(r_ss, 1)
                    act.wait_ge(r_ms, before + t + 1)
                    act_fn(std[:, 4 + t:5 + t], ms[:, 4 + t:5 + t], ACT.Sqrt).then_inc(r_std, 1)
                    for q in range(4):
                        act.wait_ge(r_tr, h * 16 + 4 * t + q + 1)
                        act.wait_ge(r_lg, h * 16 + 4 * t + q + 1)
                        act_fn(tgrp[q % 2], ps[:, 4 + q % 2, :], ACT.Copy).then_inc(r_grp, 1)
                act.wait_ge(r_shift, 2 * h + 1)
                act_fn(ex_g, sh_g, ACT.Exp).then_inc(r_exp, 1)
                act.wait_ge(r_shift, 2 * h + 2)
                act_fn(ex_e, sh_e, ACT.Exp).then_inc(r_exp, 1)

            def round_x(i, q):
                act.wait_ge(m_xtr, 4 * i + q + 1)
                act_fn(xT_hi[:, 4 * q:4 * q + 4, :], ps[:, 2 + q % 2, :].rearrange("p (k n) -> p k n", k=4),
                       ACT.Copy).then_inc(m_xhi, 1)

            def silu_of(i, turn, first=False):
                act.wait_ge(unit_done, multiplied(turn, 4))
                if not first:
                    act.wait_ge(m_hid, i)
                act_fn(silu[:, :], ps[:, 0, :], ACT.Silu).then_inc(m_silu, 1)

            def round_h(i):
                act.wait_ge(m_htr, i + 1)
                act_fn(hT_hi[:, :, :].rearrange("p k n -> p (k n)"), ps[:, 1, :], ACT.Copy).then_inc(m_hhi, 1)

            def read_y(i, turn, c):
                act.wait_ge(unit_done, multiplied(turn, c))
                act.wait_ge(m_yfree, i + 1)
                for b in range(4):
                    act_fn(yb[:, b * BANK:(b + 1) * BANK], ps[:, 4 + b, :], ACT.Copy).then_inc(m_y, 1)

            def chunks(turn, first, last):
                for c in range(first, last):
                    hi(turn, c)

            for q in range(4):
                round_x(0, q)
            chunks(EXP_TURN, 0, 6)
            silu_of(0, EXP_TURN, first=True)
            chunks(EXP_TURN, 6, 10)
            for q in range(4):
                round_x(1, q)

            def expert(i, more):
                turn = LOOP_TURN + 3 * i
                chunks(turn, 2, 3)
                round_h(i)
                chunks(turn, 3, 6)
                silu_of(i + 1, turn)
                chunks(turn, 6, 10)
                if more:
                    act.wait_ge(unit_done, multiplied(turn, NW))
                    round_x(i + 2, 0)
                    round_x(i + 2, 1)
                chunks(turn, 10, 11)
                if more:
                    round_x(i + 2, 2)
                chunks(turn, 11, 12)
                if more:
                    round_x(i + 2, 3)
                chunks(turn, 12, 14)
                read_y(i, turn, NE)

            with act.Fori(0, E - 2) as i:
                expert(i, True)
            expert(E - 2, False)
            round_h(E - 1)
            chunks(LAST_TURN, 2, 4)
            read_y(E - 1, LAST_TURN, 4)
            act.wait_ge(count_ready, 1)
            n = act.value_load(n_extra[0:1, 0:1], min_val=0, max_val=EXTRA)
            with act.Fori(0, EXTRA) as i:
                with act.If(i < n):
                    turn = EXTRA_TURN + 3 * i
                    for q in range(4):
                        round_x(i + E, q)
                    chunks(turn, 0, 6)
                    silu_of(i + E, turn)
                    chunks(turn, 6, 9)
                    round_h(i + E)
                    chunks(turn, 9, 12)
                    read_y(i + E, turn, NE)

            with act.Fori(0, S // P // 2) as i:
                for k in range(2):
                    act.wait_ge(f_sum, 4 * i + 2 * k + 2)
                    act_fn(ye[:, k, 0, :], xb[:, k, :], ACT.Square, accum_out=fst[:, k, 0:1]).then_inc(f_sq, 1)
                    act.wait_ge(f_ms, 2 * i + k + 1)
                    act_fn(fst[:, k, 2:3], fst[:, k, 1:2], ACT.Sqrt).then_inc(f_std, 1)
                    act.wait_ge(f_out, 2 * i + k + 1)
                    act.dma_start(out[bass.ds((2 * i + k) * P, P), :], ye[:, k, 1, :]).then_inc(f_stored[k], 16)
            for k in range(2):
                act.wait_ge(f_stored[k], 16 * (S // P // 2))

        @block.vector
        def _(dve):
            dve.sem_inc(lo_ready, FREE_RAW)
            dve.sem_inc(a_lo, FREE_GROUPS)
            dve.sem_inc(bank_read[1], FREE_BANK)
            dve.sem_inc(x1_part, FREE_BLOCKS)
            tt, ts, stt = nc.vector.tensor_tensor, nc.vector.tensor_scalar, nc.vector.scalar_tensor_tensor

            def lo(turn, c):
                for j in range(2):
                    s = (2 * c + j) % SPLIT
                    dve.wait_ge(hi_ready, 8 * turn + 2 * c + j + 1)
                    tt(w_lo[:, s, :], raw[:, c % RAW, j * UNIT:(j + 1) * UNIT], w_hi[:, s, :].bitcast(F32),
                       ALU.subtract).then_inc(lo_ready, 1)

            class Steps:

                def __init__(self, base):
                    self.base, self.n = base, 0

                def __call__(self, ins):
                    self.n += 1
                    ins.then_inc(step, 1)

                def wait(self):
                    dve.wait_ge(step, self.base + self.n)

                def then(self, ins):
                    self(ins)
                    self.wait()

            do = Steps(0)
            for v, to in ((EPS, eps_t[:, :]), (1.0 / DC, mean1[:, :]), (1.0, ones[:, :]), (0.0, halo_z[:, :, :]),
                          (0.0, halo_x[:, :, :]), (0.0, carry[:, :])):
                do(nc.vector.memset(to, v))
            dve.wait_ge(const_set, 11)
            for g in range(POOLS):
                do(ts(inv[:, g, :], inv[:, g, :], float(2 << g), None, ALU.min))
            do.wait()
            nc.vector.reciprocal(inv[:, :, :], inv[:, :, :]).then_inc(dve_set, 1)
            dve.wait_ge(dve_set, 1)
            SET = do.n

            with dve.Fori(0, HALVES) as h:
                turn = half_turn(h)
                before = h * TT
                do = Steps(h * STEPS + SET)

                def rest_of_input(t):
                    for q in range(4):
                        dve.wait_ge(a_hi, h * 16 + 4 * t + q + 1)
                        tt(act_lo[:, 4 * q:4 * q + 4, t * P:(t + 1) * P],
                           ps[:, 2 + q % 2, :].rearrange("p (k n) -> p k n", k=4),
                           act_hi[:, 4 * q:4 * q + 4, t * P:(t + 1) * P].bitcast(F32),
                           ALU.subtract).then_inc(a_lo, 1)

                for t in range(TT):
                    dve.wait_ge(a_ss, before + t + 1)
                    ts(ms[:, t:t + 1], ss[:, t:t + 1], 1.0 / D, EPS, ALU.mult, ALU.add).then_inc(a_ms, 1)
                    dve.wait_ge(a_std, before + t + 1)
                    nc.vector.reciprocal(rstd[:, t:t + 1], std[:, t:t + 1]).then_inc(a_rstd, 1)
                    dve.wait_ge(a_rstd, before + t + 1)
                    if t == 0:
                        dve.wait_ge(gain_landed, h * 32 + 16)
                    stt(xt[t], xt[t], rstd[:, t:t + 1], gain, ALU.mult, ALU.mult).then_inc(a_xn, 1)
                    if t:
                        rest_of_input(t - 1)
                rest_of_input(TT - 1)

                do.then(nc.vector.tensor_copy(z[:, :, 2:32], halo_z[:, :, :]))

                def gated_value(j):
                    dve.wait_ge(bank_read[0], h * 14 + j + 1 + FREE_BANK)
                    dve.wait_ge(unit_done, multiplied(turn, 2 * j + 2))
                    tt(z[:, j, 32:], ps[:, 1, :], sig[j % 2], ALU.mult).then_inc(bank_read[1], 1)

                def taps(first, last):
                    for m in range(first, last):
                        j, i = divmod(m, TAPS)
                        source = z[:, j, 2 + i:2 + i + HALF]
                        w = chan[:, j, i:i + 1]
                        if i == 0:
                            dve.wait_ge(bank_read[1], h * 14 + j + 1 + FREE_BANK)
                            ts(zc[:, j, :], source, w, chan[:, j, TAPS:TAPS + 1], ALU.mult, ALU.add)\
                                .then_inc(tap, 1)
                        else:
                            dve.wait_ge(tap, h * (KB * TAPS) + m)
                            stt(zc[:, j, :], source, w, zc[:, j, :], ALU.mult, ALU.add).then_inc(tap, 1)

                def pooled(g):
                    c = 12 + g
                    do(nc.vector.tensor_copy(ext[:, 1:PLEAD], halo_x[:, g, :]))
                    dve.wait_ge(bank_read[c % 2], h * 14 + c // 2 + 1 + FREE_BANK)
                    do.wait()
                    a = ext
                    for n in range(g + 1):
                        b = (sums, sums2)[n % 2]
                        at0, s = 2 << n, 1 << n
                        do.then(tt(b[:, at0:], a[:, at0:], a[:, at0 - s:-s], ALU.add))
                        a = b
                    do.then(tt(a[:, PLEAD:2 * PLEAD], a[:, PLEAD:2 * PLEAD], inv[:, g, :], ALU.mult))
                    do(nc.vector.memset(inv[:, g, :], 1.0 / (2 << g)))
                    do(nc.vector.tensor_copy(halo_x[:, g, :], ext[:, -PLEAD + 1:]))
                    do(tt(xa[:, g, 0:PLEAD], a[:, PLEAD:2 * PLEAD], ext[:, PLEAD:2 * PLEAD], ALU.subtract))
                    stt(xa[:, g, PLEAD:], a[:, 2 * PLEAD:], 1.0 / (2 << g), ext[:, 2 * PLEAD:],
                        ALU.mult, ALU.subtract).then_inc(pool_d, 1)

                def v_stats(t):
                    dve.wait_ge(v_tok, 2 * before + 2 * t + 2)
                    for n in range(2):
                        do(nc.vector.bn_stats(vstat[:, t, 6 * n:6 * n + 6],
                                              vT[:, 3 * n:3 * n + 3, t * P:(t + 1) * P]))
                    do.wait()
                    apart(dve)
                    ins = nc.vector.bn_aggr(vmean[:, t, :], vstat[:, t, :])
                    if t < TT - 1:
                        do(ins)
                    else:
                        ins.then_inc(v_var, 1)

                def v_norm(t):
                    v = vT[:, :, t * P:(t + 1) * P]
                    do.then(ts(v, v, vmean[:, t, 0:1], vrstd[:, t:t + 1], ALU.subtract, ALU.mult))
                    do.then(tt(v, v, ln_g[:, :, :], ALU.mult))
                    tt(v, v, ln_b[:, :, :], ALU.add).then_inc(v_ln, 1)

                PER = 8
                for c in range(NIN):
                    lo(turn, c)
                    if 2 <= c <= 12 and c % 2 == 0:
                        gated_value(c // 2 - 1)
                    if 13 <= c <= 16:
                        pooled(c - 13)
                    if c == 24:
                        for t in range(3):
                            v_stats(t)
                    if c == 25:
                        v_stats(3)
                    if c == 26:
                        dve.wait_ge(v_std, h + 1)
                        do.then(nc.vector.reciprocal(vrstd[:, :], vstd[:, :]))
                        v_norm(0)
                        v_norm(1)
                    if c == 27:
                        v_norm(2)
                        v_norm(3)
                    if c >= 3:
                        taps(min((c - 3) * PER, KB * TAPS), min((c - 2) * PER, KB * TAPS))
                dve.wait_ge(tap, h * (KB * TAPS) + KB * TAPS)
                do(nc.vector.tensor_copy(halo_z[:, :, :], z[:, :, 2 + HALF:]))

                def y_rest(k, source):
                    dve.wait_ge(y_hi, h * KD + k + 1)
                    tt(act_lo[:, k, :], source, act_hi[:, k, :].bitcast(F32), ALU.subtract).then_inc(y_lo, 1)

                dve.wait_ge(c_mean, h + 1)
                for j in range(KB):
                    tt(zc[:, j, :], zc[:, j, :], ps[:, 0, :], ALU.subtract).then_inc(c_cent, 1)
                for g in range(POOLS):
                    y_rest(g, xa[:, g, :])
                for j in range(KB):
                    dve.wait_ge(gate_mm, h * KB + j + 1)
                    gate = ps[:, 2 + j, :].rearrange("p (n t) -> p n t", n=TT)
                    do.then(tt(gate, gate, gate_b[:, j:j + 1, :].to_broadcast([P, TT, P]), ALU.add))
                    tt(uT[:, j, :], ps[:, 2 + j, :], uT[:, j, :], ALU.mult).then_inc(gated, 1)
                for j in range(KB):
                    y_rest(POOLS + j, uT[:, j, :])
                dve.wait_ge(c_std, h + 1)
                do.then(nc.vector.reciprocal(vT[:, 1, :], vT[:, 0, :]))
                for j in range(KB):
                    tt(zc[:, j, :], zc[:, j, :], vT[:, 1, :], ALU.mult).then_inc(c_norm, 1)
                for n in range(KB):
                    y_rest(POOLS + KB + n, ps[:, 2 + n, :])

                def add_rows(n, sub):
                    dve.wait_ge(unit_done, multiplied(turn + OUT_TURN + n, RAW))
                    for t in range(TT):
                        to = xt[t][:, bass.ds(n * BANK, BANK)]
                        if sub == 0:
                            dve.wait_ge(x_landed[t], h * 32 + 32)
                        tt(to, to, ps[:, (4 if sub == 0 else 0) + t, :], ALU.add).then_inc(x1_part, 1)

                lo(turn + OUT_TURN, 0)
                lo(turn + OUT_TURN, 1)
                for n in range(4):
                    lo(turn + OUT_TURN + n, 2)
                    lo(turn + OUT_TURN + n, 3)
                    if n < 3:
                        lo(turn + OUT_TURN + n + 1, 0)
                        lo(turn + OUT_TURN + n + 1, 1)
                    add_rows(n, n % 2)

                do(nc.vector.memset(lg[:, :, G:], -3.0e38))
                for t in range(TT):
                    dve.wait_ge(r_ss, before + t + 1)
                    ts(ms[:, 4 + t:5 + t], ss[:, 4 + t:5 + t], 1.0 / D, EPS, ALU.mult, ALU.add).then_inc(r_ms, 1)
                    dve.wait_ge(r_std, before + t + 1)
                    nc.vector.reciprocal(rstd[:, 4 + t:5 + t], std[:, 4 + t:5 + t]).then_inc(r_rstd, 1)
                    dve.wait_ge(r_rstd, before + t + 1)
                    if t == 0:
                        dve.wait_ge(gain_landed, h * 32 + 32)
                    stt(scratch, xt[t], rstd[:, 4 + t:5 + t], gain, ALU.mult, ALU.mult).then_inc(r_xn, 1)

                dve.wait_ge(r_lg, h * 16 + 16 + FREE_GROUPS)
                logits = ps[:, 6, 0:TT * (G + E)].rearrange("p (t n) -> p t n", t=TT)

                def over_tiles(v, n):
                    return v.unsqueeze(1).to_broadcast([P, TT, n])

                def over_last(v, n):
                    return v.unsqueeze(2).to_broadcast([P, TT, n])

                do(tt(lg[:, :, 0:G], logits[:, :, 0:G], over_tiles(rb[:, 0:G], G), ALU.add))
                do.then(tt(le, logits[:, :, G:], over_tiles(rb[:, G:], E), ALU.add))
                apart(dve)
                for t in range(TT):
                    do(nc.vector.max(top_g[:, t, :], lg[:, t, :]))
                do.wait()
                tt(sh_g, lg[:, :, 0:G], top_g[:, :, 0:1].to_broadcast([P, TT, G]), ALU.subtract).then_inc(r_shift, 1)
                for t in range(TT):
                    do(nc.vector.max_index(idx_g.bitcast(U32)[:, t, :], top_g[:, t, :], lg[:, t, :]))
                do.wait()
                do.then(nc.vector.tensor_copy(gf, idx_g.bitcast(U32)[:, :, 0]))
                do.then(tt(onehot_g, over_tiles(iota_g[:, :], G), over_last(gf, G), ALU.is_equal))
                for g in range(G):
                    one = onehot_g[:, :, g:g + 1].to_broadcast([P, TT, EG])
                    if g == 0:
                        do.then(tt(le8, le[:, :, 0:EG], one, ALU.mult))
                    else:
                        do.then(tt(prod8, le[:, :, g * EG:(g + 1) * EG], one, ALU.mult))
                        do.then(tt(le8, le8, prod8, ALU.add))
                apart(dve)
                for t in range(TT):
                    do(nc.vector.max(top_e[:, t, :], le8[:, t, :]))
                do.wait()
                tt(sh_e, le8, top_e[:, :, 0:1].to_broadcast([P, TT, EG]), ALU.subtract).then_inc(r_shift, 1)
                for t in range(TT):
                    do(nc.vector.max_index(idx_e.bitcast(U32)[:, t, :], top_e[:, t, :], le8[:, t, :]))
                do(ts(ge, gf, float(EG), None, ALU.mult))
                do.wait()
                do.then(nc.vector.tensor_copy(ef, idx_e.bitcast(U32)[:, :, 0:2]))
                do.then(tt(hot[:, :, 0, 0:EG], over_tiles(iota_e[:, 0:EG], EG), over_last(ef[:, :, 0], EG),
                           ALU.is_equal))
                do.then(tt(hot[:, :, 1, 0:EG], over_tiles(iota_e[:, 0:EG], EG), over_last(ef[:, :, 1], EG),
                           ALU.is_equal))
                dve.wait_ge(r_exp, 2 * h + 2)
                for k in range(2):
                    do.then(tt(prod8, hot[:, :, k, 0:EG], ex_e, ALU.mult))
                    do.then(nc.vector.tensor_reduce(wk[:, :, k:k + 1], prod8, AX.X, ALU.add))
                do(nc.vector.tensor_reduce(sum_g, ex_g, AX.X, ALU.add))
                do(nc.vector.tensor_reduce(sum_e, ex_e, AX.X, ALU.add))
                do.wait()
                do(nc.vector.reciprocal(sum_g, sum_g))
                do(nc.vector.reciprocal(sum_e, sum_e))
                do.wait()
                do.then(tt(wk, wk, sum_e.unsqueeze(2).to_broadcast([P, TT, 2]), ALU.mult))
                do.then(tt(sum_p, wk[:, :, 0], wk[:, :, 1], ALU.add))
                do(nc.vector.reciprocal(sum_p, sum_p))
                do.then(tt(wk, wk, sum_g.unsqueeze(2).to_broadcast([P, TT, 2]), ALU.mult))
                do(tt(wts[:, bass.ds(before, TT), :], wk, sum_p.unsqueeze(2).to_broadcast([P, TT, 2]), ALU.mult))
                do.then(tt(ef, ef, ge.unsqueeze(2).to_broadcast([P, TT, 2]), ALU.add))
                for k in range(2):
                    do(tt(hot[:, :, k, :], over_tiles(iota_e[:, :], E), over_last(ef[:, :, k], E), ALU.is_equal))
                do.wait()
                tt(both, hot[:, :, 0, :], hot[:, :, 1, :], ALU.add).then_inc(r_hot, 1)
                dve.wait_ge(r_rank, h + 1)
                counted = ps[:, 7, 0:TT * 2 * E].rearrange("p (t a e) -> p t a e", t=TT, a=2)
                for t in range(TT):
                    do.then(tt(rank[:, t, :], counted[:, t, 0, :], carry[:, :], ALU.add))
                    do.then(tt(carry[:, :], counted[:, t, 1, :], carry[:, :], ALU.add))
                do.then(tt(rank, rank, over_tiles(iota_l[:, :], E), ALU.add))
                for k in range(2):
                    do.then(tt(hot_rank, hot[:, :, k, :], rank, ALU.mult))
                    do.then(nc.vector.tensor_reduce(dest_f[:, :, k:k + 1], hot_rank, AX.X, ALU.add))
                do.then(nc.vector.tensor_copy(asg_i[:, :, :], asg_f[:, :, :]))
                do.then(ts(asg_f[:, :, :], asg_f[:, :, :], 2.0 * HALF, None, ALU.add))
                nc.vector.tensor_copy(dest_i[:, :, :], dest_f).then_inc(r_dest, 1)
                assert do.n == STEPS, f"STEPS = {do.n}"

            do = Steps(SET + HALVES * STEPS)
            dve.wait_ge(list_in, 16)
            nc.vector.tensor_copy(lst_f[:, :], lst_i[:, :]).then_inc(list_f, 1)
            dve.wait_ge(list_tr, 1)
            nc.vector.tensor_copy(slot_i[:, :], ps[:, 0, 0:E]).then_inc(slots, 1)
            dve.wait_ge(slots, 1)
            ts(tok_i[:, :], slot_i[:, :], 1, None, ALU.logical_shift_right).then_inc(slots, 1)

            def rest_of_x(i, q):
                dve.wait_ge(m_xhi, 4 * i + q + 1)
                tt(xT_lo[:, 4 * q:4 * q + 4, :], ps[:, 2 + q % 2, :].rearrange("p (k n) -> p k n", k=4),
                   xT_hi[:, 4 * q:4 * q + 4, :].bitcast(F32), ALU.subtract).then_inc(m_xlo, 1)

            def hidden(i, turn, first=False):
                dve.wait_ge(m_silu, i + 1)
                dve.wait_ge(unit_done, multiplied(turn, NW))
                if not first:
                    dve.wait_ge(m_htr, i)
                tt(hid[:, :], ps[:, 1, :], silu[:, :], ALU.mult).then_inc(m_hid, 1)

            def rest_of_h(i):
                dve.wait_ge(m_hhi, i + 1)
                tt(hT_lo[:, :, :].rearrange("p k n -> p (k n)"), ps[:, 1, :],
                   hT_hi[:, :, :].rearrange("p k n -> p (k n)").bitcast(F32), ALU.subtract).then_inc(m_hlo, 1)

            def chunks(turn, first, last):
                for c in range(first, last):
                    lo(turn, c)

            for q in range(4):
                rest_of_x(0, q)

            dve.wait_ge(m_zero, 5)
            for b in range(7):
                do(ts(over[:, b, :], carry[:, :], float(P * (b + 1)), None, ALU.is_gt))
            do.wait()
            flat = over[:, :, :].rearrange("p b e -> p (b e)")
            flat_cum = cum[:, :, :].rearrange("p b e -> p (b e)")
            do.then(nc.vector.tensor_tensor_scan(flat_cum, allone[:, :], flat, 0.0, ALU.mult, ALU.add))
            nc.vector.tensor_copy(n_extra[:, :], cum[:, 6, E - 1:E]).then_inc(count_ready, 1)
            dve.wait_ge(count_ready, 1)
            do.then(tt(flat_cum, flat_cum, flat, ALU.mult))
            for r in range(2):
                do.then(stt(flat, flat_cum, iota_1[:, 0:1], code[:, r, :, :].rearrange("p b e -> p (b e)"),
                            ALU.is_equal, ALU.mult, accum_out=tab_f[:, r:r + 1]))
            nc.vector.tensor_copy(tab_i[:, :], tab_f[:, :]).then_inc(tab_ready, 1)

            chunks(EXP_TURN, 0, 9)
            hidden(0, EXP_TURN, first=True)
            for q in range(4):
                rest_of_x(1, q)
            chunks(EXP_TURN, 9, 10)

            def expert(i, more):
                turn = LOOP_TURN + 3 * i
                chunks(turn, 2, 3)
                rest_of_h(i)
                chunks(turn, 3, 10)
                hidden(i + 1, turn)
                if more:
                    rest_of_x(i + 2, 0)
                    rest_of_x(i + 2, 1)
                chunks(turn, 10, 11)
                if more:
                    rest_of_x(i + 2, 2)
                chunks(turn, 11, 12)
                if more:
                    rest_of_x(i + 2, 3)
                chunks(turn, 12, 14)

            with dve.Fori(0, E - 2) as i:
                expert(i, True)
            expert(E - 2, False)
            rest_of_h(E - 1)
            chunks(LAST_TURN, 2, 4)
            n = dve.value_load(n_extra[0:1, 0:1], min_val=0, max_val=EXTRA)
            with dve.Fori(0, EXTRA) as i:
                with dve.If(i < n):
                    turn = EXTRA_TURN + 3 * i
                    dve.wait_ge(e_list, 16 * i + 16)
                    ts(ix_new[:, :], ix_asg[:, :], 1, None, ALU.logical_shift_right).then_inc(e_tok, 1)
                    for q in range(4):
                        rest_of_x(i + E, q)
                    chunks(turn, 0, 8)
                    hidden(i + E, turn)
                    chunks(turn, 8, 9)
                    rest_of_h(i + E)
                    chunks(turn, 9, 12)

            dve.wait_ge(f_gain, 16)
            with dve.Fori(0, S // P // 2) as i:
                for k in range(2):
                    nc.vector.tensor_copy(wcol[:, k, :], wts[:, bass.ds(2 * i + k, 1), :]).then_inc(f_col, 1)
                    dve.wait_ge(f_col, 2 * i + k + 1)
                    dve.wait_ge(f_landed[k], 32 * i + 32)
                    for a in range(2):
                        stt(xb[:, k, :], ye[:, k, a, :], wcol[:, k, a:a + 1], xb[:, k, :], ALU.mult, ALU.add)\
                            .then_inc(f_sum, 1)
                        dve.wait_ge(f_sum, 4 * i + 2 * k + a + 1)
                    dve.wait_ge(f_sq, 2 * i + k + 1)
                    ts(fst[:, k, 1:2], fst[:, k, 0:1], 1.0 / D, EPS, ALU.mult, ALU.add).then_inc(f_ms, 1)
                    dve.wait_ge(f_std, 2 * i + k + 1)
                    nc.vector.reciprocal(fst[:, k, 3:4], fst[:, k, 2:3]).then_inc(f_rstd, 1)
                    dve.wait_ge(f_rstd, 2 * i + k + 1)
                    stt(ye[:, k, 1, :], xb[:, k, :], fst[:, k, 3:4], gfin[:, :], ALU.mult, ALU.mult)\
                        .then_inc(f_out, 1)

        @block.tensor
        def _(pe):
            pe.sem_inc(unit_done, FREE_UNITS)
            pe.sem_inc(r_lg, FREE_GROUPS)
            mm = nc.tensor.matmul

            def transposes(source, bank, count, done, n=P):
                for a in range(count):
                    last = nc.tensor.transpose(ps[:, bank, a * P:(a + 1) * P], source(a), ident[:, :])
                last.then_inc(done, 1)

            def three(out_, s_hi, s_lo, m_hi, m_lo, start, stop):
                mm(out_, s_hi, m_hi, start=start, stop=False)
                mm(out_, s_hi, m_lo, start=False, stop=False)
                return mm(out_, s_lo, m_hi, start=False, stop=stop)

            pe.wait_ge(const_set, 6)
            NC = TAPS + 3
            for j in range(KB):
                nc.tensor.transpose(ps[:, 0, j * NC:(j + 1) * NC], zv[0:NC, j * P:(j + 1) * P], ident[0:NC, 0:NC])\
                    .then_inc(const_tr, 1)
            nc.tensor.transpose(ps[:, 0, KB * NC:KB * NC + POOLS], zv[0:POOLS, DC:DC + P], ident[0:POOLS, 0:POOLS])\
                .then_inc(const_tr, 1)
            for j in range(KB):
                nc.tensor.transpose(ps[:, 1 + j // 4, (j % 4) * P:(j % 4 + 1) * P],
                                    zv[:, 1024 + j * P:1024 + (j + 1) * P], ident[:, :]).then_inc(const_tr, 1)
            pe.wait_ge(const_ev, 4)
            pe.wait_ge(dve_set, 1)

            with pe.Fori(0, HALVES) as h:
                turn = half_turn(h)
                before = h * TT

                for t in range(TT):
                    pe.wait_ge(a_xn, before + t + 1)
                    for q in range(4):
                        pe.wait_ge(a_lo, h * 16 + 4 * t + q + 1)
                        transposes(lambda a: xt[t][:, (4 * q + a) * P:(4 * q + a + 1) * P], 2 + q % 2, 4, a_tr)
                pe.wait_ge(a_lo, h * 16 + 16 + FREE_GROUPS)

                def product(unit, m, reads):
                    pe.wait_ge(bank_read[m], h * 14 + reads + FREE_BANK)
                    for j in range(2):
                        s = 2 * m + j
                        pe.wait_ge(lo_ready, unit + s + 1 + FREE_RAW)
                        for k in range(8):
                            cols = slice(k * P, (k + 1) * P)
                            last = three(ps[:, m, :], w_hi[:, s, cols], w_lo[:, s, cols],
                                         act_hi[:, 8 * j + k, :], act_lo[:, 8 * j + k, :],
                                         j == 0 and k == 0, j == 1 and k == 7)
                        last.then_inc(unit_done, 1)

                def pairs(first, last):
                    with pe.Fori(first, last) as i:
                        for m in range(2):
                            product(h * UH + 4 * i, m, i)

                def v_transposes(t):
                    b = 2 + 2 * (t % 3)
                    for a in range(KB):
                        last = nc.tensor.transpose(ps[:, b + a // 4, (a % 4) * P:(a % 4 + 1) * P],
                                                   vT[:, a, t * P:(t + 1) * P], ident[:, :])
                    last.then_inc(v_tr, 1)

                apart(pe)
                pairs(0, 9)
                pe.wait_ge(pool_d, h * POOLS + POOLS)
                for g in range(POOLS):
                    mm(ps[:, 2 + g, :], pool_wt[:, g, :], xa[:, g, :], start=True, stop=True).then_inc(pool_mm, 1)
                pairs(9, 11)
                product(h * UH + 44, 0, 11)
                pe.wait_ge(bank_read[1], h * 14 + 11 + FREE_BANK)
                pe.wait_ge(pool_y, h * POOLS + POOLS)
                for t in range(3):
                    v_transposes(t)
                product(h * UH + 44, 1, 11)
                pe.wait_ge(v_tok, 2 * before + 2)
                v_transposes(3)
                pairs(12, 14)

                pe.wait_ge(v_ln, before + TT)
                for j in range(KB):
                    for t in range(TT):
                        cols = slice(t * P, (t + 1) * P)
                        last = mm(ps[:, 2 + j, cols], vT[:, j, cols], wmT[:, j, :], start=True, stop=True)
                    last.then_inc(gate_mm, 1)
                pe.wait_ge(tap, h * (KB * TAPS) + KB * TAPS)
                pe.wait_ge(bank_read[0], h * 14 + 14 + FREE_BANK)
                for j in range(KB):
                    last = mm(ps[:, 0, :], mean1[:, :], zc[:, j, :], start=j == 0, stop=j == KB - 1)
                last.then_inc(c_mean, 1)
                pe.wait_ge(bank_read[1], h * 14 + 14 + FREE_BANK)
                for j in range(KB):
                    pe.wait_ge(c_sq, h * KB + j + 1)
                    last = mm(ps[:, 1, :], mean1[:, :], vT[:, j, :], start=j == 0, stop=j == KB - 1)
                last.then_inc(c_var, 1)
                pe.wait_ge(c_act, h * KB + KB)
                pe.wait_ge(gated, h * KB + KB)
                for n in range(KB):
                    pe.wait_ge(pw_landed[n % 2], h * 48 + 16 * (n // 2) + 16)
                    for k in range(KB):
                        last = mm(ps[:, 2 + n, :], pw[:, n % 2, k, :], zc[:, k, :], start=k == 0, stop=k == KB - 1)
                    last.then_inc(pw_mm, 1)

                pe.wait_ge(y_lo, h * KD + KD)
                apart(pe)
                with pe.Fori(0, 2) as i:
                    for m in range(2):
                        for g in range(4):
                            for j in range(2):
                                s = (2 * g + j) % SPLIT
                                pe.wait_ge(lo_ready, h * UH + 2 * NIN + 16 * i + 8 * m + 2 * g + j + 1 + FREE_RAW)
                                for a in range(2):
                                    k = 4 * g + 2 * j + a
                                    cols = slice(a * BANK, (a + 1) * BANK)
                                    for t in range(TT):
                                        if k == 0:
                                            pe.wait_ge(x1_part, h * 16 + 8 * i + 4 * m + t + 1)
                                        rows = slice(t * P, (t + 1) * P)
                                        last = three(ps[:, (4 if m == 0 else 0) + t, :],
                                                     act_hi[:, k, rows], act_lo[:, k, rows],
                                                     w_hi[:, s, cols], w_lo[:, s, cols], k == 0, k == KD - 1)
                                last.then_inc(unit_done, 1)

                def logits(n):
                    t, q = divmod(n, 4)
                    pe.wait_ge(r_grp, h * 16 + n + 1 + FREE_GROUPS)
                    for a in range(4):
                        last = mm(ps[:, 6, t * (G + E):(t + 1) * (G + E)], tgrp[q % 2][:, a * P:(a + 1) * P],
                                  rw[:, 4 * q + a, :], start=q == 0 and a == 0, stop=q == 3 and a == 3)
                    last.then_inc(r_lg, 1)

                for n in range(4 * TT):
                    t, q = divmod(n, 4)
                    if q == 0:
                        pe.wait_ge(r_xn, before + t + 1)
                    pe.wait_ge(r_grp, h * 16 + n + 1)
                    transposes(lambda a: scratch[:, (4 * q + a) * P:(4 * q + a + 1) * P], 4 + q % 2, 4, r_tr)
                    if n:
                        logits(n - 1)
                logits(4 * TT - 1)
                pe.wait_ge(r_hot, h + 1)
                for t in range(TT):
                    at_ = 2 * E * t
                    mm(ps[:, 7, at_:at_ + E], tri[:, :], both[:, t, :], start=True, stop=True)
                    last = mm(ps[:, 7, at_ + E:at_ + 2 * E], ones[:, :], both[:, t, :], start=True, stop=True)
                last.then_inc(r_rank, 1)

            pe.wait_ge(list_f, 1)
            nc.tensor.transpose(ps[:, 0, 0:E], lst_f[:, :], ident[0:E, 0:E]).then_inc(list_tr, 1)

            def x_columns(i, q):
                if q == 0:
                    pe.wait_ge(m_gathered, 16 * i + 16)
                if q >= 2:
                    pe.wait_ge(m_xlo, 4 * i + q - 1)
                transposes(lambda a: xg[:, (4 * q + a) * P:(4 * q + a + 1) * P], 2 + q % 2, 4, m_xtr)

            def h_columns(i):
                pe.wait_ge(m_hid, i + 1)
                transposes(lambda a: hid[:, a * P:(a + 1) * P], 1, KF, m_htr)

            def up(turn_, c):
                for j in range(2):
                    s = (2 * c + j) % SPLIT
                    pe.wait_ge(lo_ready, split_of(turn_, c, j))
                    for a in range(2):
                        k = 4 * (c % 4) + 2 * j + a
                        cols = slice(a * BANK, (a + 1) * BANK)
                        last = three(ps[:, c // 4, :], xT_hi[:, k, :], xT_lo[:, k, :],
                                     w_hi[:, s, cols], w_lo[:, s, cols], k == 0, k == KD - 1)
                    last.then_inc(unit_done, 1)

            def down(turn_, c, f):
                for j in range(2):
                    s = (2 * c + j) % SPLIT
                    pe.wait_ge(lo_ready, split_of(turn_, c, j))
                    for a in range(2):
                        cols = slice(a * BANK, (a + 1) * BANK)
                        last = three(ps[:, 4 + 2 * j + a, :], hT_hi[:, f, :], hT_lo[:, f, :],
                                     w_hi[:, s, cols], w_lo[:, s, cols], f == 0, f == KF - 1)
                    last.then_inc(unit_done, 1)

            for q in range(4):
                x_columns(0, q)
            pe.wait_ge(m_xlo, 4)
            for c in range(NW):
                up(EXP_TURN, c)
            for q in range(4):
                x_columns(1, q)

            def expert(i, more):
                turn_ = LOOP_TURN + 3 * i
                pe.wait_ge(m_xlo, 4 * i + 8)
                pe.wait_ge(m_silu, i + 1)
                up(turn_, 0)
                h_columns(i)
                for c in range(1, 4):
                    up(turn_, c)
                pe.wait_ge(m_hlo, i + 1)
                for c in range(4, NW):
                    up(turn_, c)
                    if more and c >= 6:
                        x_columns(i + 2, c - 6)
                pe.wait_ge(m_y, 4 * i + FREE_BANK)
                for f in range(KF):
                    down(turn_, NW + f, f)
                    if more and f < 2:
                        x_columns(i + 2, f + 2)

            with pe.Fori(0, E - 2) as i:
                expert(i, True)
            expert(E - 2, False)
            h_columns(E - 1)
            pe.wait_ge(m_hlo, E)
            pe.wait_ge(m_y, 4 * (E - 1) + FREE_BANK)
            for f in range(KF):
                down(LAST_TURN, f, f)
            pe.wait_ge(count_ready, 1)
            n = pe.value_load(n_extra[0:1, 0:1], min_val=0, max_val=EXTRA)
            with pe.Fori(0, EXTRA) as i:
                with pe.If(i < n):
                    turn_ = EXTRA_TURN + 3 * i
                    for q in range(4):
                        x_columns(i + E, q)
                    pe.wait_ge(m_xlo, 4 * i + (4 * E + 4))
                    pe.wait_ge(m_silu, i + E)
                    for c in range(4):
                        up(turn_, c)
                    pe.wait_ge(m_hlo, i + E)
                    for c in range(4, NW):
                        up(turn_, c)
                    h_columns(i + E)
                    pe.wait_ge(m_hlo, i + E + 1)
                    pe.wait_ge(m_y, 4 * i + (4 * E + FREE_BANK))
                    for f in range(KF):
                        down(turn_, NW + f, f)


INPUTS = ["x", "norm_mix", "w_in", "pool_w", "pool_scale", "sgu_ln_g", "sgu_ln_b", "sgu_w", "sgu_b",
          "conv_dw_w", "conv_dw_b", "conv_ln_g", "conv_ln_b", "conv_pw", "w_out", "norm_ffn",
          "router_g_w", "router_g_b", "router_e_w", "router_e_b", "exp_w1", "exp_w3", "exp_w2",
          "norm_final"]


def kernel(**inputs):
    import numpy as np
    from concourse import bacc
    from concourse.bass_utils import run_bass_kernel_spmd

    nc = bacc.Bacc("TRN2", target_bir_lowering=False, num_devices=1, dynamic_dma_scratch_size=8192)
    arrays, args = {}, []
    for name in INPUTS:
        a = np.ascontiguousarray(inputs[name])
        arrays[f"in_{name}"] = a
        args.append(nc.dram_tensor(f"in_{name}", a.shape, mybir.dt.from_np(a.dtype), kind="ExternalInput").ap())
    result = nc.dram_tensor("result", (1, S, D), F32, kind="ExternalOutput").ap()
    build(nc, *args, result)
    ran = run_bass_kernel_spmd(nc, [arrays], core_ids=[0])
    return ran.results[0]["result"]
```

```python
from contextlib import ExitStack

import concourse.bass as bass
from concourse import mybir

F32 = mybir.dt.float32
F32R = mybir.dt.float32r
I32 = mybir.dt.int32
U32 = mybir.dt.uint32
ALU = mybir.AluOpType
ACT = mybir.ActivationFunctionType
AX = mybir.AxisListType

P = 128
BANK = 512
S, D = 1024, 2048
KD = D // P
DA, DB, DC = 512, 768, 768
KB = DB // P
POOLS = 4
TAPS = 31
LEAD = TAPS - 1
HALF = 512
HALVES = S // HALF
TT = HALF // P
NT = S // P
PLEAD = 16
G, EG = 4, 8
E = G * EG
FE = D // 4
KF = FE // P
EPS = 1e-6

CHUNK = 2048
UNIT = CHUNK // 2
RAW = 4
SPLIT = 4
NIN = (DA + 2 * DB + 2 * DC) // P
NOUT = KD * D // CHUNK
CH = NIN + NOUT
UH = 2 * CH
CM = HALVES * CH
NW = 8
NE = NW + 4
CX = CM + E * NE
EXTRA = 15
PADS = 4096
LISTED = 1024

FREE_UNITS = SPLIT
FREE_RAW = 2 * RAW
FREE_BANK = 1
FREE_GROUPS = 2
FREE_BLOCKS = 8
FREE_TILES = 8
FREE_ROWS = 1
STEPS = 61


def build(nc, x, norm_mix, w_in, pool_w, pool_scale, sgu_ln_g, sgu_ln_b, sgu_w, sgu_b, conv_dw_w,
          conv_dw_b, conv_ln_g, conv_ln_b, conv_pw, w_out, norm_ffn, router_g_w, router_g_b,
          router_e_w, router_e_b, exp_w1, exp_w3, exp_w2, norm_final, out):
    x = x[0]
    out = out[0]
    w_in = w_in[0]
    x1_d = nc.dram_tensor("x1_d", (S, D), F32, kind="Internal").ap()
    h2_d = nc.dram_tensor("h2_d", (S, D), F32, kind="Internal").ap()
    yd = nc.dram_tensor("yd", (2 * S, D), F32, kind="Internal").ap()
    list_d = nc.dram_tensor("list_d", (E * LISTED, 1), I32, kind="Internal").ap()
    extra_d = nc.dram_tensor("extra_d", (2, 16), I32, kind="Internal").ap()

    ctx = ExitStack()
    with ctx:
        part = [ctx]

        def sb(name, shape, dt=F32):
            return part[0].enter_context(nc.sbuf_tensor(name, shape, dt))

        def sem(name):
            return ctx.enter_context(nc.semaphore(name))

        ps = ctx.enter_context(nc.psum_tensor("ps", [P, 8, BANK], F32))

        raw = sb("raw", [P, RAW, CHUNK])
        w_hi = sb("w_hi", [P, SPLIT, UNIT], F32R)
        w_lo = sb("w_lo", [P, SPLIT, UNIT], F32R)
        ident = sb("ident", [P, P])
        wts = sb("wts", [P, S // P, 2])
        carry = sb("carry", [P, E])
        n_extra = sb("n_extra", [P, 1], I32)
        eps_t = sb("eps_t", [P, 1])
        asg_i = sb("asg_i", [P, NT, 2], I32)
        dest_i = sb("dest_i", [P, NT, 2], I32)
        slot_i = sb("slot_i", [P, E], I32)
        tok_i = sb("tok_i", [P, E], I32)

        p1 = ExitStack()
        part[0] = p1
        p0 = ExitStack()
        part[0] = p0
        rows01 = sb("rows01", [P, 3, D])[:, 1:3, :]
        gain_in = sb("gain_in", [P, D])
        x_in = sb("x_in", [P, TT, D])
        p0.close()
        part[0] = p1
        act_hi = sb("act_hi", [P, TT, KD, P], F32R)
        act_lo = sb("act_lo", [P, TT, KD, P], F32R)
        mid = sb("mid", [P, KD, HALF])
        zv = sb("zv", [P, KB * (HALF + 32)])
        zc = sb("zc", [P, KB, HALF])
        pw = sb("pw", [P, 2, KB, P])
        pool_wt = sb("pool_wt", [P, POOLS, P])
        chan = sb("chan", [P, KB, TAPS + 3])
        pscale = sb("pscale", [P, POOLS])
        ln_g = sb("ln_g", [P, KB, P])
        ln_b = sb("ln_b", [P, KB, P])
        wmT = sb("wmT", [P, KB, P])
        gate_b = sb("gate_b", [P, KB, P])
        rw = sb("rw", [P, KD, G + E])
        rb = sb("rb", [P, G + E])
        mean1 = sb("mean1", [P, P])
        tri = sb("tri", [P, P])
        ones = sb("ones", [P, P])
        inv = sb("inv", [P, POOLS, PLEAD])
        halo_z = sb("halo_z", [P, KB, LEAD])
        halo_x = sb("halo_x", [P, POOLS, PLEAD - 1])
        gcol = sb("gcol", [P, KD])
        lg_all = sb("lg_all", [P, NT, G + E])
        acc = sb("acc", [P, TT, G + E])
        ss = sb("ss", [P, TT])
        ss2 = sb("ss2", [P, TT, D // BANK])
        ms = sb("ms", [P, 8])
        std = sb("std", [P, 8])
        rstd = sb("rstd", [P, 8])
        vstat = sb("vstat", [P, TT, 6 * 2])
        vmean = sb("vmean", [P, TT, 2])
        vstd = sb("vstd", [P, TT])
        vrstd = sb("vrstd", [P, TT])
        iota_p = sb("iota_p", [P, P])
        asg_m = sb("asg_m", [P, NT, 2])

        xt = [mid[:, 4 * t:4 * t + 4, :].rearrange("p a b -> p (a b)") for t in range(TT)]
        sq_rows = zv[:, 0:D]
        h2_rows = [rows01[:, 0, :], rows01[:, 1, :], xt[2], xt[3]]
        xa, uT, vT = mid[:, 0:4, :], mid[:, 4:10, :], mid[:, 10:16, :]
        sig = [mid[:, j, :] for j in range(2)]
        ext, sums = (mid[:, 12:16, :].rearrange("p a b -> p (a b)")[:, k * 528:(k + 1) * 528]
                     for k in range(2))
        sums2 = mid[:, 12:16, :].rearrange("p a b -> p (a b)")[:, 2 * 528:3 * 528]
        z = zv[:, :].rearrange("p (j t) -> p j t", j=KB)
        zt = z[:, :, 0:HALF]
        gain = zc[:, 0:4, :].rearrange("p a b -> p (a b)")
        tgrp = [zv[:, t * BANK:(t + 1) * BANK] for t in range(TT)]
        sq_block = zv[:, TT * BANK:(TT + 1) * BANK]
        at = [0]

        def small(*shape):
            n = 1
            for v in shape:
                n *= v
            v = zv[:, at[0]:at[0] + n]
            at[0] += n
            assert at[0] <= KB * (HALF + 32)
            if len(shape) == 2:
                v = v.rearrange("p (a b) -> p a b", b=shape[1])
            if len(shape) == 3:
                v = v.rearrange("p (a b c) -> p a b c", b=shape[1], c=shape[2])
            return v

        lg = small(NT, 8)
        le = small(NT, E)
        top_g, top_e = small(NT, 8), small(NT, 8)
        idx_g, idx_e = small(NT, 8), small(NT, 8)
        gf, onehot_g = small(NT), small(NT, G)
        le8, prod8 = small(NT, 8), small(NT, 8)
        sh_g, sh_e = small(NT, G), small(NT, 8)
        ex_g, ex_e = small(NT, G), small(NT, 8)
        sum_g, sum_e, sum_p = small(NT), small(NT), small(NT)
        wk = small(NT, 2)
        ef, ge = small(NT, 2), small(NT)
        hot = small(NT, 2, E)
        both = small(NT, E)
        earlier = small(NT + 1, E)
        rank = small(NT, 2)
        dest_f = small(NT, 2)
        slot_f = small(E)
        hot_rank = zc[:, 0, :].rearrange("p (t k e) -> p t k e", t=NT, k=2)
        hot_asg = zc[:, 1, :].rearrange("p (t k e) -> p t k e", t=NT, k=2)
        at_slot = x_in[:, TT - 1, :].rearrange("p (t k s) -> p t k s", t=NT, k=2)

        p1.close()
        p2 = ExitStack()
        part[0] = p2
        xg = sb("xg", [P, D])
        xT_hi = sb("xT_hi", [P, KD, P], F32R)
        xT_lo = sb("xT_lo", [P, KD, P], F32R)
        silu = sb("silu", [P, FE])
        hid = sb("hid", [P, FE])
        hT_hi = sb("hT_hi", [P, KF, P], F32R)
        hT_lo = sb("hT_lo", [P, KF, P], F32R)
        yb = sb("yb", [P, D])
        ix_tok = sb("ix_tok", [P, 1], I32)
        ix_asg = sb("ix_asg", [P, 1], I32)
        ix_new = sb("ix_new", [P, 1], I32)
        over = sb("over", [P, 7, E])
        cum = sb("cum", [P, 7, E])
        allone = sb("allone", [P, 7 * E])
        code = sb("code", [P, 2, 7, E])
        iota_1 = sb("iota_1", [P, 1])
        tab_f = sb("tab_f", [P, 2])
        tab_i = sb("tab_i", [P, 2], I32)
        row_i = sb("row_i", [1, 2, 16], I32)
        gfin = sb("gfin", [P, D])
        xb = sb("xb", [P, 2, D])
        ye = sb("ye", [P, 2, 2, D])
        fst = sb("fst", [P, 2, 4])
        wcol = sb("wcol", [P, 2, 2])
        p2.close()

        raw_landed = [sem(f"raw_landed{i}") for i in range(RAW)]
        hi_ready = sem("hi_ready")
        lo_ready = sem("lo_ready")
        unit_done = sem("unit_done")
        const_now = sem("const_now")
        const_in = sem("const_in")
        const_set = sem("const_set")
        const_tr = sem("const_tr")
        const_ev = sem("const_ev")
        dve_set = sem("dve_set")
        waited = sem("waited")
        xin_landed = [sem(f"xin_landed{t}") for t in range(TT)]
        gin_landed = sem("gin_landed")
        xres_landed = sem("xres_landed")
        gain_landed = sem("gain_landed")
        a_ss, a_ms, a_std, a_rstd, a_xn = (sem(n) for n in ("a_ss", "a_ms", "a_std", "a_rstd", "a_xn"))
        a_tr, a_hi, a_lo = sem("a_tr"), sem("a_hi"), sem("a_lo")
        bank_read = [sem("bank_read0"), sem("bank_read1")]
        step = sem("step")
        tap = sem("tap")
        pool_d = sem("pool_d")
        pool_mm, pool_y = sem("pool_mm"), sem("pool_y")
        v_tr, v_tok, v_var, v_std, v_ln = (sem(n) for n in ("v_tr", "v_tok", "v_var", "v_std", "v_ln"))
        gate_mm, gated = sem("gate_mm"), sem("gated")
        c_mean, c_cent, c_sq, c_var, c_std, c_norm, c_act = (
            sem(n) for n in ("c_mean", "c_cent", "c_sq", "c_var", "c_std", "c_norm", "c_act"))
        pw_landed = [sem("pw_landed0"), sem("pw_landed1")]
        pw_mm = sem("pw_mm")
        pw_read = sem("pw_read")
        y_hi, y_lo = sem("y_hi"), sem("y_lo")
        x1_part = sem("x1_part")
        r_ss, r_ms, r_std, r_rstd, r_h2 = (sem(n) for n in ("r_ss", "r_ms", "r_std", "r_rstd", "r_h2"))
        r_tr, r_cols, r_lg, r_acc = sem("r_tr"), sem("r_cols"), sem("r_lg"), sem("r_acc")
        r_shift, r_exp, r_hot, r_rank, r_slot, r_table, r_dest = (
            sem(n) for n in ("r_shift", "r_exp", "r_hot", "r_rank", "r_slot", "r_table", "r_dest"))
        x1_free = sem("x1_free")
        h2_free = sem("h2_free")
        x1_stored, listed = sem("x1_stored"), sem("listed")
        h2_stored = [sem("h2_stored0"), sem("h2_stored1")]
        list_blank = sem("list_blank")
        slots = sem("slots")
        tab_ready, tab_out, tab_in, count_ready = (
            sem(n) for n in ("tab_ready", "tab_out", "tab_in", "count_ready"))
        m_zero, m_ix, m_gathered = sem("m_zero"), sem("m_ix"), sem("m_gathered")
        m_xtr, m_xhi, m_xlo = sem("m_xtr"), sem("m_xhi"), sem("m_xlo")
        m_silu, m_hid, m_htr, m_hhi, m_hlo = (
            sem(n) for n in ("m_silu", "m_hid", "m_htr", "m_hhi", "m_hlo"))
        m_y, m_ystored, m_yfree = sem("m_y"), sem("m_ystored"), sem("m_yfree")
        e_list, e_tok = sem("e_list"), sem("e_tok")
        f_landed = [sem("f_landed0"), sem("f_landed1")]
        f_gain = sem("f_gain")
        f_col, f_sum, f_sq, f_ms, f_std, f_rstd, f_out = (
            sem(n) for n in ("f_col", "f_sum", "f_sq", "f_ms", "f_std", "f_rstd", "f_out"))
        f_stored = [sem("f_stored0"), sem("f_stored1")]

        block = ctx.enter_context(nc.Block())


        def unit_free(turn, c, j):
            return 8 * turn + 2 * c + j + 1

        def multiplied(turn, c):
            return 8 * turn + 2 * c + FREE_UNITS

        def split_of(turn, c, j):
            return 8 * turn + 2 * c + j + 1 + FREE_RAW

        def half_turn(h):
            return h * (CH // RAW)

        def apart(engine):
            engine.sem_inc(waited, 1)

        INB = [4, 0, 4, 0]
        GATEB = [2, 3, 0, 1, 2, 3]
        NOW = 9
        PWB = [6, 7, 2, 3, 4, 5]
        OUT_TURN = NIN // RAW
        EXP_TURN = CM // RAW
        LOOP_TURN = EXP_TURN + NW // RAW
        LAST_TURN = CX // RAW - 1
        EXTRA_TURN = CX // RAW

        @block.sync
        def _(sp):
            def load(turn, c, source):
                sp.wait_ge(lo_ready, 8 * turn + 2 * c + 2)
                n = source.shape[-1]
                sp.dma_start(raw[:, c % RAW, :].rearrange("p (a b) -> p a b", b=n), source)\
                  .then_inc(raw_landed[c % RAW], 16)

            def w_in_tile(col):
                return w_in[:, bass.ds(col, P)].rearrange("(k p) n -> p k n", p=P)

            def load_up(turn, e):
                for c in range(NW):
                    w = (exp_w1 if c < 4 else exp_w3)[0]
                    v = w[bass.ds(e, 1), (c % 4) * 4 * P:(c % 4 + 1) * 4 * P, :]
                    load(turn, c, v.rearrange("e (k p) n -> p (e k) n", p=P))

            def load_down(turn, e):
                for f in range(KF):
                    load(turn, f, exp_w2[0][bass.ds(e, 1), f * P:(f + 1) * P, :].rearrange("e p n -> p e n"))

            rows = [(zv[0:TAPS, 0:DC], conv_dw_w[0])]
            rows += [(zv[TAPS + r:TAPS + r + 1, 0:DC], v) for r, v in enumerate((conv_dw_b, conv_ln_g, conv_ln_b))]
            rows += [(zv[0:POOLS, DC:DC + P], pool_scale[0].rearrange("(g c) -> g c", c=P)),
                     (zv[0:KD, DC + P:DC + 2 * P], norm_ffn[0].rearrange("(k c) -> k c", c=P)),
                     (zv[:, 1024:1024 + DB].rearrange("p (j s) -> p j s", j=KB), sgu_w[0].rearrange("j t s -> t j s"))]
            assert len(rows) + 2 == NOW
            for to, source in rows:
                sp.dma_start(to, source).then_inc(const_now, 16)

            with sp.Fori(0, HALVES) as h:
                sp.wait_ge(unit_done, multiplied(half_turn(h), 0))
                apart(sp)
                for t in range(TT):
                    sp.dma_start(x_in[:, t, :], x[bass.ds(h * HALF + t * P, P), :]).then_inc(xin_landed[t], 16)
                    if t == 0:
                        sp.dma_start(gain_in[:, :], norm_mix.to_broadcast([P, D])).then_inc(gin_landed, 16)
                with sp.Fori(0, KB // 2) as i:
                    for m in range(4):
                        col = DA + 2 * DB + (DC if m % 2 == 0 else 0) + (m // 2) * P
                        load(half_turn(h) + i, m, w_in_tile(i * (2 * P) + col))
                for c in range(12, NIN):
                    col = (c - 12) * P if c < 16 else DA + (DB if c < 22 else 0) + (c - 16) % KB * P
                    load(half_turn(h), c, w_in[:, col:col + P].rearrange("(k p) n -> p k n", p=P))
                with sp.Fori(0, D // BANK) as n:
                    for g in range(4):
                        v = w_out[0][g * 4 * P:(g + 1) * 4 * P, bass.ds(n * BANK, BANK)]
                        load(half_turn(h) + OUT_TURN + n, g, v.rearrange("(k p) n -> p k n", p=P))
            load_up(EXP_TURN, 0)
            with sp.Fori(0, E - 1) as i:
                load_up(LOOP_TURN + 3 * i, i + 1)
                load_down(LOOP_TURN + 3 * i + 2, i)
            load_down(LAST_TURN, E - 1)
            sp.wait_ge(count_ready, 1)
            n = sp.value_load(n_extra[0:1, 0:1], min_val=0, max_val=EXTRA)
            sp.wait_ge(tab_in, 32)
            with sp.Fori(0, EXTRA) as i:
                with sp.If(i < n):
                    e = sp.value_load(row_i[0:1, 1, bass.ds(i, 1)], min_val=0, max_val=E - 1)
                    load_up(EXTRA_TURN + 3 * i, e)
                    load_down(EXTRA_TURN + 3 * i + 2, e)
                    sp.nop()
            sp.wait_ge(m_yfree, n + (E + 1))

            def load_tile(i, k):
                sp.dma_start(xb[:, k, :], x1_d[bass.ds((2 * i + k) * P, P), :]).then_inc(f_landed[k], 16)
                rows = yd[bass.ds((2 * i + k) * (2 * P), 2 * P), :]
                sp.dma_start(ye[:, k, :, :], rows.rearrange("(p a) n -> p a n", a=2)).then_inc(f_landed[k], 16)

            for k in range(2):
                load_tile(0, k)
            with sp.Fori(1, S // P // 2) as i:
                for k in range(2):
                    sp.wait_ge(f_stored[k], 16 * i)
                    load_tile(i, k)

        @block.gpsimd
        def _(pool):
            pool.sem_inc(m_yfree, 1)
            pool.sem_inc(h2_free, 2 * FREE_ROWS)
            pool.sem_inc(x1_free, FREE_ROWS)

            wnat = zv[:, 1024:1024 + DB].rearrange("p (j s) -> p j s", j=KB)
            pool.memset(ident[:, :], 0.0).then_inc(const_set, 1)
            pool.memset(tri[:, :], 1.0).then_inc(const_set, 1)
            blank = xt[TT - 1].bitcast(I32)[:, 0:E * LISTED // P]
            pool.memset(blank, PADS).then_inc(const_set, 1)
            pool.wait_ge(const_set, 3)
            pool.affine_select(out=ident[:, :], in_=ident[:, :], compare_op=ALU.not_equal, fill=1.0, base=0,
                               pattern=[[-1, P]], channel_multiplier=1).then_inc(const_set, 1)
            pool.affine_select(out=tri[:, :], in_=tri[:, :], compare_op=ALU.is_gt, fill=0.0, base=0,
                               pattern=[[1, P]], channel_multiplier=-1).then_inc(const_set, 1)
            pool.wait_ge(const_now, 16 * NOW)
            pool.affine_select(out=wnat, in_=wnat, compare_op=ALU.is_ge, fill=0.0, base=0,
                               pattern=[[0, KB], [-1, P]], channel_multiplier=1).then_inc(const_set, 1)
            for to, pattern, base, mult in (
                    (iota_p[:, :], [[1, P]], 0, 0), (asg_i[:, :, :], [[2 * P, NT], [1, 2]], 0, 2),
                    (asg_m[:, :, :], [[2 * P, NT], [1, 2]], -PADS, 2),
                    (inv[:, :, :], [[0, POOLS], [1, PLEAD]], 1, 0)):
                pool.iota(to, pattern, base=base, channel_multiplier=mult,
                          allow_small_or_imprecise_dtypes=True).then_inc(const_set, 1)
            pool.dma_start(list_d.rearrange("(p n) o -> p (n o)", p=P), blank).then_inc(list_blank, 16)
            for to, source in (
                    (pool_wt[:, :, :], pool_w[0].rearrange("g c d -> c g d")),
                    (ln_g[:, :, :].rearrange("p a b -> p (a b)"), sgu_ln_g.to_broadcast([P, DB])),
                    (ln_b[:, :, :].rearrange("p a b -> p (a b)"), sgu_ln_b.to_broadcast([P, DB])),
                    (gate_b[:, :, :].rearrange("p a b -> p (a b)"),
                     sgu_b.rearrange("o j t -> o (j t)").to_broadcast([P, KB * P])),
                    (rb[:, 0:G], router_g_b.to_broadcast([P, G])),
                    (rb[:, G:], router_e_b.to_broadcast([P, E]))):
                pool.dma_start(to, source).then_inc(const_in, 16)

            with pool.Fori(0, HALVES) as h:
                def rows(t):
                    return bass.ds(h * HALF + t * P, P)

                for n in range(KB):
                    if n >= 2:
                        pool.wait_ge(pw_mm, h * KB + n - 1)
                        apart(pool)
                    pool.dma_start(pw[:, n % 2, :, :],
                                   conv_pw[0, :, n * P:(n + 1) * P].rearrange("(k p) n -> p k n", p=P))\
                        .then_inc(pw_landed[n % 2], 16)
                pool.wait_ge(pw_mm, h * KB + KB)
                apart(pool)
                pool.dma_start(gain, norm_ffn.to_broadcast([P, D])).then_inc(gain_landed, 16)
                pool.wait_ge(y_lo, h * KD + KD)
                apart(pool)
                by_tile = mid[:, :, :].rearrange("p (t a) b -> p t (a b)", t=TT)
                pool.dma_start(by_tile, x[bass.ds(h * HALF, HALF), :].rearrange("(t p) n -> p t n", p=P))\
                    .then_inc(xres_landed, 16)
                for n in range(D // BANK):
                    pool.wait_ge(x1_part, h * 16 + 4 * n + 4 + FREE_BLOCKS)
                    apart(pool)
                    cols = slice(n * BANK, (n + 1) * BANK)
                    pool.dma_start(x1_d[bass.ds(h * HALF, HALF), cols].rearrange("(t p) n -> p t n", p=P),
                                   by_tile[:, :, cols]).then_inc(x1_stored, 16)
                pool.wait_ge(x1_stored, h * 64 + 64)
                pool.sem_inc(x1_free, 1)
                for t in range(TT):
                    pool.wait_ge(r_h2, h * TT + t + 1)
                    apart(pool)
                    pool.dma_start(h2_d[bass.ds(h * HALF + t * P, P), :], h2_rows[t]).then_inc(h2_stored[t // 2], 16)
                for k in range(2):
                    pool.wait_ge(h2_stored[k], h * 32 + 32)
                    pool.sem_inc(h2_free, 1)

            pool.wait_ge(unit_done, multiplied(EXP_TURN, 0))
            pool.memset(xg[:, :], 0.0).then_inc(m_zero, 1)
            def gather(i, index):
                pool.indirect_dma_start(xg[:, :], None, h2_d,
                                        bass.IndirectOffsetOnAxis(ap=index.bitcast(U32), axis=0),
                                        bounds_check=S - 1, oob_is_err=False).then_inc(m_gathered, 16)
                pool.wait_ge(m_gathered, 16 * i + 16)
                apart(pool)

            def scatter(i):
                pool.wait_ge(m_y, 4 * i + 4 + FREE_BANK)
                apart(pool)
                index = ix_asg[:, :].bitcast(U32)
                pool.indirect_dma_start(yd, bass.IndirectOffsetOnAxis(ap=index, axis=0), yb[:, :], None,
                                        bounds_check=2 * S - 1, oob_is_err=False).then_inc(m_ystored, 16)
                pool.wait_ge(m_ystored, 16 * i + 16)
                apart(pool)
                pool.sem_inc(m_yfree, 1)

            pool.wait_ge(slots, 1)
            for i in range(2):
                if i:
                    pool.wait_ge(slots, 2)
                    pool.memset(allone[:, :], 1.0).then_inc(m_zero, 1)
                    pool.iota(iota_1[:, :], [[0, 1]], base=1, channel_multiplier=1,
                              allow_small_or_imprecise_dtypes=True).then_inc(m_zero, 1)
                    pool.iota(code[:, 0, :, :], [[1, 7], [EG, E]], base=1, channel_multiplier=0,
                              allow_small_or_imprecise_dtypes=True).then_inc(m_zero, 1)
                    pool.iota(code[:, 1, :, :], [[0, 7], [1, E]], base=0, channel_multiplier=0,
                              allow_small_or_imprecise_dtypes=True).then_inc(m_zero, 1)
                    pool.dma_start(gfin[:, :], norm_final.rearrange("(o n) -> o n", o=1).to_broadcast([P, D]))\
                        .then_inc(f_gain, 16)
                    pool.wait_ge(m_xtr, 4)
                pool.tensor_copy(ix_tok[:, :], tok_i[:, i:i + 1]).then_inc(m_ix, 1)
                pool.wait_ge(m_ix, i + 1)
                gather(i, ix_tok[:, :])
            pool.wait_ge(r_dest, 1)
            for t in range(NT):
                for k in range(2):
                    index = dest_i[:, t, k:k + 1].bitcast(U32)
                    pool.indirect_dma_start(list_d, bass.IndirectOffsetOnAxis(ap=index, axis=0),
                                            asg_i[:, t, k:k + 1], None,
                                            bounds_check=E * LISTED - 1, oob_is_err=False)\
                        .then_inc(listed, 16)
            pool.wait_ge(tab_ready, 1)
            for r in range(2):
                pool.dma_start(extra_d[r, :].rearrange("(n o) -> n o", o=1), tab_i[0:16, r:r + 1])\
                    .then_inc(tab_out, 16)
            pool.wait_ge(tab_out, 32)
            for r in range(2):
                pool.dma_start(row_i[0:1, r, :], extra_d[r:r + 1, :]).then_inc(tab_in, 16)
            pool.wait_ge(x1_stored, HALVES * (D // BANK) * 16)
            pool.wait_ge(listed, 2 * NT * 16)
            with pool.Fori(0, E - 2) as i:
                pool.wait_ge(m_xtr, 4 * i + 8)
                pool.tensor_copy(ix_tok[:, :], tok_i[:, bass.ds(i + 2, 1)]).then_inc(m_ix, 1)
                pool.wait_ge(m_ix, 2 * i + 3)
                apart(pool)
                gather(i + 2, ix_tok[:, :])
                pool.tensor_copy(ix_asg[:, :], slot_i[:, bass.ds(i, 1)]).then_inc(m_ix, 1)
                pool.wait_ge(m_ix, 2 * i + 4)
                scatter(i)
            for i in (E - 2, E - 1):
                pool.tensor_copy(ix_asg[:, :], slot_i[:, i:i + 1]).then_inc(m_ix, 1)
                pool.wait_ge(m_ix, E + i + 1)
                scatter(i)
            pool.wait_ge(count_ready, 1)
            n = pool.value_load(n_extra[0:1, 0:1], min_val=0, max_val=EXTRA)
            pool.wait_ge(tab_in, 32)
            with pool.Fori(0, EXTRA) as i:
                with pool.If(i < n):
                    r = pool.value_load(row_i[0:1, 0, bass.ds(i, 1)], min_val=0, max_val=E * EG - 1)
                    pool.dma_start(ix_asg[:, :], list_d[bass.ds(r * P, P), :]).then_inc(e_list, 16)
                    pool.wait_ge(e_list, 16 * i + 16)
                    pool.wait_ge(e_tok, i + 1)
                    apart(pool)
                    gather(i + E, ix_new[:, :])
                    scatter(i + E)

        @block.scalar
        def _(act):
            act.sem_inc(m_y, FREE_BANK)
            act.sem_inc(bank_read[0], FREE_BANK)
            act_fn = nc.scalar.activation

            def hi(turn, c):
                act.wait_ge(raw_landed[c % RAW], 16 * (turn + c // RAW + 1))
                for j in range(2):
                    act.wait_ge(unit_done, unit_free(turn, c, j))
                    act_fn(w_hi[:, (2 * c + j) % SPLIT, :], raw[:, c % RAW, j * UNIT:(j + 1) * UNIT],
                           ACT.Copy).then_inc(hi_ready, 1)

            act.dma_start(rw[:, :, 0:G], router_g_w[0].rearrange("(k p) n -> p k n", p=P)).then_inc(const_now, 16)
            act.dma_start(rw[:, :, G:], router_e_w[0].rearrange("(k p) n -> p k n", p=P)).then_inc(const_now, 16)

            act.wait_ge(const_tr, 2 * KB + 2)
            NC = TAPS + 3
            act_fn(chan[:, :, :].rearrange("p a b -> p (a b)"), ps[:, 0, 0:KB * NC], ACT.Copy).then_inc(const_ev, 1)
            act_fn(pscale[:, :], ps[:, 0, KB * NC:KB * NC + POOLS], ACT.Copy).then_inc(const_ev, 1)
            act_fn(gcol[:, :], ps[:, 0, KB * NC + POOLS:KB * NC + POOLS + KD], ACT.Copy).then_inc(const_ev, 1)
            act_fn(wmT[:, 0:4, :], ps[:, 1, :].rearrange("p (a b) -> p a b", a=4), ACT.Copy).then_inc(const_ev, 1)
            act_fn(wmT[:, 4:6, :], ps[:, 2, 0:2 * P].rearrange("p (a b) -> p a b", a=2), ACT.Copy)\
                .then_inc(const_ev, 1)
            act.wait_ge(dve_set, 2)

            with act.Fori(0, HALVES) as h:
                turn = half_turn(h)
                before = h * TT

                def round_input(t):
                    if t == 1:
                        act.wait_ge(h2_free, 2 * h + 1)
                    for q in range(4):
                        act.wait_ge(a_tr, h * 16 + 4 * t + q + 1)
                        act_fn(act_hi[:, t, 4 * q:4 * q + 4, :].rearrange("p k n -> p (k n)"),
                               ps[:, INB[t] + q, :], ACT.Copy).then_inc(a_hi, 1)

                act.wait_ge(unit_done, multiplied(turn, 0))
                act.wait_ge(r_acc, h * 4 + FREE_BANK)
                for t in range(TT):
                    act.wait_ge(xin_landed[t], h * 16 + 16)
                    if t:
                        act.wait_ge(a_ss, before + t)
                    act_fn(sq_rows, x_in[:, t, :], ACT.Square, accum_out=ss[:, t:t + 1]).then_inc(a_ss, 1)
                    act.wait_ge(a_ms, before + t + 1)
                    act_fn(std[:, t:t + 1], ms[:, t:t + 1], ACT.Sqrt).then_inc(a_std, 1)
                    if t:
                        round_input(t - 1)
                round_input(TT - 1)

                def read(c):
                    bank = ps[:, c % 2, :]
                    act.wait_ge(unit_done, multiplied(turn, c + 1))
                    if c < 12:
                        j = c // 2
                        if j >= 2:
                            act.wait_ge(bank_read[1], h * 14 + j)
                        if j == 0:
                            act.wait_ge(h2_free, 2 * h + 2 * FREE_ROWS)
                            act.wait_ge(list_blank, 16)
                        act_fn(sig[j % 2], bank, ACT.Sigmoid).then_inc(bank_read[0], 1)
                    elif c < 16:
                        if c > 12:
                            act.wait_ge(pool_d, h * POOLS + c - 12)
                        act_fn(ext[:, PLEAD:], bank, ACT.Copy).then_inc(bank_read[c % 2], 1)
                    elif c < 22:
                        if c == 16:
                            act.wait_ge(pool_d, h * POOLS + POOLS)
                        act_fn(vT[:, c - 16, :], bank, ACT.Gelu_apprx_tanh).then_inc(bank_read[c % 2], 1)
                    else:
                        act_fn(uT[:, c - 22, :], bank, ACT.Gelu_apprx_tanh).then_inc(bank_read[c % 2], 1)

                def read_pointwise(n0):
                    for n in range(KB):
                        act.wait_ge(pw_mm, h * KB + n + 1)
                        act_fn(zt[:, n, :], ps[:, PWB[n], :], ACT.Copy).then_inc(pw_read, 1)

                def v_tokens(t):
                    b = 2 + 2 * (t % 2)
                    act.wait_ge(v_tr, before + t + 1)
                    act_fn(vT[:, 0:4, t * P:(t + 1) * P], ps[:, b, :].rearrange("p (k n) -> p k n", k=4),
                           ACT.Copy).then_inc(v_tok, 1)
                    act_fn(vT[:, 4:6, t * P:(t + 1) * P],
                           ps[:, b + 1, 0:2 * P].rearrange("p (k n) -> p k n", k=2), ACT.Copy).then_inc(v_tok, 1)

                for c in range(NIN):
                    hi(turn, c)
                    if c and (c > 12 or c % 2 == 1):
                        read(c - 1)
                    if c == 19:
                        for g in range(POOLS):
                            act.wait_ge(pool_mm, h * POOLS + g + 1)
                            act_fn(xa[:, g, :], ps[:, 2 + g, :], ACT.Copy, scale=pscale[:, g:g + 1])\
                                .then_inc(pool_y, 1)
                    if c == 24:
                        for j in range(KB):
                            act.wait_ge(c_cent, h * KB + j + 1)
                            act_fn(zt[:, j, :], zc[:, j, :], ACT.Square).then_inc(c_sq, 1)
                    if c == 26:
                        act.wait_ge(c_var, h + 1)
                        act_fn(zt[:, 0, :], ps[:, 7, :], ACT.Sqrt, bias=eps_t[:, 0:1]).then_inc(c_std, 1)
                    if c == 24:
                        v_tokens(0)
                        v_tokens(1)
                    if c == 25:
                        v_tokens(2)
                        v_tokens(3)
                    if c == 27:
                        act.wait_ge(v_var, h + 1)
                        act_fn(vstd[:, :], vmean[:, :, 1], ACT.Sqrt, bias=eps_t[:, 0:1]).then_inc(v_std, 1)
                        for j in range(KB):
                            act.wait_ge(c_norm, h * KB + j + 1)
                            act_fn(zc[:, j, :], zc[:, j, :], ACT.Silu, bias=chan[:, j, TAPS + 2:TAPS + 3],
                                   scale=chan[:, j, TAPS + 1:TAPS + 2]).then_inc(c_act, 1)
                hi(turn + OUT_TURN, 0)
                read(NIN - 1)

                def y_round(k, source):
                    act_fn(act_hi[:, :, k, :], source.rearrange("p (t n) -> p t n", t=TT), ACT.Copy)\
                        .then_inc(y_hi, 1)

                act.wait_ge(pool_y, h * POOLS + POOLS)
                for g in range(POOLS):
                    y_round(g, xa[:, g, :])
                hi(turn + OUT_TURN, 1)
                read_pointwise(0)
                for j in range(KB):
                    act.wait_ge(gated, h * KB + j + 1)
                    y_round(POOLS + j, uT[:, j, :])
                act.wait_ge(pw_read, h * KB + KB)
                for n in range(KB):
                    y_round(POOLS + KB + n, zt[:, n, :])

                def of_block(n):
                    for t in range(TT):
                        act.wait_ge(x1_part, h * 16 + 4 * n + t + 1 + FREE_BLOCKS)
                        if n or t:
                            act.wait_ge(r_ss, h * 16 + 4 * n + t)
                        else:
                            act.wait_ge(y_lo, h * KD + KD)
                        act_fn(sq_block, xt[t][:, n * BANK:(n + 1) * BANK], ACT.Square,
                               accum_out=ss2[:, t, n:n + 1]).then_inc(r_ss, 1)
                    if n:
                        act.wait_ge(r_lg, h * 4 + n)
                    for t in range(TT):
                        act.wait_ge(r_tr, h * 16 + 4 * n + t + 1)
                        act_fn(tgrp[t], ps[:, (4 if n % 2 == 0 else 0) + t, :], ACT.Copy).then_inc(r_cols, 1)

                for n in range(4):
                    for c in range(2 if n == 0 else 0, RAW):
                        hi(turn + OUT_TURN + n, c)
                        if n and c == 2:
                            of_block(n - 1)
                of_block(3)
                act.wait_ge(r_ms, h + 1)
                act_fn(std[:, 4:8], ms[:, 4:8], ACT.Sqrt).then_inc(r_std, 1)

            act.wait_ge(r_shift, 1)
            act_fn(ex_g, sh_g, ACT.Exp).then_inc(r_exp, 1)
            act.wait_ge(r_shift, 2)
            act_fn(ex_e, sh_e, ACT.Exp).then_inc(r_exp, 1)

            def round_x(i, q):
                act.wait_ge(m_xtr, 4 * i + q + 1)
                act_fn(xT_hi[:, 4 * q:4 * q + 4, :], ps[:, 2 + q % 2, :].rearrange("p (k n) -> p k n", k=4),
                       ACT.Copy).then_inc(m_xhi, 1)

            def silu_of(i, turn, first=False):
                act.wait_ge(unit_done, multiplied(turn, 4))
                if not first:
                    act.wait_ge(m_hid, i)
                act_fn(silu[:, :], ps[:, 0, :], ACT.Silu).then_inc(m_silu, 1)

            def round_h(i):
                act.wait_ge(m_htr, i + 1)
                act_fn(hT_hi[:, :, :].rearrange("p k n -> p (k n)"), ps[:, 1, :], ACT.Copy).then_inc(m_hhi, 1)

            def read_y(i, turn, c):
                act.wait_ge(unit_done, multiplied(turn, c))
                act.wait_ge(m_yfree, i + 1)
                for b in range(4):
                    act_fn(yb[:, b * BANK:(b + 1) * BANK], ps[:, 4 + b, :], ACT.Copy).then_inc(m_y, 1)

            def chunks(turn, first, last):
                for c in range(first, last):
                    hi(turn, c)

            for q in range(4):
                round_x(0, q)
            chunks(EXP_TURN, 0, 6)
            silu_of(0, EXP_TURN, first=True)
            chunks(EXP_TURN, 6, 10)
            for q in range(4):
                round_x(1, q)

            def expert(i, more):
                turn = LOOP_TURN + 3 * i
                chunks(turn, 2, 3)
                round_h(i)
                chunks(turn, 3, 6)
                silu_of(i + 1, turn)
                chunks(turn, 6, 10)
                if more:
                    act.wait_ge(unit_done, multiplied(turn, NW))
                    round_x(i + 2, 0)
                    round_x(i + 2, 1)
                chunks(turn, 10, 11)
                if more:
                    round_x(i + 2, 2)
                chunks(turn, 11, 12)
                if more:
                    round_x(i + 2, 3)
                chunks(turn, 12, 14)
                read_y(i, turn, NE)

            with act.Fori(0, E - 2) as i:
                expert(i, True)
            expert(E - 2, False)
            round_h(E - 1)
            chunks(LAST_TURN, 2, 4)
            read_y(E - 1, LAST_TURN, 4)
            act.wait_ge(count_ready, 1)
            n = act.value_load(n_extra[0:1, 0:1], min_val=0, max_val=EXTRA)
            with act.Fori(0, EXTRA) as i:
                with act.If(i < n):
                    turn = EXTRA_TURN + 3 * i
                    for q in range(4):
                        round_x(i + E, q)
                    chunks(turn, 0, 6)
                    silu_of(i + E, turn)
                    chunks(turn, 6, 9)
                    round_h(i + E)
                    chunks(turn, 9, 12)
                    read_y(i + E, turn, NE)

            with act.Fori(0, S // P // 2) as i:
                for k in range(2):
                    act.wait_ge(f_sum, 4 * i + 2 * k + 2)
                    act_fn(ye[:, k, 0, :], xb[:, k, :], ACT.Square, accum_out=fst[:, k, 0:1]).then_inc(f_sq, 1)
                    act.wait_ge(f_ms, 2 * i + k + 1)
                    act_fn(fst[:, k, 2:3], fst[:, k, 1:2], ACT.Sqrt).then_inc(f_std, 1)
                    act.wait_ge(f_out, 2 * i + k + 1)
                    act.dma_start(out[bass.ds((2 * i + k) * P, P), :], ye[:, k, 1, :]).then_inc(f_stored[k], 16)
            for k in range(2):
                act.wait_ge(f_stored[k], 16 * (S // P // 2))

        @block.vector
        def _(dve):
            dve.sem_inc(lo_ready, FREE_RAW)
            dve.sem_inc(a_lo, FREE_TILES)
            dve.sem_inc(r_acc, FREE_BANK)
            dve.sem_inc(bank_read[1], FREE_BANK)
            dve.sem_inc(x1_part, FREE_BLOCKS)
            tt, ts, stt = nc.vector.tensor_tensor, nc.vector.tensor_scalar, nc.vector.scalar_tensor_tensor

            def lo(turn, c):
                for j in range(2):
                    s = (2 * c + j) % SPLIT
                    dve.wait_ge(hi_ready, 8 * turn + 2 * c + j + 1)
                    tt(w_lo[:, s, :], raw[:, c % RAW, j * UNIT:(j + 1) * UNIT], w_hi[:, s, :].bitcast(F32),
                       ALU.subtract).then_inc(lo_ready, 1)

            class Steps:

                def __init__(self, base):
                    self.base, self.n = base, 0

                def __call__(self, ins):
                    self.n += 1
                    ins.then_inc(step, 1)

                def wait(self):
                    dve.wait_ge(step, self.base + self.n)

                def then(self, ins):
                    self(ins)
                    self.wait()

            do = Steps(0)
            for v, to in ((EPS, eps_t[:, :]), (1.0 / DC, mean1[:, :]), (1.0, ones[:, :]), (0.0, halo_z[:, :, :]),
                          (0.0, halo_x[:, :, :])):
                do(nc.vector.memset(to, v))
            dve.wait_ge(const_set, 10)
            for g in range(POOLS):
                do(ts(inv[:, g, :], inv[:, g, :], float(2 << g), None, ALU.min))
            do.wait()
            nc.vector.reciprocal(inv[:, :, :], inv[:, :, :]).then_inc(dve_set, 1)
            dve.wait_ge(dve_set, 1)
            SET = do.n
            dve.wait_ge(const_ev, 5)
            dve.wait_ge(const_now, 16 * NOW)
            tt(rw[:, :, :], rw[:, :, :], gcol[:, :].unsqueeze(2).to_broadcast([P, KD, G + E]), ALU.mult)\
                .then_inc(dve_set, 1)

            with dve.Fori(0, HALVES) as h:
                turn = half_turn(h)
                before = h * TT
                do = Steps(h * STEPS + SET)

                def rest_of_input(t):
                    dve.wait_ge(a_tr, h * 16 + 4 * t + 4)
                    for q in range(4):
                        dve.wait_ge(a_hi, h * 16 + 4 * t + q + 1)
                        k4 = slice(4 * q, 4 * q + 4)
                        tt(act_lo[:, t, k4, :].rearrange("p k n -> p (k n)"), ps[:, INB[t] + q, :],
                           act_hi[:, t, k4, :].rearrange("p k n -> p (k n)").bitcast(F32),
                           ALU.subtract).then_inc(a_lo, 1)

                for t in range(TT):
                    dve.wait_ge(a_ss, before + t + 1)
                    ts(ms[:, t:t + 1], ss[:, t:t + 1], 1.0 / D, EPS, ALU.mult, ALU.add).then_inc(a_ms, 1)
                    dve.wait_ge(a_std, before + t + 1)
                    nc.vector.reciprocal(rstd[:, t:t + 1], std[:, t:t + 1]).then_inc(a_rstd, 1)
                    dve.wait_ge(a_rstd, before + t + 1)
                    if t == 0:
                        dve.wait_ge(gin_landed, h * 16 + 16)
                    stt(x_in[:, t, :], x_in[:, t, :], rstd[:, t:t + 1], gain_in[:, :], ALU.mult, ALU.mult)\
                        .then_inc(a_xn, 1)
                    if t:
                        rest_of_input(t - 1)
                rest_of_input(TT - 1)

                do.then(nc.vector.tensor_copy(z[:, :, 2:32], halo_z[:, :, :]))

                def gated_value(j):
                    dve.wait_ge(bank_read[0], h * 14 + j + 1 + FREE_BANK)
                    dve.wait_ge(unit_done, multiplied(turn, 2 * j + 2))
                    tt(z[:, j, 32:], ps[:, 1, :], sig[j % 2], ALU.mult).then_inc(bank_read[1], 1)

                def taps(first, last):
                    for m in range(first, last):
                        i, j = divmod(m % (2 * TAPS), 2)
                        j += 2 * (m // (2 * TAPS))
                        source = z[:, j, 2 + i:2 + i + HALF]
                        w = chan[:, j, i:i + 1]
                        if i == 0:
                            dve.wait_ge(bank_read[1], h * 14 + j + 1 + FREE_BANK)
                            ts(zc[:, j, :], source, w, chan[:, j, TAPS:TAPS + 1], ALU.mult, ALU.add)\
                                .then_inc(tap, 1)
                        else:
                            dve.wait_ge(tap, h * (KB * TAPS) + m - 1)
                            stt(zc[:, j, :], source, w, zc[:, j, :], ALU.mult, ALU.add).then_inc(tap, 1)

                def pooled(g):
                    c = 12 + g
                    do(nc.vector.tensor_copy(ext[:, 1:PLEAD], halo_x[:, g, :]))
                    dve.wait_ge(bank_read[c % 2], h * 14 + c // 2 + 1 + FREE_BANK)
                    do.wait()
                    a = ext
                    for n in range(g + 1):
                        b = (sums, sums2)[n % 2]
                        at0, s = 2 << n, 1 << n
                        do.then(tt(b[:, at0:], a[:, at0:], a[:, at0 - s:-s], ALU.add))
                        a = b
                    do.then(tt(a[:, PLEAD:2 * PLEAD], a[:, PLEAD:2 * PLEAD], inv[:, g, :], ALU.mult))
                    do(nc.vector.memset(inv[:, g, :], 1.0 / (2 << g)))
                    do(nc.vector.tensor_copy(halo_x[:, g, :], ext[:, -PLEAD + 1:]))
                    do(tt(xa[:, g, 0:PLEAD], a[:, PLEAD:2 * PLEAD], ext[:, PLEAD:2 * PLEAD], ALU.subtract))
                    stt(xa[:, g, PLEAD:], a[:, 2 * PLEAD:], 1.0 / (2 << g), ext[:, 2 * PLEAD:],
                        ALU.mult, ALU.subtract).then_inc(pool_d, 1)

                def v_stats(t):
                    dve.wait_ge(v_tok, 2 * before + 2 * t + 2)
                    for n in range(2):
                        do(nc.vector.bn_stats(vstat[:, t, 6 * n:6 * n + 6],
                                              vT[:, 3 * n:3 * n + 3, t * P:(t + 1) * P]))
                    do.wait()
                    apart(dve)
                    ins = nc.vector.bn_aggr(vmean[:, t, :], vstat[:, t, :])
                    if t < TT - 1:
                        do(ins)
                    else:
                        ins.then_inc(v_var, 1)

                def v_norm(t):
                    v = vT[:, :, t * P:(t + 1) * P]
                    do.then(ts(v, v, vmean[:, t, 0:1], vrstd[:, t:t + 1], ALU.subtract, ALU.mult))
                    do.then(tt(v, v, ln_g[:, :, :], ALU.mult))
                    tt(v, v, ln_b[:, :, :], ALU.add).then_inc(v_ln, 1)

                done = 0
                for c in range(NIN):
                    lo(turn, c)
                    if 2 <= c <= 12 and c % 2 == 0:
                        gated_value(c // 2 - 1)
                    if c == 13:
                        dve.wait_ge(list_blank, 16)
                        dve.wait_ge(const_in, 16 * 6)
                    if 13 <= c <= 16:
                        pooled(c - 13)
                    if c == 24:
                        dve.wait_ge(c_mean, h + 1)
                        for j in range(KB):
                            tt(zc[:, j, :], zc[:, j, :], ps[:, 6, :], ALU.subtract).then_inc(c_cent, 1)
                    if c == 25:
                        v_stats(0)
                        v_stats(1)
                    if c == 26:
                        v_stats(2)
                        v_stats(3)
                    if c == 27:
                        dve.wait_ge(c_std, h + 1)
                        do.then(nc.vector.reciprocal(zt[:, 1, :], zt[:, 0, :]))
                        for j in range(KB):
                            tt(zc[:, j, :], zc[:, j, :], zt[:, 1, :], ALU.mult).then_inc(c_norm, 1)
                    if c == 27:
                        dve.wait_ge(v_std, h + 1)
                        do.then(nc.vector.reciprocal(vrstd[:, :], vstd[:, :]))
                        for t in range(TT):
                            v_norm(t)
                    if 4 <= c <= 22:
                        last = min(KB * TAPS, done + (6 if 13 <= c <= 16 else 10 if c < 13 else 12))
                        taps(done, last)
                        done = last
                    if c == 22:
                        assert done == KB * TAPS
                        dve.wait_ge(tap, h * (KB * TAPS) + KB * TAPS)
                        do.then(nc.vector.tensor_copy(halo_z[:, :, :], z[:, :, 2 + HALF:]))

                def y_rest(k, source):
                    dve.wait_ge(y_hi, h * KD + k + 1)
                    tt(act_lo[:, :, k, :], source.rearrange("p (t n) -> p t n", t=TT),
                       act_hi[:, :, k, :].bitcast(F32), ALU.subtract).then_inc(y_lo, 1)

                def gate(j):
                    dve.wait_ge(gate_mm, h * KB + j + 1)
                    g = ps[:, GATEB[j], :].rearrange("p (n t) -> p n t", n=TT)
                    do.then(tt(g, g, gate_b[:, j:j + 1, :].to_broadcast([P, TT, P]), ALU.add))
                    tt(uT[:, j, :], ps[:, GATEB[j], :], uT[:, j, :], ALU.mult).then_inc(gated, 1)

                lo(turn + OUT_TURN, 0)
                for g in range(POOLS):
                    y_rest(g, xa[:, g, :])
                lo(turn + OUT_TURN, 1)
                gate(0)
                for j in range(KB):
                    if j < KB - 1:
                        gate(j + 1)
                    y_rest(POOLS + j, uT[:, j, :])
                for n in range(KB):
                    y_rest(POOLS + KB + n, zt[:, n, :])

                def add_rows(n, sub):
                    dve.wait_ge(unit_done, multiplied(turn + OUT_TURN + n, RAW))
                    for t in range(TT):
                        to = xt[t][:, bass.ds(n * BANK, BANK)]
                        if n == 0:
                            dve.wait_ge(xres_landed, h * 16 + 16)
                        tt(to, to, ps[:, (4 if sub == 0 else 0) + t, :], ALU.add).then_inc(x1_part, 1)

                def add_logits(n):
                    dve.wait_ge(r_lg, h * 4 + n + 1)
                    part_ = ps[:, 4 if n % 2 == 0 else 0, 0:TT * (G + E)].rearrange("p (t n) -> p t n", t=TT)
                    if n == 0:
                        ins = nc.vector.tensor_copy(acc[:, :, :], part_)
                    else:
                        dve.wait_ge(r_acc, h * 4 + n + FREE_BANK)
                        ins = tt(acc[:, :, :], acc[:, :, :], part_, ALU.add)
                    ins.then_inc(r_acc, 1)

                for n in range(4):
                    lo(turn + OUT_TURN + n, 2)
                    lo(turn + OUT_TURN + n, 3)
                    if n:
                        add_logits(n - 1)
                    if n < 3:
                        lo(turn + OUT_TURN + n + 1, 0)
                    add_rows(n, n % 2)
                    if n < 3:
                        lo(turn + OUT_TURN + n + 1, 1)

                dve.wait_ge(r_ss, h * 16 + 16)
                do.then(nc.vector.tensor_reduce(ms[:, 0:4], ss2[:, :, :], AX.X, ALU.add))
                ts(ms[:, 4:8], ms[:, 0:4], 1.0 / D, EPS, ALU.mult, ALU.add).then_inc(r_ms, 1)
                dve.wait_ge(r_std, h + 1)
                nc.vector.reciprocal(rstd[:, 4:8], std[:, 4:8]).then_inc(r_rstd, 1)
                dve.wait_ge(r_rstd, h + 1)
                add_logits(3)
                dve.wait_ge(r_acc, h * 4 + 4 + FREE_BANK)
                do(tt(lg_all[:, bass.ds(before, TT), :], acc[:, :, :],
                      rstd[:, 4:8].unsqueeze(2).to_broadcast([P, TT, G + E]), ALU.mult))
                dve.wait_ge(gain_landed, h * 16 + 16)
                for t in range(TT):
                    if t == 2:
                        dve.wait_ge(x1_free, h + 1 + FREE_ROWS)
                    stt(h2_rows[t], xt[t], rstd[:, 4 + t:5 + t], gain, ALU.mult, ALU.mult).then_inc(r_h2, 1)
                do.wait()
                assert do.n == STEPS, f"STEPS = {do.n}"

            do = Steps(SET + HALVES * STEPS)
            dve.wait_ge(r_h2, NT)

            def over_tiles(v, n):
                return v.unsqueeze(1).to_broadcast([P, NT, n])

            def over_last(v, n):
                return v.unsqueeze(2).to_broadcast([P, NT, n])

            do(nc.vector.memset(lg[:, :, G:], -3.0e38))
            do(tt(lg[:, :, 0:G], lg_all[:, :, 0:G], over_tiles(rb[:, 0:G], G), ALU.add))
            do.then(tt(le, lg_all[:, :, G:], over_tiles(rb[:, G:], E), ALU.add))
            for t in range(NT):
                do(nc.vector.max(top_g[:, t, :], lg[:, t, :]))
            do.wait()
            tt(sh_g, lg[:, :, 0:G], top_g[:, :, 0:1].to_broadcast([P, NT, G]), ALU.subtract).then_inc(r_shift, 1)
            for t in range(NT):
                do(nc.vector.max_index(idx_g.bitcast(U32)[:, t, :], top_g[:, t, :], lg[:, t, :]))
            do.wait()
            do.then(nc.vector.tensor_copy(gf, idx_g.bitcast(U32)[:, :, 0]))
            do.then(tt(onehot_g, over_tiles(iota_p[:, 0:G], G), over_last(gf, G), ALU.is_equal))
            for g in range(G):
                one = onehot_g[:, :, g:g + 1].to_broadcast([P, NT, EG])
                if g == 0:
                    do.then(tt(le8, le[:, :, 0:EG], one, ALU.mult))
                else:
                    do.then(tt(prod8, le[:, :, g * EG:(g + 1) * EG], one, ALU.mult))
                    do.then(tt(le8, le8, prod8, ALU.add))
            for t in range(NT):
                do(nc.vector.max(top_e[:, t, :], le8[:, t, :]))
            do.wait()
            tt(sh_e, le8, top_e[:, :, 0:1].to_broadcast([P, NT, EG]), ALU.subtract).then_inc(r_shift, 1)
            for t in range(NT):
                do(nc.vector.max_index(idx_e.bitcast(U32)[:, t, :], top_e[:, t, :], le8[:, t, :]))
            do(ts(ge, gf, float(EG), None, ALU.mult))
            do.wait()
            do.then(nc.vector.tensor_copy(wk, idx_e.bitcast(U32)[:, :, 0:2]))
            do.then(tt(ef, wk, ge.unsqueeze(2).to_broadcast([P, NT, 2]), ALU.add))
            for k in range(2):
                do(tt(hot[:, :, k, :], over_tiles(iota_p[:, 0:E], E), over_last(ef[:, :, k], E), ALU.is_equal))
            do.wait()
            do(nc.vector.memset(earlier[:, 0, :], 0.0))
            do.then(tt(both, hot[:, :, 0, :], hot[:, :, 1, :], ALU.add))
            for t in range(NT):
                do.then(tt(earlier[:, t + 1, :], earlier[:, t, :], both[:, t, :], ALU.add))
            nc.vector.sem_inc(r_hot, 1)
            do(tt(hot_asg, hot, asg_m[:, :, :].unsqueeze(3).to_broadcast([P, NT, 2, E]), ALU.mult))
            dve.wait_ge(r_rank, 1)
            counted = ps[:, 7, 0:NT * E].rearrange("p (t o e) -> p t o e", t=NT, o=1)
            do.then(tt(hot_rank, hot, counted.to_broadcast([P, NT, 2, E]), ALU.mult))
            do.then(nc.vector.tensor_reduce(rank, hot_rank, AX.X, ALU.add))
            tt(at_slot, iota_p[:, :].unsqueeze(1).unsqueeze(1).to_broadcast([P, NT, 2, P]),
               rank.unsqueeze(3).to_broadcast([P, NT, 2, P]), ALU.is_equal).then_inc(r_slot, 1)
            do(nc.vector.tensor_copy(carry[:, :], ps[:, 7, NT * E:(NT + 1) * E]))
            do.then(stt(dest_f, ef, float(LISTED), rank, ALU.mult, ALU.add))
            nc.vector.tensor_copy(dest_i[:, :, :], dest_f).then_inc(r_dest, 1)
            dve.wait_ge(r_table, 1)
            do.then(ts(slot_f, ps[:, 6, 0:E], float(PADS), None, ALU.add))
            do.then(nc.vector.tensor_copy(slot_i[:, :], slot_f))
            do.then(ts(tok_i[:, :], slot_i[:, :], 1, None, ALU.logical_shift_right))
            nc.vector.sem_inc(slots, 1)
            dve.wait_ge(r_exp, 2)
            for k in range(2):
                do.then(tt(prod8, over_tiles(iota_p[:, 0:EG], EG), over_last(wk[:, :, k], EG), ALU.is_equal))
                do.then(tt(prod8, prod8, ex_e, ALU.mult))
                do.then(nc.vector.tensor_reduce(wk[:, :, k:k + 1], prod8, AX.X, ALU.add))
            do(nc.vector.tensor_reduce(sum_g, ex_g, AX.X, ALU.add))
            do(nc.vector.tensor_reduce(sum_e, ex_e, AX.X, ALU.add))
            do.wait()
            do(nc.vector.reciprocal(sum_g, sum_g))
            do(nc.vector.reciprocal(sum_e, sum_e))
            do.wait()
            do.then(tt(wk, wk, sum_e.unsqueeze(2).to_broadcast([P, NT, 2]), ALU.mult))
            do.then(tt(sum_p, wk[:, :, 0], wk[:, :, 1], ALU.add))
            do(nc.vector.reciprocal(sum_p, sum_p))
            do.then(tt(wk, wk, sum_g.unsqueeze(2).to_broadcast([P, NT, 2]), ALU.mult))
            do.then(tt(wts[:, :, :], wk, sum_p.unsqueeze(2).to_broadcast([P, NT, 2]), ALU.mult))
            nc.vector.sem_inc(slots, 1)

            def rest_of_x(i, q):
                dve.wait_ge(m_xhi, 4 * i + q + 1)
                tt(xT_lo[:, 4 * q:4 * q + 4, :], ps[:, 2 + q % 2, :].rearrange("p (k n) -> p k n", k=4),
                   xT_hi[:, 4 * q:4 * q + 4, :].bitcast(F32), ALU.subtract).then_inc(m_xlo, 1)

            def hidden(i, turn, first=False):
                dve.wait_ge(m_silu, i + 1)
                dve.wait_ge(unit_done, multiplied(turn, NW))
                if not first:
                    dve.wait_ge(m_htr, i)
                tt(hid[:, :], ps[:, 1, :], silu[:, :], ALU.mult).then_inc(m_hid, 1)

            def rest_of_h(i):
                dve.wait_ge(m_hhi, i + 1)
                tt(hT_lo[:, :, :].rearrange("p k n -> p (k n)"), ps[:, 1, :],
                   hT_hi[:, :, :].rearrange("p k n -> p (k n)").bitcast(F32), ALU.subtract).then_inc(m_hlo, 1)

            def chunks(turn, first, last):
                for c in range(first, last):
                    lo(turn, c)

            for q in range(4):
                rest_of_x(0, q)

            dve.wait_ge(m_zero, 5)
            for b in range(7):
                do(ts(over[:, b, :], carry[:, :], float(P * (b + 1)), None, ALU.is_gt))
            do.wait()
            flat = over[:, :, :].rearrange("p b e -> p (b e)")
            flat_cum = cum[:, :, :].rearrange("p b e -> p (b e)")
            do.then(nc.vector.tensor_tensor_scan(flat_cum, allone[:, :], flat, 0.0, ALU.mult, ALU.add))
            nc.vector.tensor_copy(n_extra[:, :], cum[:, 6, E - 1:E]).then_inc(count_ready, 1)
            dve.wait_ge(count_ready, 1)
            do.then(tt(flat_cum, flat_cum, flat, ALU.mult))
            for r in range(2):
                do.then(stt(flat, flat_cum, iota_1[:, 0:1], code[:, r, :, :].rearrange("p b e -> p (b e)"),
                            ALU.is_equal, ALU.mult, accum_out=tab_f[:, r:r + 1]))
            nc.vector.tensor_copy(tab_i[:, :], tab_f[:, :]).then_inc(tab_ready, 1)

            chunks(EXP_TURN, 0, 9)
            hidden(0, EXP_TURN, first=True)
            for q in range(4):
                rest_of_x(1, q)
            chunks(EXP_TURN, 9, 10)

            def expert(i, more):
                turn = LOOP_TURN + 3 * i
                chunks(turn, 2, 3)
                rest_of_h(i)
                chunks(turn, 3, 10)
                hidden(i + 1, turn)
                if more:
                    rest_of_x(i + 2, 0)
                    rest_of_x(i + 2, 1)
                chunks(turn, 10, 11)
                if more:
                    rest_of_x(i + 2, 2)
                chunks(turn, 11, 12)
                if more:
                    rest_of_x(i + 2, 3)
                chunks(turn, 12, 14)

            with dve.Fori(0, E - 2) as i:
                expert(i, True)
            expert(E - 2, False)
            rest_of_h(E - 1)
            chunks(LAST_TURN, 2, 4)
            n = dve.value_load(n_extra[0:1, 0:1], min_val=0, max_val=EXTRA)
            with dve.Fori(0, EXTRA) as i:
                with dve.If(i < n):
                    turn = EXTRA_TURN + 3 * i
                    dve.wait_ge(e_list, 16 * i + 16)
                    ts(ix_new[:, :], ix_asg[:, :], 1, None, ALU.logical_shift_right).then_inc(e_tok, 1)
                    for q in range(4):
                        rest_of_x(i + E, q)
                    chunks(turn, 0, 8)
                    hidden(i + E, turn)
                    chunks(turn, 8, 9)
                    rest_of_h(i + E)
                    chunks(turn, 9, 12)

            dve.wait_ge(f_gain, 16)
            with dve.Fori(0, S // P // 2) as i:
                for k in range(2):
                    nc.vector.tensor_copy(wcol[:, k, :], wts[:, bass.ds(2 * i + k, 1), :]).then_inc(f_col, 1)
                    dve.wait_ge(f_col, 2 * i + k + 1)
                    dve.wait_ge(f_landed[k], 32 * i + 32)
                    for a in range(2):
                        stt(xb[:, k, :], ye[:, k, a, :], wcol[:, k, a:a + 1], xb[:, k, :], ALU.mult, ALU.add)\
                            .then_inc(f_sum, 1)
                        dve.wait_ge(f_sum, 4 * i + 2 * k + a + 1)
                    dve.wait_ge(f_sq, 2 * i + k + 1)
                    ts(fst[:, k, 1:2], fst[:, k, 0:1], 1.0 / D, EPS, ALU.mult, ALU.add).then_inc(f_ms, 1)
                    dve.wait_ge(f_std, 2 * i + k + 1)
                    nc.vector.reciprocal(fst[:, k, 3:4], fst[:, k, 2:3]).then_inc(f_rstd, 1)
                    dve.wait_ge(f_rstd, 2 * i + k + 1)
                    stt(ye[:, k, 1, :], xb[:, k, :], fst[:, k, 3:4], gfin[:, :], ALU.mult, ALU.mult)\
                        .then_inc(f_out, 1)

        @block.tensor
        def _(pe):
            pe.sem_inc(unit_done, FREE_UNITS)
            mm = nc.tensor.matmul

            def transposes(source, bank, count, done, n=P):
                for a in range(count):
                    last = nc.tensor.transpose(ps[:, bank, a * P:(a + 1) * P], source(a), ident[:, :])
                last.then_inc(done, 1)

            def three(out_, s_hi, s_lo, m_hi, m_lo, start, stop):
                mm(out_, s_hi, m_hi, start=start, stop=False)
                mm(out_, s_hi, m_lo, start=False, stop=False)
                return mm(out_, s_lo, m_hi, start=False, stop=stop)

            pe.wait_ge(const_set, 6)
            NC = TAPS + 3
            for j in range(KB):
                nc.tensor.transpose(ps[:, 0, j * NC:(j + 1) * NC], zv[0:NC, j * P:(j + 1) * P], ident[0:NC, 0:NC])\
                    .then_inc(const_tr, 1)
            nc.tensor.transpose(ps[:, 0, KB * NC:KB * NC + POOLS], zv[0:POOLS, DC:DC + P], ident[0:POOLS, 0:POOLS])\
                .then_inc(const_tr, 1)
            at_ = KB * NC + POOLS
            nc.tensor.transpose(ps[:, 0, at_:at_ + KD], zv[0:KD, DC + P:DC + 2 * P], ident[0:KD, 0:KD])\
                .then_inc(const_tr, 1)
            for j in range(KB):
                nc.tensor.transpose(ps[:, 1 + j // 4, (j % 4) * P:(j % 4 + 1) * P],
                                    zv[:, 1024 + j * P:1024 + (j + 1) * P], ident[:, :]).then_inc(const_tr, 1)
            pe.wait_ge(const_ev, 5)
            pe.wait_ge(dve_set, 2)

            with pe.Fori(0, HALVES) as h:
                turn = half_turn(h)
                before = h * TT

                pe.wait_ge(r_acc, h * 4 + FREE_BANK)
                for t in range(TT):
                    pe.wait_ge(a_xn, before + t + 1)
                    pe.wait_ge(a_lo, h * 16 + 4 * t + 4)
                    for q in range(4):
                        transposes(lambda a: x_in[:, t, (4 * q + a) * P:(4 * q + a + 1) * P], INB[t] + q, 4, a_tr)
                pe.wait_ge(a_lo, h * 16 + 16 + FREE_TILES)

                def product(unit, m, reads):
                    pe.wait_ge(bank_read[m], h * 14 + reads + FREE_BANK)
                    for j in range(2):
                        s = 2 * m + j
                        pe.wait_ge(lo_ready, unit + s + 1 + FREE_RAW)
                        for k in range(8):
                            cols = slice(k * P, (k + 1) * P)
                            last = three(ps[:, m, :].rearrange("p (t n) -> p t n", t=TT), w_hi[:, s, cols], w_lo[:, s, cols],
                                         act_hi[:, :, 8 * j + k, :], act_lo[:, :, 8 * j + k, :],
                                         j == 0 and k == 0, j == 1 and k == 7)
                        last.then_inc(unit_done, 1)

                def pairs(first, last):
                    with pe.Fori(first, last) as i:
                        for m in range(2):
                            product(h * UH + 4 * i, m, i)

                def v_transposes(t):
                    b = 2 + 2 * (t % 2)
                    for a in range(KB):
                        last = nc.tensor.transpose(ps[:, b + a // 4, (a % 4) * P:(a % 4 + 1) * P],
                                                   vT[:, a, t * P:(t + 1) * P], ident[:, :])
                    last.then_inc(v_tr, 1)

                apart(pe)
                pairs(0, 9)
                pe.wait_ge(pool_d, h * POOLS + POOLS)
                pe.wait_ge(const_in, 16 * 6)
                for g in range(POOLS):
                    mm(ps[:, 2 + g, :], pool_wt[:, g, :], xa[:, g, :], start=True, stop=True).then_inc(pool_mm, 1)
                pairs(9, 11)
                product(h * UH + 44, 0, 11)
                pe.wait_ge(tap, h * (KB * TAPS) + KB * TAPS)
                for j in range(KB):
                    last = mm(ps[:, 6, :], mean1[:, :], zc[:, j, :], start=j == 0, stop=j == KB - 1)
                last.then_inc(c_mean, 1)
                pe.wait_ge(bank_read[1], h * 14 + 11 + FREE_BANK)
                pe.wait_ge(pool_y, h * POOLS + POOLS)
                v_transposes(0)
                v_transposes(1)
                product(h * UH + 44, 1, 11)
                pe.wait_ge(v_tok, 2 * before + 4)
                v_transposes(2)
                v_transposes(3)
                product(h * UH + 48, 0, 12)
                product(h * UH + 48, 1, 12)
                for j in range(KB):
                    pe.wait_ge(c_sq, h * KB + j + 1)
                    last = mm(ps[:, 7, :], mean1[:, :], zt[:, j, :], start=j == 0, stop=j == KB - 1)
                last.then_inc(c_var, 1)
                pairs(13, 14)
                pe.wait_ge(c_act, h * KB + KB)
                pe.wait_ge(v_tok, 2 * before + 2 * TT)
                for n in range(KB):
                    pe.wait_ge(pw_landed[n % 2], h * 48 + 16 * (n // 2) + 16)
                    for k in range(KB):
                        last = mm(ps[:, PWB[n], :], pw[:, n % 2, k, :], zc[:, k, :], start=k == 0, stop=k == KB - 1)
                    last.then_inc(pw_mm, 1)

                pe.wait_ge(v_ln, before + TT)
                pe.wait_ge(pw_read, h * KB + KB)

                def gates(j):
                    if j in (2, 3):
                        pe.wait_ge(bank_read[j - 2], h * 14 + 14 + FREE_BANK)
                    if j >= 4:
                        pe.wait_ge(gated, h * KB + j - 3)
                    for t in range(TT):
                        cols = slice(t * P, (t + 1) * P)
                        last = mm(ps[:, GATEB[j], cols], vT[:, j, cols], wmT[:, j, :], start=True, stop=True)
                    last.then_inc(gate_mm, 1)

                for j in range(4):
                    gates(j)

                def columns(n):
                    for t in range(TT):
                        pe.wait_ge(x1_part, h * 16 + 4 * n + t + 1 + FREE_BLOCKS)
                        transposes(lambda a: xt[t][:, (4 * n + a) * P:(4 * n + a + 1) * P],
                                   (4 if n % 2 == 0 else 0) + t, 4, r_tr)

                def logits(n):
                    pe.wait_ge(r_cols, h * 16 + 4 * n + 4)
                    for t in range(TT):
                        for a in range(4):
                            last = mm(ps[:, 4 if n % 2 == 0 else 0, t * (G + E):(t + 1) * (G + E)],
                                      tgrp[t][:, a * P:(a + 1) * P], rw[:, 4 * n + a, :],
                                      start=a == 0, stop=a == 3)
                    last.then_inc(r_lg, 1)

                for n in range(D // BANK):
                    if n >= 2:
                        pe.wait_ge(r_acc, h * 4 + n - 1 + FREE_BANK)
                    for g in range(4):
                        for j in range(2):
                            s = (2 * g + j) % SPLIT
                            pe.wait_ge(lo_ready, split_of(turn + OUT_TURN + n, g, j))
                            for a in range(2):
                                k = 4 * g + 2 * j + a
                                cols = slice(a * BANK, (a + 1) * BANK)
                                if n == 0:
                                    pe.wait_ge(y_lo, h * KD + k + 1)
                                for t in range(TT):
                                    last = three(ps[:, (4 if n % 2 == 0 else 0) + t, :],
                                                 act_hi[:, t, k, :], act_lo[:, t, k, :],
                                                 w_hi[:, s, cols], w_lo[:, s, cols], k == 0, k == KD - 1)
                            last.then_inc(unit_done, 1)
                        if n == 0 and g == 0:
                            gates(4)
                            gates(5)
                        if n and g == 0:
                            columns(n - 1)
                        if n and g == 1:
                            logits(n - 1)
                columns(3)
                logits(3)

            pe.wait_ge(r_hot, 1)
            mm(ps[:, 7, 0:(NT + 1) * E], ones[:, :], earlier.rearrange("p t e -> p (t e)"), start=True, stop=False)
            mm(ps[:, 7, 0:NT * E], tri[:, :], both.rearrange("p t e -> p (t e)"), start=False, stop=True)\
                .then_inc(r_rank, 1)
            pe.wait_ge(r_slot, 1)
            for t in range(NT):
                for k in range(2):
                    last = mm(ps[:, 6, 0:E], at_slot[:, t, k, :], hot_asg[:, t, k, :],
                              start=t == 0 and k == 0, stop=t == NT - 1 and k == 1)
            last.then_inc(r_table, 1)


            def x_columns(i, q):
                if q == 0:
                    pe.wait_ge(m_gathered, 16 * i + 16)
                if q >= 2:
                    pe.wait_ge(m_xlo, 4 * i + q - 1)
                transposes(lambda a: xg[:, (4 * q + a) * P:(4 * q + a + 1) * P], 2 + q % 2, 4, m_xtr)

            def h_columns(i):
                pe.wait_ge(m_hid, i + 1)
                transposes(lambda a: hid[:, a * P:(a + 1) * P], 1, KF, m_htr)

            def up(turn_, c):
                for j in range(2):
                    s = (2 * c + j) % SPLIT
                    pe.wait_ge(lo_ready, split_of(turn_, c, j))
                    for a in range(2):
                        k = 4 * (c % 4) + 2 * j + a
                        cols = slice(a * BANK, (a + 1) * BANK)
                        last = three(ps[:, c // 4, :], xT_hi[:, k, :], xT_lo[:, k, :],
                                     w_hi[:, s, cols], w_lo[:, s, cols], k == 0, k == KD - 1)
                    last.then_inc(unit_done, 1)

            def down(turn_, c, f):
                for j in range(2):
                    s = (2 * c + j) % SPLIT
                    pe.wait_ge(lo_ready, split_of(turn_, c, j))
                    for a in range(2):
                        cols = slice(a * BANK, (a + 1) * BANK)
                        last = three(ps[:, 4 + 2 * j + a, :], hT_hi[:, f, :], hT_lo[:, f, :],
                                     w_hi[:, s, cols], w_lo[:, s, cols], f == 0, f == KF - 1)
                    last.then_inc(unit_done, 1)

            for q in range(4):
                x_columns(0, q)
            pe.wait_ge(m_xlo, 4)
            for c in range(NW):
                up(EXP_TURN, c)
            for q in range(4):
                x_columns(1, q)

            def expert(i, more):
                turn_ = LOOP_TURN + 3 * i
                pe.wait_ge(m_xlo, 4 * i + 8)
                pe.wait_ge(m_silu, i + 1)
                up(turn_, 0)
                h_columns(i)
                for c in range(1, 4):
                    up(turn_, c)
                pe.wait_ge(m_hlo, i + 1)
                for c in range(4, NW):
                    up(turn_, c)
                    if more and c >= 6:
                        x_columns(i + 2, c - 6)
                pe.wait_ge(m_y, 4 * i + FREE_BANK)
                for f in range(KF):
                    down(turn_, NW + f, f)
                    if more and f < 2:
                        x_columns(i + 2, f + 2)

            with pe.Fori(0, E - 2) as i:
                expert(i, True)
            expert(E - 2, False)
            h_columns(E - 1)
            pe.wait_ge(m_hlo, E)
            pe.wait_ge(m_y, 4 * (E - 1) + FREE_BANK)
            for f in range(KF):
                down(LAST_TURN, f, f)
            pe.wait_ge(count_ready, 1)
            n = pe.value_load(n_extra[0:1, 0:1], min_val=0, max_val=EXTRA)
            with pe.Fori(0, EXTRA) as i:
                with pe.If(i < n):
                    turn_ = EXTRA_TURN + 3 * i
                    for q in range(4):
                        x_columns(i + E, q)
                    pe.wait_ge(m_xlo, 4 * i + (4 * E + 4))
                    pe.wait_ge(m_silu, i + E)
                    for c in range(4):
                        up(turn_, c)
                    pe.wait_ge(m_hlo, i + E)
                    for c in range(4, NW):
                        up(turn_, c)
                    h_columns(i + E)
                    pe.wait_ge(m_hlo, i + E + 1)
                    pe.wait_ge(m_y, 4 * i + (4 * E + FREE_BANK))
                    for f in range(KF):
                        down(turn_, NW + f, f)


INPUTS = ["x", "norm_mix", "w_in", "pool_w", "pool_scale", "sgu_ln_g", "sgu_ln_b", "sgu_w", "sgu_b",
          "conv_dw_w", "conv_dw_b", "conv_ln_g", "conv_ln_b", "conv_pw", "w_out", "norm_ffn",
          "router_g_w", "router_g_b", "router_e_w", "router_e_b", "exp_w1", "exp_w3", "exp_w2",
          "norm_final"]


def kernel(**inputs):
    import numpy as np
    from concourse import bacc
    from concourse.bass_utils import run_bass_kernel_spmd

    nc = bacc.Bacc("TRN2", target_bir_lowering=False, num_devices=1, dynamic_dma_scratch_size=8192)
    arrays, args = {}, []
    for name in INPUTS:
        a = np.ascontiguousarray(inputs[name])
        arrays[f"in_{name}"] = a
        args.append(nc.dram_tensor(f"in_{name}", a.shape, mybir.dt.from_np(a.dtype), kind="ExternalInput").ap())
    result = nc.dram_tensor("result", (1, S, D), F32, kind="ExternalOutput").ap()
    build(nc, *args, result)
    ran = run_bass_kernel_spmd(nc, [arrays], core_ids=[0])
    return ran.results[0]["result"]
```

```python
from contextlib import ExitStack

import concourse.bass as bass
from concourse import mybir

F32 = mybir.dt.float32
F32R = mybir.dt.float32r
I32 = mybir.dt.int32
U32 = mybir.dt.uint32
ALU = mybir.AluOpType
ACT = mybir.ActivationFunctionType
AX = mybir.AxisListType

P = 128
BANK = 512
S, D = 1024, 2048
KD = D // P
DA, DB, DC = 512, 768, 768
KB = DB // P
POOLS = 4
TAPS = 31
LEAD = TAPS - 1
HALF = 512
HALVES = S // HALF
TT = HALF // P
NT = S // P
PLEAD = 16
G, EG = 4, 8
E = G * EG
FE = D // 4
KF = FE // P
EPS = 1e-6

CHUNK = 2048
UNIT = CHUNK // 2
RAW = 4
SPLIT = 4
NIN = (DA + 2 * DB + 2 * DC) // P
NOUT = KD * D // CHUNK
CH = NIN + NOUT
UH = 2 * CH
CM = HALVES * CH
NW = 8
NE = NW + 4
CX = CM + E * NE
PIECE = ((0, 64), (64, 32), (96, 32))
PIECES = len(PIECE)
PIECE_ROWS = max(n for _, n in PIECE)
FB = 4
EXTRA = 15
PADS = 4096
LISTED = 1024

FREE_UNITS = SPLIT
FREE_RAW = 2 * RAW
FREE_BANK = 1
FREE_BLOCKS = 8
FREE_TILES = 8
FREE_ROWS = 1
STEPS = 69


def build(nc, x, norm_mix, w_in, pool_w, pool_scale, sgu_ln_g, sgu_ln_b, sgu_w, sgu_b, conv_dw_w,
          conv_dw_b, conv_ln_g, conv_ln_b, conv_pw, w_out, norm_ffn, router_g_w, router_g_b,
          router_e_w, router_e_b, exp_w1, exp_w3, exp_w2, norm_final, out):
    x = x[0]
    out = out[0]
    w_in = w_in[0]
    x1_d = nc.dram_tensor("x1_d", (S, D), F32, kind="Internal").ap()
    h2_d = nc.dram_tensor("h2_d", (S, D), F32, kind="Internal").ap()
    yd = nc.dram_tensor("yd", (2 * S, D), F32, kind="Internal").ap()
    list_d = nc.dram_tensor("list_d", (E * LISTED, 1), I32, kind="Internal").ap()
    spare_d = nc.dram_tensor("spare_d", (8, 1), F32, kind="Internal").ap()
    extra_d = nc.dram_tensor("extra_d", (2, 16), I32, kind="Internal").ap()

    ctx = ExitStack()
    with ctx:
        part = [ctx]

        def sb(name, shape, dt=F32):
            return part[0].enter_context(nc.sbuf_tensor(name, shape, dt))

        def sem(name):
            return ctx.enter_context(nc.semaphore(name))

        ps = ctx.enter_context(nc.psum_tensor("ps", [P, 8, BANK], F32))

        raw = sb("raw", [P, RAW, CHUNK])
        w_hi = sb("w_hi", [P, SPLIT, UNIT], F32R)
        w_lo = sb("w_lo", [P, SPLIT, UNIT], F32R)
        ident = sb("ident", [P, P])
        wts = sb("wts", [P, S // P, 2])
        carry = sb("carry", [P, E])
        n_extra = sb("n_extra", [P, 1], I32)
        eps_t = sb("eps_t", [P, 1])
        asg_i = sb("asg_i", [P, NT, 2], I32)
        dest_i = sb("dest_i", [P, NT, 2], I32)
        slot_i = sb("slot_i", [PIECE_ROWS, PIECES, E], I32)
        tok_i = sb("tok_i", [PIECE_ROWS, PIECES, E], I32)
        count_i = sb("count_i", [P, E], I32)

        p1 = ExitStack()
        part[0] = p1
        p0 = ExitStack()
        part[0] = p0
        rows01 = sb("rows01", [P, 3, D])[:, 1:3, :]
        gain_in = sb("gain_in", [P, D])
        x_in = sb("x_in", [P, TT, D])
        p0.close()
        part[0] = p1
        act_hi = sb("act_hi", [P, TT, KD, P], F32R)
        act_lo = sb("act_lo", [P, TT, KD, P], F32R)
        mid = sb("mid", [P, KD, HALF])
        p0 = ExitStack()
        part[0] = p0
        zc_hi = sb("zc_hi", [P, KB, HALF], F32R)
        sb("behind_z", [P, KB * 32])
        zc_lo = sb("zc_lo", [P, KB, HALF], F32R)
        p0.close()
        part[0] = p1
        zv = sb("zv", [P, KB * (HALF + 32)])
        zc = sb("zc", [P, KB, HALF])
        pw = sb("pw", [P, 2, KB, P])
        pool_wt = sb("pool_wt", [P, POOLS, P])
        chan = sb("chan", [P, KB, TAPS + 3])
        pscale = sb("pscale", [P, POOLS])
        p0 = ExitStack()
        part[0] = p0
        hot_asg_t = sb("hot_asg_t", [P, NT, 2, E], F32R)
        p0.close()
        part[0] = p1
        ln_g = sb("ln_g", [P, KB, P])
        ln_b = sb("ln_b", [P, KB, P])
        wmT = sb("wmT", [P, KB, P])
        gate_b = sb("gate_b", [P, KB, P])
        rw = sb("rw", [P, KD, G + E])
        rb = sb("rb", [P, G + E])
        mean1 = sb("mean1", [P, P])
        tri = sb("tri", [P, P])
        ones = sb("ones", [P, P])
        inv = sb("inv", [P, POOLS, PLEAD])
        halo_z = sb("halo_z", [P, KB, LEAD])
        halo_x = sb("halo_x", [P, POOLS, PLEAD - 1])
        gcol = sb("gcol", [P, KD])
        lg_all = sb("lg_all", [P, NT, G + E])
        acc = sb("acc", [P, TT, G + E])
        ss = sb("ss", [P, TT])
        ss2 = sb("ss2", [P, TT, D // BANK])
        ms = sb("ms", [P, 8])
        std = sb("std", [P, 8])
        rstd = sb("rstd", [P, 8])
        vstat = sb("vstat", [P, TT, 6 * 2])
        vmean = sb("vmean", [P, TT, 2])
        vstd = sb("vstd", [P, TT])
        vrstd = sb("vrstd", [P, TT])
        iota_p = sb("iota_p", [P, P])
        asg_m = sb("asg_m", [P, NT, 2])

        xt = [mid[:, 4 * t:4 * t + 4, :].rearrange("p a b -> p (a b)") for t in range(TT)]
        sq_rows = zv[:, 0:D]
        h2_rows = [rows01[:, 0, :], rows01[:, 1, :], xt[2], xt[3]]
        xa, uT, vT = mid[:, 0:4, :], mid[:, 4:10, :], mid[:, 10:16, :]
        sig = [mid[:, j, :] for j in range(2)]
        ext, sums = (mid[:, 12:16, :].rearrange("p a b -> p (a b)")[:, k * 528:(k + 1) * 528]
                     for k in range(2))
        sums2 = mid[:, 12:16, :].rearrange("p a b -> p (a b)")[:, 2 * 528:3 * 528]
        z = zv[:, :].rearrange("p (j t) -> p j t", j=KB)
        zt = z[:, :, 0:HALF]
        gain = zc[:, 0:4, :].rearrange("p a b -> p (a b)")
        tgrp = [zv[:, t * BANK:(t + 1) * BANK] for t in range(TT)]
        sq_block = zv[:, TT * BANK:(TT + 1) * BANK]
        at = [0]

        def small(*shape):
            n = 1
            for v in shape:
                n *= v
            v = zv[:, at[0]:at[0] + n]
            at[0] += n
            assert at[0] <= KB * (HALF + 32)
            if len(shape) == 2:
                v = v.rearrange("p (a b) -> p a b", b=shape[1])
            if len(shape) == 3:
                v = v.rearrange("p (a b c) -> p a b c", b=shape[1], c=shape[2])
            return v

        lg = small(NT, 8)
        le = small(NT, E)
        top_g, top_e = small(NT, 8), small(NT, 8)
        idx_g, idx_e = small(NT, 8), small(NT, 8)
        gf, onehot_g = small(NT), small(NT, G)
        le8, prod8 = small(NT, 8), small(NT, 8)
        sh_g, sh_e = small(NT, G), small(NT, 8)
        ex_g, ex_e = small(NT, G), small(NT, 8)
        sum_g, sum_e, sum_p = small(NT), small(NT), small(NT)
        wk = small(NT, 2)
        ef, ge = small(NT, 2), small(NT)
        hot = small(NT, 2, E)
        both = small(NT, E)
        earlier = small(NT + 1, E)
        rank = small(NT, 2)
        dest_f = small(NT, 2)
        slot_f = small(PIECES, E)[0:PIECE_ROWS]
        hot_rank = zc[:, 0, :].rearrange("p (t k e) -> p t k e", t=NT, k=2)
        hot_asg = hot_asg_t[:, :, :, :]
        at_slot = act_hi[:, TT - 1, :, :].rearrange("p (t k) s -> p t k s", t=NT)

        p1.close()
        p2 = ExitStack()
        part[0] = p2
        xg = sb("xg", [P, D])
        xT_hi = sb("xT_hi", [P, KD, P], F32R)
        xT_lo = sb("xT_lo", [P, KD, P], F32R)
        silu = sb("silu", [P, FE])
        hid = sb("hid", [P, FE])
        hT_hi = sb("hT_hi", [P, KF, P], F32R)
        hT_lo = sb("hT_lo", [P, KF, P], F32R)
        raw_more = sb("raw_more", [P, RAW, CHUNK])
        raw_high = sb("raw_high", [P, RAW, CHUNK])
        yb = sb("yb", [P, D])
        ix_tok = sb("ix_tok", [PIECE_ROWS, PIECES], I32)
        ix_asg = sb("ix_asg", [PIECE_ROWS, PIECES], I32)
        ix_more = sb("ix_more", [P, 1], I32)
        ix_new = sb("ix_new", [P, 1], I32)
        over = sb("over", [P, 7, E])
        cum = sb("cum", [P, 7, E])
        allone = sb("allone", [P, 7 * E])
        code = sb("code", [P, 2, 7, E])
        iota_1 = sb("iota_1", [P, 1])
        tab_f = sb("tab_f", [P, 2])
        tab_i = sb("tab_i", [P, 2], I32)
        row_i = sb("row_i", [1, 2, 16], I32)
        gfin = sb("gfin", [P, D])
        fst = sb("fst", [P, NT, 4])
        xb = sb("xb", [P, NT - FB, D])
        x1_rows = [xb[:, t, :] for t in range(NT - FB)] + [raw_more[:, t, :] for t in range(FB)]
        p2.close()
        p3 = ExitStack()
        part[0] = p3
        ye_a = sb("ye_a", [P, FB // 2, 2, D])
        sb("between", [P, RAW, CHUNK])
        ye_b = sb("ye_b", [P, FB // 2, 2, D])
        ye = [(ye_a, ye_b)[k // 2][:, k % 2, :, :] for k in range(FB)]
        p3.close()

        def sems(names):
            return (sem(n) for n in names.split())

        raw_landed = [sem(f"raw_landed{i}") for i in range(RAW)]
        m_landed = [sem(f"m_landed{i}") for i in range(NE)]
        hi_ready, lo_ready, unit_done = sems("hi_ready lo_ready unit_done")
        const_now, const_in, const_set, const_tr, const_ev, dve_set = sems(
            "const_now const_in const_set const_tr const_ev dve_set")
        waited = sem("waited")
        xin_landed = [sem(f"xin_landed{t}") for t in range(TT)]
        gin_landed = sem("gin_landed")
        a_ss, a_ms, a_std, a_rstd, a_xn, a_tr, a_hi, a_lo = sems("a_ss a_ms a_std a_rstd a_xn a_tr a_hi a_lo")
        bank_read = [sem("bank_read0"), sem("bank_read1")]
        step = sem("step")
        tap = sem("tap")
        pool_d, pool_mm, pool_y = sems("pool_d pool_mm pool_y")
        v_tr, v_tok, v_var, v_std, v_ln, gate_mm, gated = sems("v_tr v_tok v_var v_std v_ln gate_mm gated")
        c_sum, c_mean, c_cent, c_sq, c_sqsum, c_var, c_std, c_norm, c_act = sems(
            "c_sum c_mean c_cent c_sq c_sqsum c_var c_std c_norm c_act")
        pw_landed = [sem("pw_landed0"), sem("pw_landed1")]
        zc_round, zc_rest, pw_round, pw_rest, pw_mm = sems("zc_round zc_rest pw_round pw_rest pw_mm")
        y_hi, y_lo, xres_landed, x1_part = sems("y_hi y_lo xres_landed x1_part")
        gain_landed, r_ss, r_ms, r_std, r_rstd, r_h2 = sems("gain_landed r_ss r_ms r_std r_rstd r_h2")
        r_tr, r_cols, r_lg, r_acc = sems("r_tr r_cols r_lg r_acc")
        r_shift, r_exp, r_hot, r_rank, r_slot, r_table, r_dest, slots = sems(
            "r_shift r_exp r_hot r_rank r_slot r_table r_dest slots")
        x1_free = sem("x1_free")
        h2_free = sem("h2_free")
        x1_stored = sem("x1_stored")
        h2_stored = [sem("h2_stored0"), sem("h2_stored1")]
        list_blank, listed = sems("list_blank listed")
        count_ready, tab_ready, tab_out, tab_in = sems("count_ready tab_ready tab_out tab_in")
        m_zero, m_ix, m_gathered = sems("m_zero m_ix m_gathered")
        m_rows = sem("m_rows")
        m_xtr, m_xhi, m_xlo = sems("m_xtr m_xhi m_xlo")
        m_silu, m_hid, m_htr, m_hhi, m_hlo = sems("m_silu m_hid m_htr m_hhi m_hlo")
        m_y, m_ystored, m_yfree = sems("m_y m_ystored m_yfree")
        e_list, e_tok, e_gathered, e_ystored = sems("e_list e_tok e_gathered e_ystored")
        f_x = [sem(f"f_x{t}") for t in range(NT)]
        f_y = [sem(f"f_y{t}") for t in range(NT)]
        f_gain, f_sum, f_sq, f_ms, f_std, f_rstd, f_out = sems("f_gain f_sum f_sq f_ms f_std f_rstd f_out")
        f_stored = [sem(f"f_stored{k}") for k in range(FB)]

        block = ctx.enter_context(nc.Block())

        def unit_free(turn, c, j):
            return 8 * turn + 2 * c + j + 1

        def multiplied(turn, c):
            return 8 * turn + 2 * c + FREE_UNITS

        def split_of(turn, c, j):
            return 8 * turn + 2 * c + j + 1 + FREE_RAW

        def half_turn(h):
            return h * (CH // RAW)

        def apart(engine):
            engine.sem_inc(waited, 1)

        class Place:
            def __init__(self, turn, first, rounds):
                self.turn, self.first, self.rounds = turn, first, rounds

            def slot(self, c):
                s = (self.first + c) % NE
                return (raw, raw_more, raw_high)[s // RAW][:, s % RAW, :]

            def landed(self, c):
                return m_landed[(self.first + c) % NE]

            def times(self, c):
                return 16 * (self.rounds + (self.first + c) // NE + 1)

        def first_place():
            return Place(EXP_TURN, 0, 0)

        def item_place(i):
            return Place(LOOP_TURN + 3 * i, NW, i)

        def last_place():
            return Place(LAST_TURN, NW, E - 1)

        def extra_place(i):
            return Place(EXTRA_TURN + 3 * i, 0, i + E)

        INB = [4, 0, 4, 0]
        GATEB = [0, 1, 2, 3, 0, 1]
        NOW, LATER = 7, 8

        def split_place(k):
            return k if k < POOLS else k + KB if k < POOLS + KB else k - KB

        PWB = [6, 7, 2, 3, 4, 5]
        OUT_TURN = NIN // RAW
        EXP_TURN = CM // RAW
        LOOP_TURN = EXP_TURN + NW // RAW
        LAST_TURN = CX // RAW - 1
        EXTRA_TURN = CX // RAW

        @block.sync
        def _(sp):
            def load(turn, c, source):
                sp.wait_ge(lo_ready, 8 * turn + 2 * c + 2)
                n = source.shape[-1]
                sp.dma_start(raw[:, c % RAW, :].rearrange("p (a b) -> p a b", b=n), source)\
                  .then_inc(raw_landed[c % RAW], 16)

            def w_in_tile(col):
                return w_in[:, bass.ds(col, P)].rearrange("(k p) n -> p k n", p=P)

            def load_expert(place, c, source):
                n = source.shape[-1]
                sp.dma_start(place.slot(c).rearrange("p (a b) -> p a b", b=n), source)\
                  .then_inc(place.landed(c), 16)

            def load_up(place, e, fresh=False):
                for c in range(NW):
                    w = (exp_w1 if c < 4 else exp_w3)[0]
                    v = w[bass.ds(e, 1), (c % 4) * 4 * P:(c % 4 + 1) * 4 * P, :]
                    if not fresh:
                        sp.wait_ge(lo_ready, 8 * place.turn + 2 * (c - NE) + 2 + FREE_RAW)
                    elif c < RAW:
                        sp.wait_ge(lo_ready, 8 * place.turn + 2 * c + 2)
                    elif c == RAW:
                        sp.wait_ge(unit_done, multiplied(EXP_TURN, 0))
                        sp.wait_ge(x1_free, HALVES + FREE_ROWS)
                    load_expert(place, c, v.rearrange("e (k p) n -> p (e k) n", p=P))

            def load_down(place, first, e):
                for f in range(KF):
                    c = first + f
                    sp.wait_ge(lo_ready, 8 * place.turn + 2 * (c - NE) + 2 + FREE_RAW)
                    load_expert(place, c, exp_w2[0][bass.ds(e, 1), f * P:(f + 1) * P, :].rearrange("e p n -> p e n"))

            rows = [(zv[0:TAPS, 0:DC], conv_dw_w[0])]
            rows += [(zv[TAPS + r:TAPS + r + 1, 0:DC], v) for r, v in enumerate((conv_dw_b, conv_ln_g, conv_ln_b))]
            rows += [(zv[0:POOLS, DC:DC + P], pool_scale[0].rearrange("(g c) -> g c", c=P)),
                     (zv[0:KD, DC + P:DC + 2 * P], norm_ffn[0].rearrange("(k c) -> k c", c=P)),
                     (zv[:, 1024:1024 + DB].rearrange("p (j s) -> p j s", j=KB), sgu_w[0].rearrange("j t s -> t j s"))]
            assert len(rows) == NOW
            for to, source in rows:
                sp.dma_start(to, source).then_inc(const_now, 16)

            with sp.Fori(0, HALVES) as h:
                sp.wait_ge(unit_done, multiplied(half_turn(h), 0))
                apart(sp)
                for t in range(TT):
                    sp.dma_start(x_in[:, t, :], x[bass.ds(h * HALF + t * P, P), :]).then_inc(xin_landed[t], 16)
                    if t == 0:
                        sp.dma_start(gain_in[:, :], norm_mix.to_broadcast([P, D])).then_inc(gin_landed, 16)
                        sp.wait_ge(x1_free, h + FREE_ROWS)
                        apart(sp)
                with sp.Fori(0, KB // 2) as i:
                    for m in range(4):
                        col = DA + 2 * DB + (DC if m % 2 == 0 else 0) + (m // 2) * P
                        load(half_turn(h) + i, m, w_in_tile(i * (2 * P) + col))
                for c in range(12, NIN):
                    col = (c - 12) * P if c < 16 else DA + (DB if c < 22 else 0) + (c - 16) % KB * P
                    load(half_turn(h), c, w_in[:, col:col + P].rearrange("(k p) n -> p k n", p=P))
                with sp.Fori(0, D // BANK) as n:
                    for g in range(4):
                        v = w_out[0][g * 4 * P:(g + 1) * 4 * P, bass.ds(n * BANK, BANK)]
                        load(half_turn(h) + OUT_TURN + n, g, v.rearrange("(k p) n -> p k n", p=P))
            load_up(first_place(), 0, fresh=True)
            sp.wait_ge(h2_free, 2 * HALVES + 2 * FREE_ROWS)
            with sp.Fori(0, E - 1) as i:
                load_up(item_place(i), i + 1)
                load_down(item_place(i), NW, i)
            load_down(last_place(), 0, E - 1)
            sp.wait_ge(count_ready, 1)
            n = sp.value_load(n_extra[0:1, 0:1], min_val=0, max_val=EXTRA)
            sp.wait_ge(tab_in, 32)
            with sp.Fori(0, EXTRA) as i:
                with sp.If(i < n):
                    e = sp.value_load(row_i[0:1, 1, bass.ds(i, 1)], min_val=0, max_val=E - 1)
                    load_up(extra_place(i), e)
                    load_down(extra_place(i), NW, e)
                    sp.nop()

            def load_rows(t):
                sp.dma_start(x1_rows[t], x1_d[t * P:(t + 1) * P, :]).then_inc(f_x[t], 16)

            def load_pairs(t):
                sp.dma_start(ye[t % FB], yd[2 * t * P:2 * (t + 1) * P, :].rearrange("(p a) n -> p a n", a=2))\
                    .then_inc(f_y[t], 16)

            for t in range(NT - FB):
                load_rows(t)
            sp.wait_ge(lo_ready, n * (2 * NE) + (2 * (CX - RAW) + FREE_RAW))
            apart(sp)
            for t in range(NT - FB, NT):
                load_rows(t)
            sp.wait_ge(m_yfree, n + (E + 1))
            apart(sp)
            for t in range(FB):
                load_pairs(t)
            for t in range(FB, NT):
                sp.wait_ge(f_stored[t % FB], 16)
                load_pairs(t)

        @block.gpsimd
        def _(pool):
            pool.sem_inc(m_yfree, 1)
            pool.sem_inc(h2_free, 2 * FREE_ROWS)
            pool.sem_inc(x1_free, FREE_ROWS)

            wnat = zv[:, 1024:1024 + DB].rearrange("p (j s) -> p j s", j=KB)
            pool.memset(ident[:, :], 0.0).then_inc(const_set, 1)
            pool.memset(tri[:, :], 1.0).then_inc(const_set, 1)
            blank = xt[TT - 1].bitcast(I32)[:, 0:E * LISTED // P]
            pool.memset(blank, PADS).then_inc(const_set, 1)
            pool.wait_ge(const_set, 3)
            pool.affine_select(out=ident[:, :], in_=ident[:, :], compare_op=ALU.not_equal, fill=1.0, base=0,
                               pattern=[[-1, P]], channel_multiplier=1).then_inc(const_set, 1)
            pool.affine_select(out=tri[:, :], in_=tri[:, :], compare_op=ALU.is_gt, fill=0.0, base=0,
                               pattern=[[1, P]], channel_multiplier=-1).then_inc(const_set, 1)
            for to, pattern, base, mult in (
                    (iota_p[:, :], [[1, P]], 0, 0), (asg_i[:, :, :], [[2 * P, NT], [1, 2]], 0, 2),
                    (asg_m[:, :, :], [[2 * P, NT], [1, 2]], -PADS, 2),
                    (inv[:, :, :], [[0, POOLS], [1, PLEAD]], 1, 0)):
                pool.iota(to, pattern, base=base, channel_multiplier=mult,
                          allow_small_or_imprecise_dtypes=True).then_inc(const_set, 1)
            pool.wait_ge(const_now, 16 * NOW)
            pool.affine_select(out=wnat, in_=wnat, compare_op=ALU.is_ge, fill=0.0, base=0,
                               pattern=[[0, KB], [-1, P]], channel_multiplier=1).then_inc(const_set, 1)
            pool.dma_start(list_d.rearrange("(p n) o -> p (n o)", p=P), blank).then_inc(list_blank, 16)
            for to, source in (
                    (pool_wt[:, :, :], pool_w[0].rearrange("g c d -> c g d")),
                    (ln_g[:, :, :].rearrange("p a b -> p (a b)"), sgu_ln_g.to_broadcast([P, DB])),
                    (ln_b[:, :, :].rearrange("p a b -> p (a b)"), sgu_ln_b.to_broadcast([P, DB])),
                    (gate_b[:, :, :].rearrange("p a b -> p (a b)"),
                     sgu_b.rearrange("o j t -> o (j t)").to_broadcast([P, KB * P])),
                    (rw[:, :, 0:G], router_g_w[0].rearrange("(k p) n -> p k n", p=P)),
                    (rw[:, :, G:], router_e_w[0].rearrange("(k p) n -> p k n", p=P)),
                    (rb[:, 0:G], router_g_b.to_broadcast([P, G])),
                    (rb[:, G:], router_e_b.to_broadcast([P, E]))):
                pool.dma_start(to, source).then_inc(const_in, 16)

            with pool.Fori(0, HALVES) as h:
                def rows(t):
                    return bass.ds(h * HALF + t * P, P)

                for n in range(KB):
                    if n >= 2:
                        pool.wait_ge(pw_rest, h * KB + n - 1)
                        apart(pool)
                    pool.dma_start(pw[:, n % 2, :, :],
                                   conv_pw[0, :, n * P:(n + 1) * P].rearrange("(k p) n -> p k n", p=P))\
                        .then_inc(pw_landed[n % 2], 16)
                pool.wait_ge(pw_mm, h * KB + KB)
                apart(pool)
                pool.dma_start(gain, norm_ffn.to_broadcast([P, D])).then_inc(gain_landed, 16)
                pool.wait_ge(y_lo, h * KD + KD)
                apart(pool)
                by_tile = mid[:, :, :].rearrange("p (t a) b -> p t (a b)", t=TT)
                pool.dma_start(by_tile, x[bass.ds(h * HALF, HALF), :].rearrange("(t p) n -> p t n", p=P))\
                    .then_inc(xres_landed, 16)
                for n in range(D // BANK):
                    pool.wait_ge(x1_part, h * 16 + 4 * n + 4 + FREE_BLOCKS)
                    apart(pool)
                    cols = slice(n * BANK, (n + 1) * BANK)
                    pool.dma_start(x1_d[bass.ds(h * HALF, HALF), cols].rearrange("(t p) n -> p t n", p=P),
                                   by_tile[:, :, cols]).then_inc(x1_stored, 16)
                pool.wait_ge(x1_stored, h * 64 + 64)
                pool.sem_inc(x1_free, 1)
                for t in range(TT):
                    pool.wait_ge(r_h2, h * TT + t + 1)
                    apart(pool)
                    pool.dma_start(h2_d[bass.ds(h * HALF + t * P, P), :], h2_rows[t]).then_inc(h2_stored[t // 2], 16)
                for k in range(2):
                    pool.wait_ge(h2_stored[k], h * 32 + 32)
                    pool.sem_inc(h2_free, 1)

            pool.wait_ge(unit_done, multiplied(EXP_TURN, 0))
            pool.memset(xg[:, :], 0.0).then_inc(m_zero, 1)
            def gather_slots(at_, index, done):
                pool.indirect_dma_start(xg[at_, :], None, h2_d,
                                        bass.IndirectOffsetOnAxis(ap=index.bitcast(U32), axis=0),
                                        bounds_check=S - 1, oob_is_err=False).then_inc(done, 16)

            def scatter_slots(at_, index, done):
                pool.indirect_dma_start(yd, bass.IndirectOffsetOnAxis(ap=index.bitcast(U32), axis=0),
                                        yb[at_, :], None, bounds_check=2 * S - 1, oob_is_err=False)\
                    .then_inc(done, 16)

            def pieces(count, row, move, index, done):
                for b, (start, n) in enumerate(PIECE):
                    at_ = slice(start, start + n)
                    if b == 0:
                        move(at_, index[0:n, 0:1], done)
                    else:
                        with pool.If(count > start):
                            move(at_, index[0:n, b:b + 1], done)
                        with pool.Else():
                            pool.dma_start(spare_d[row + b:row + b + 1, :], ident[0:1, 0:1]).then_inc(done, 16)

            def gather(i, expert):
                count = pool.value_load(count_i[0:1, expert], min_val=0, max_val=S)
                pieces(count, 0, gather_slots, ix_tok, m_gathered)

            def gathered(i):
                pool.wait_ge(m_gathered, (16 * PIECES) * i + 16 * PIECES)
                apart(pool)
                pool.sem_inc(m_rows, 1)

            def scatter(i, expert):
                count = pool.value_load(count_i[0:1, expert], min_val=0, max_val=S)
                pool.wait_ge(m_y, 4 * i + 4 + FREE_BANK)
                apart(pool)
                pieces(count, PIECES, scatter_slots, ix_asg, m_ystored)

            def scattered(i):
                pool.wait_ge(m_ystored, (16 * PIECES) * i + 16 * PIECES)
                apart(pool)
                pool.sem_inc(m_yfree, 1)

            pool.wait_ge(slots, 1)
            for i in range(2):
                if i:
                    pool.wait_ge(slots, 2)
                    pool.memset(allone[:, :], 1.0).then_inc(m_zero, 1)
                    pool.iota(iota_1[:, :], [[0, 1]], base=1, channel_multiplier=1,
                              allow_small_or_imprecise_dtypes=True).then_inc(m_zero, 1)
                    pool.iota(code[:, 0, :, :], [[1, 7], [EG, E]], base=1, channel_multiplier=0,
                              allow_small_or_imprecise_dtypes=True).then_inc(m_zero, 1)
                    pool.iota(code[:, 1, :, :], [[0, 7], [1, E]], base=0, channel_multiplier=0,
                              allow_small_or_imprecise_dtypes=True).then_inc(m_zero, 1)
                    pool.dma_start(gfin[:, :], norm_final.rearrange("(o n) -> o n", o=1).to_broadcast([P, D]))\
                        .then_inc(f_gain, 16)
                    pool.wait_ge(m_xtr, 4)
                pool.tensor_copy(ix_tok[:, :], tok_i[:, :, i]).then_inc(m_ix, 1)
                pool.wait_ge(m_ix, i + 1)
                gather(i, slice(i, i + 1))
                gathered(i)
            pool.wait_ge(r_dest, 1)
            for t in range(NT):
                for k in range(2):
                    index = dest_i[:, t, k:k + 1].bitcast(U32)
                    pool.indirect_dma_start(list_d, bass.IndirectOffsetOnAxis(ap=index, axis=0),
                                            asg_i[:, t, k:k + 1], None,
                                            bounds_check=E * LISTED - 1, oob_is_err=False)\
                        .then_inc(listed, 16)
            pool.wait_ge(tab_ready, 1)
            for r in range(2):
                pool.dma_start(extra_d[r, :].rearrange("(n o) -> n o", o=1), tab_i[0:16, r:r + 1])\
                    .then_inc(tab_out, 16)
            pool.wait_ge(tab_out, 32)
            for r in range(2):
                pool.dma_start(row_i[0:1, r, :], extra_d[r:r + 1, :]).then_inc(tab_in, 16)
            pool.wait_ge(x1_stored, HALVES * (D // BANK) * 16)
            pool.wait_ge(listed, 2 * NT * 16)
            pool.wait_ge(m_xtr, 8)
            pool.tensor_copy(ix_tok[:, :], tok_i[:, :, 2]).then_inc(m_ix, 1)
            pool.wait_ge(m_ix, 3)
            gather(2, slice(2, 3))
            gathered(2)
            with pool.Fori(1, E - 2) as i:
                pool.wait_ge(m_xtr, 4 * i + 8)
                pool.tensor_copy(ix_tok[:, :], tok_i[:, :, bass.ds(i + 2, 1)].rearrange("p b o -> p (b o)"))\
                    .then_inc(m_ix, 1)
                pool.wait_ge(m_ix, 2 * i + 2)
                apart(pool)
                gather(i + 2, bass.ds(i + 2, 1))
                pool.tensor_copy(ix_asg[:, :], slot_i[:, :, bass.ds(i - 1, 1)].rearrange("p b o -> p (b o)"))\
                    .then_inc(m_ix, 1)
                pool.wait_ge(m_ix, 2 * i + 3)
                scatter(i - 1, bass.ds(i - 1, 1))
                gathered(i + 2)
                scattered(i - 1)
            for i in range(E - 3, E):
                pool.tensor_copy(ix_asg[:, :], slot_i[:, :, i]).then_inc(m_ix, 1)
                pool.wait_ge(m_ix, E + i + 1)
                scatter(i, slice(i, i + 1))
                scattered(i)
            pool.wait_ge(count_ready, 1)
            n = pool.value_load(n_extra[0:1, 0:1], min_val=0, max_val=EXTRA)
            pool.wait_ge(tab_in, 32)
            with pool.Fori(0, EXTRA) as i:
                with pool.If(i < n):
                    r = pool.value_load(row_i[0:1, 0, bass.ds(i, 1)], min_val=0, max_val=E * EG - 1)
                    pool.dma_start(ix_more[:, :], list_d[bass.ds(r * P, P), :]).then_inc(e_list, 16)
                    pool.wait_ge(e_list, 16 * i + 16)
                    pool.wait_ge(e_tok, i + 1)
                    apart(pool)
                    gather_slots(slice(0, P), ix_new[:, :], e_gathered)
                    pool.wait_ge(e_gathered, 16 * i + 16)
                    apart(pool)
                    pool.sem_inc(m_rows, 1)
                    pool.wait_ge(m_y, 4 * i + (4 * E + 4 + FREE_BANK))
                    apart(pool)
                    scatter_slots(slice(0, P), ix_more[:, :], e_ystored)
                    pool.wait_ge(e_ystored, 16 * i + 16)
                    apart(pool)
                    pool.sem_inc(m_yfree, 1)

        @block.scalar
        def _(act):
            act.sem_inc(m_y, FREE_BANK)
            act.sem_inc(bank_read[0], FREE_BANK)
            act_fn = nc.scalar.activation

            def hi(turn, c):
                act.wait_ge(raw_landed[c % RAW], 16 * (turn + c // RAW + 1))
                for j in range(2):
                    act.wait_ge(unit_done, unit_free(turn, c, j))
                    act_fn(w_hi[:, (2 * c + j) % SPLIT, :], raw[:, c % RAW, j * UNIT:(j + 1) * UNIT],
                           ACT.Copy).then_inc(hi_ready, 1)

            act.wait_ge(const_tr, 2 * KB + 2)
            NC = TAPS + 3
            act_fn(chan[:, :, :].rearrange("p a b -> p (a b)"), ps[:, 0, 0:KB * NC], ACT.Copy).then_inc(const_ev, 1)
            act_fn(pscale[:, :], ps[:, 0, KB * NC:KB * NC + POOLS], ACT.Copy).then_inc(const_ev, 1)
            act_fn(gcol[:, :], ps[:, 0, KB * NC + POOLS:KB * NC + POOLS + KD], ACT.Copy).then_inc(const_ev, 1)
            act_fn(wmT[:, 0:4, :], ps[:, 1, :].rearrange("p (a b) -> p a b", a=4), ACT.Copy).then_inc(const_ev, 1)
            act_fn(wmT[:, 4:6, :], ps[:, 2, 0:2 * P].rearrange("p (a b) -> p a b", a=2), ACT.Copy)\
                .then_inc(const_ev, 1)
            act.wait_ge(dve_set, 1)

            with act.Fori(0, HALVES) as h:
                turn = half_turn(h)
                before = h * TT

                def round_input(t):
                    if t == 1:
                        act.wait_ge(h2_free, 2 * h + 1)
                    for q in range(4):
                        act.wait_ge(a_tr, h * 16 + 4 * t + q + 1)
                        act_fn(act_hi[:, t, 4 * q:4 * q + 4, :].rearrange("p k n -> p (k n)"),
                               ps[:, INB[t] + q, :], ACT.Copy).then_inc(a_hi, 1)

                act.wait_ge(unit_done, multiplied(turn, 0))
                act.wait_ge(r_acc, h * 4 + FREE_BANK)
                for t in range(TT):
                    act.wait_ge(xin_landed[t], h * 16 + 16)
                    if t:
                        act.wait_ge(a_ss, before + t)
                    act_fn(sq_rows, x_in[:, t, :], ACT.Square, accum_out=ss[:, t:t + 1]).then_inc(a_ss, 1)
                    act.wait_ge(a_ms, before + t + 1)
                    act_fn(std[:, t:t + 1], ms[:, t:t + 1], ACT.Sqrt).then_inc(a_std, 1)
                    if t:
                        round_input(t - 1)
                round_input(TT - 1)

                def read(c):
                    bank = ps[:, c % 2, :]
                    act.wait_ge(unit_done, multiplied(turn, c + 1))
                    if c < 12:
                        j = c // 2
                        if j >= 2:
                            act.wait_ge(bank_read[1], h * 14 + j)
                        if j == 0:
                            act.wait_ge(h2_free, 2 * h + 2 * FREE_ROWS)
                            act.wait_ge(list_blank, 16)
                        act_fn(sig[j % 2], bank, ACT.Sigmoid).then_inc(bank_read[0], 1)
                    elif c < 16:
                        if c > 12:
                            act.wait_ge(pool_d, h * POOLS + c - 12)
                        act_fn(ext[:, PLEAD:], bank, ACT.Copy).then_inc(bank_read[c % 2], 1)
                    elif c < 22:
                        if c == 16:
                            act.wait_ge(pool_d, h * POOLS + POOLS)
                        act_fn(vT[:, c - 16, :], bank, ACT.Gelu_apprx_tanh).then_inc(bank_read[c % 2], 1)
                    else:
                        act_fn(uT[:, c - 22, :], bank, ACT.Gelu_apprx_tanh).then_inc(bank_read[c % 2], 1)

                def v_tokens(t):
                    b = 2 + 2 * (t % 2)
                    act.wait_ge(v_tr, before + t + 1)
                    act_fn(vT[:, 0:4, t * P:(t + 1) * P], ps[:, b, :].rearrange("p (k n) -> p k n", k=4),
                           ACT.Copy).then_inc(v_tok, 1)
                    act_fn(vT[:, 4:6, t * P:(t + 1) * P],
                           ps[:, b + 1, 0:2 * P].rearrange("p (k n) -> p k n", k=2), ACT.Copy).then_inc(v_tok, 1)

                for c in range(NIN):
                    hi(turn, c)
                    if c == 24:
                        v_tokens(0)
                        v_tokens(1)
                        for j in range(KB):
                            act.wait_ge(c_cent, h * KB + j + 1)
                            act_fn(zt[:, j, :], zc[:, j, :], ACT.Square).then_inc(c_sq, 1)
                    if c and (c > 12 or c % 2 == 1):
                        read(c - 1)
                    if c == 19:
                        for g in range(POOLS):
                            act.wait_ge(pool_mm, h * POOLS + g + 1)
                            act_fn(xa[:, g, :], ps[:, 2 + g, :], ACT.Copy, scale=pscale[:, g:g + 1])\
                                .then_inc(pool_y, 1)
                    if c == 26:
                        act.wait_ge(c_var, h + 1)
                        act_fn(zt[:, 0, :], ps[:, 7, :], ACT.Sqrt, bias=eps_t[:, 0:1]).then_inc(c_std, 1)
                        act.wait_ge(v_var, h + 1)
                        act_fn(vstd[:, :], vmean[:, :, 1], ACT.Sqrt, bias=eps_t[:, 0:1]).then_inc(v_std, 1)
                    if c == 25:
                        v_tokens(2)
                        v_tokens(3)
                    if c == 27:
                        for j in range(KB):
                            act.wait_ge(c_norm, h * KB + j + 1)
                            act_fn(zc[:, j, :], zc[:, j, :], ACT.Silu, bias=chan[:, j, TAPS + 2:TAPS + 3],
                                   scale=chan[:, j, TAPS + 1:TAPS + 2]).then_inc(c_act, 1)
                for j in range(KB):
                    act.wait_ge(c_act, h * KB + KB)
                    act_fn(zc_hi[:, j, :], zc[:, j, :], ACT.Copy).then_inc(zc_round, 1)
                hi(turn + OUT_TURN, 0)
                act.wait_ge(unit_done, multiplied(turn, NIN))
                for n in range(KB):
                    if n >= TT:
                        act.wait_ge(pw_mm, h * KB + n - TT + 1)
                    act.wait_ge(pw_landed[n % 2], h * 48 + 16 * (n // 2) + 16)
                    act_fn(act_hi[:, n % TT, POOLS:POOLS + KB, :], pw[:, n % 2, :, :], ACT.Copy).then_inc(pw_round, 1)
                    if n == 1:
                        read(NIN - 1)

                def y_round(k, source):
                    act_fn(act_hi[:, :, k, :], source.rearrange("p (t n) -> p t n", t=TT), ACT.Copy)\
                        .then_inc(y_hi, 1)

                act.wait_ge(pool_y, h * POOLS + POOLS)
                for g in range(POOLS):
                    y_round(g, xa[:, g, :])
                hi(turn + OUT_TURN, 1)
                for n in range(KB):
                    act.wait_ge(pw_mm, h * KB + n + 1)
                    y_round(POOLS + KB + n, ps[:, PWB[n], :])
                for j in range(KB):
                    act.wait_ge(gated, h * KB + j + 1)
                    y_round(POOLS + j, uT[:, j, :])

                def of_block(n):
                    for t in range(TT):
                        act.wait_ge(x1_part, h * 16 + 4 * n + t + 1 + FREE_BLOCKS)
                        if n or t:
                            act.wait_ge(r_ss, h * 16 + 4 * n + t)
                        else:
                            act.wait_ge(y_lo, h * KD + KD)
                        act_fn(sq_block, xt[t][:, n * BANK:(n + 1) * BANK], ACT.Square,
                               accum_out=ss2[:, t, n:n + 1]).then_inc(r_ss, 1)
                    if n:
                        act.wait_ge(r_lg, h * 4 + n)
                    for t in range(TT):
                        act.wait_ge(r_tr, h * 16 + 4 * n + t + 1)
                        act_fn(tgrp[t], ps[:, (4 if n % 2 == 0 else 0) + t, :], ACT.Copy).then_inc(r_cols, 1)

                for n in range(4):
                    for c in range(2 if n == 0 else 0, RAW):
                        hi(turn + OUT_TURN + n, c)
                        if n and c == 2:
                            of_block(n - 1)
                of_block(3)
                act.wait_ge(r_ms, h + 1)
                act_fn(std[:, 4:8], ms[:, 4:8], ACT.Sqrt).then_inc(r_std, 1)

            act.wait_ge(r_shift, 1)
            act_fn(ex_g, sh_g, ACT.Exp).then_inc(r_exp, 1)
            act.wait_ge(r_shift, 2)
            act_fn(ex_e, sh_e, ACT.Exp).then_inc(r_exp, 1)

            def round_x(i, q):
                act.wait_ge(m_xtr, 4 * i + q + 1)
                act_fn(xT_hi[:, 4 * q:4 * q + 4, :], ps[:, 2 + q % 2, :].rearrange("p (k n) -> p k n", k=4),
                       ACT.Copy).then_inc(m_xhi, 1)

            def silu_of(i, turn, first=False):
                act.wait_ge(unit_done, multiplied(turn, 4))
                if not first:
                    act.wait_ge(m_hid, i)
                act_fn(silu[:, :], ps[:, 0, :], ACT.Silu).then_inc(m_silu, 1)

            def round_h(i):
                act.wait_ge(m_htr, i + 1)
                act_fn(hT_hi[:, :, :].rearrange("p k n -> p (k n)"), ps[:, 1, :], ACT.Copy).then_inc(m_hhi, 1)

            def read_y(i, turn, c):
                act.wait_ge(unit_done, multiplied(turn, c))
                act.wait_ge(m_yfree, i + 1)
                for b in range(4):
                    act_fn(yb[:, b * BANK:(b + 1) * BANK], ps[:, 4 + b, :], ACT.Copy).then_inc(m_y, 1)

            def chunks(place, first, last):
                for c in range(first, last):
                    act.wait_ge(place.landed(c), place.times(c))
                    for j in range(2):
                        act.wait_ge(unit_done, unit_free(place.turn, c, j))
                        act_fn(w_hi[:, (2 * c + j) % SPLIT, :], place.slot(c)[:, j * UNIT:(j + 1) * UNIT],
                               ACT.Copy).then_inc(hi_ready, 1)

            for q in range(4):
                round_x(0, q)
            chunks(first_place(), 0, 6)
            silu_of(0, EXP_TURN, first=True)
            chunks(first_place(), 6, 10)
            for q in range(4):
                round_x(1, q)

            def expert(i, more):
                turn, place = LOOP_TURN + 3 * i, item_place(i)
                chunks(place, 2, 3)
                round_h(i)
                chunks(place, 3, 6)
                silu_of(i + 1, turn)
                chunks(place, 6, 10)
                if more:
                    act.wait_ge(unit_done, multiplied(turn, NW))
                    round_x(i + 2, 0)
                    round_x(i + 2, 1)
                chunks(place, 10, 11)
                if more:
                    round_x(i + 2, 2)
                chunks(place, 11, 12)
                if more:
                    round_x(i + 2, 3)
                chunks(place, 12, 14)
                read_y(i, turn, NE)

            with act.Fori(0, E - 2) as i:
                expert(i, True)
            expert(E - 2, False)
            round_h(E - 1)
            chunks(last_place(), 2, 4)
            read_y(E - 1, LAST_TURN, 4)
            act.wait_ge(count_ready, 1)
            n = act.value_load(n_extra[0:1, 0:1], min_val=0, max_val=EXTRA)
            with act.Fori(0, EXTRA) as i:
                with act.If(i < n):
                    turn, place = EXTRA_TURN + 3 * i, extra_place(i)
                    for q in range(4):
                        round_x(i + E, q)
                    chunks(place, 0, 6)
                    silu_of(i + E, turn)
                    chunks(place, 6, 9)
                    round_h(i + E)
                    chunks(place, 9, 12)
                    read_y(i + E, turn, NE)

            for t in range(NT):
                k = t % FB
                act.wait_ge(f_sum, 2 * t + 2)
                act_fn(ye[k][:, 0, :], x1_rows[t], ACT.Square, accum_out=fst[:, t, 0:1]).then_inc(f_sq, 1)
                act.wait_ge(f_ms, t + 1)
                act_fn(fst[:, t, 2:3], fst[:, t, 1:2], ACT.Sqrt).then_inc(f_std, 1)
                act.wait_ge(f_out, t + 1)
                act.dma_start(out[t * P:(t + 1) * P, :], ye[k][:, 1, :]).then_inc(f_stored[k], 16)
            for k in range(FB):
                act.wait_ge(f_stored[k], 16 * (NT // FB))

        @block.vector
        def _(dve):
            dve.sem_inc(lo_ready, FREE_RAW)
            dve.sem_inc(a_lo, FREE_TILES)
            dve.sem_inc(r_acc, FREE_BANK)
            dve.sem_inc(bank_read[1], FREE_BANK)
            dve.sem_inc(x1_part, FREE_BLOCKS)
            tt, ts, stt = nc.vector.tensor_tensor, nc.vector.tensor_scalar, nc.vector.scalar_tensor_tensor

            def lo(turn, c):
                for j in range(2):
                    s = (2 * c + j) % SPLIT
                    dve.wait_ge(hi_ready, 8 * turn + 2 * c + j + 1)
                    tt(w_lo[:, s, :], raw[:, c % RAW, j * UNIT:(j + 1) * UNIT], w_hi[:, s, :].bitcast(F32),
                       ALU.subtract).then_inc(lo_ready, 1)

            class Steps:

                def __init__(self, base):
                    self.base, self.n = base, 0

                def __call__(self, ins):
                    self.n += 1
                    ins.then_inc(step, 1)

                def wait(self):
                    dve.wait_ge(step, self.base + self.n)

                def then(self, ins):
                    self(ins)
                    self.wait()

            do = Steps(0)
            for v, to in ((EPS, eps_t[:, :]), (1.0 / DC, mean1[:, :]), (1.0, ones[:, :]), (0.0, halo_z[:, :, :]),
                          (0.0, halo_x[:, :, :])):
                do(nc.vector.memset(to, v))
            dve.wait_ge(const_set, 9)
            for g in range(POOLS):
                do(ts(inv[:, g, :], inv[:, g, :], float(2 << g), None, ALU.min))
            do.wait()
            nc.vector.reciprocal(inv[:, :, :], inv[:, :, :]).then_inc(dve_set, 1)
            dve.wait_ge(dve_set, 1)
            SET = do.n

            with dve.Fori(0, HALVES) as h:
                turn = half_turn(h)
                before = h * TT
                do = Steps(h * STEPS + SET)

                def rest_of_input(t):
                    dve.wait_ge(a_tr, h * 16 + 4 * t + 4)
                    for q in range(4):
                        dve.wait_ge(a_hi, h * 16 + 4 * t + q + 1)
                        k4 = slice(4 * q, 4 * q + 4)
                        tt(act_lo[:, t, k4, :].rearrange("p k n -> p (k n)"), ps[:, INB[t] + q, :],
                           act_hi[:, t, k4, :].rearrange("p k n -> p (k n)").bitcast(F32),
                           ALU.subtract).then_inc(a_lo, 1)

                for t in range(TT):
                    dve.wait_ge(a_ss, before + t + 1)
                    ts(ms[:, t:t + 1], ss[:, t:t + 1], 1.0 / D, EPS, ALU.mult, ALU.add).then_inc(a_ms, 1)
                    dve.wait_ge(a_std, before + t + 1)
                    nc.vector.reciprocal(rstd[:, t:t + 1], std[:, t:t + 1]).then_inc(a_rstd, 1)
                    dve.wait_ge(a_rstd, before + t + 1)
                    if t == 0:
                        dve.wait_ge(gin_landed, h * 16 + 16)
                    stt(x_in[:, t, :], x_in[:, t, :], rstd[:, t:t + 1], gain_in[:, :], ALU.mult, ALU.mult)\
                        .then_inc(a_xn, 1)
                    if t:
                        rest_of_input(t - 1)
                rest_of_input(TT - 1)

                do.then(nc.vector.tensor_copy(z[:, :, 2:32], halo_z[:, :, :]))

                def gated_value(j):
                    dve.wait_ge(bank_read[0], h * 14 + j + 1 + FREE_BANK)
                    dve.wait_ge(unit_done, multiplied(turn, 2 * j + 2))
                    tt(z[:, j, 32:], ps[:, 1, :], sig[j % 2], ALU.mult).then_inc(bank_read[1], 1)

                def taps(first, last):
                    for m in range(first, last):
                        i, j = divmod(m % (2 * TAPS), 2)
                        j += 2 * (m // (2 * TAPS))
                        source = z[:, j, 2 + i:2 + i + HALF]
                        w = chan[:, j, i:i + 1]
                        if i == 0:
                            dve.wait_ge(bank_read[1], h * 14 + j + 1 + FREE_BANK)
                            ts(zc[:, j, :], source, w, chan[:, j, TAPS:TAPS + 1], ALU.mult, ALU.add)\
                                .then_inc(tap, 1)
                        else:
                            dve.wait_ge(tap, h * (KB * TAPS) + m - 1)
                            stt(zc[:, j, :], source, w, zc[:, j, :], ALU.mult, ALU.add).then_inc(tap, 1)

                def pooled(g):
                    c = 12 + g
                    do(nc.vector.tensor_copy(ext[:, 1:PLEAD], halo_x[:, g, :]))
                    dve.wait_ge(bank_read[c % 2], h * 14 + c // 2 + 1 + FREE_BANK)
                    do.wait()
                    a = ext
                    for n in range(g + 1):
                        b = (sums, sums2)[n % 2]
                        at0, s = 2 << n, 1 << n
                        do.then(tt(b[:, at0:], a[:, at0:], a[:, at0 - s:-s], ALU.add))
                        a = b
                    do.then(tt(a[:, PLEAD:2 * PLEAD], a[:, PLEAD:2 * PLEAD], inv[:, g, :], ALU.mult))
                    do(nc.vector.memset(inv[:, g, :], 1.0 / (2 << g)))
                    do(nc.vector.tensor_copy(halo_x[:, g, :], ext[:, -PLEAD + 1:]))
                    do(tt(xa[:, g, 0:PLEAD], a[:, PLEAD:2 * PLEAD], ext[:, PLEAD:2 * PLEAD], ALU.subtract))
                    stt(xa[:, g, PLEAD:], a[:, 2 * PLEAD:], 1.0 / (2 << g), ext[:, 2 * PLEAD:],
                        ALU.mult, ALU.subtract).then_inc(pool_d, 1)

                def v_stats(t):
                    dve.wait_ge(v_tok, 2 * before + 2 * t + 2)
                    for n in range(2):
                        do(nc.vector.bn_stats(vstat[:, t, 6 * n:6 * n + 6],
                                              vT[:, 3 * n:3 * n + 3, t * P:(t + 1) * P]))
                    do.wait()
                    apart(dve)
                    ins = nc.vector.bn_aggr(vmean[:, t, :], vstat[:, t, :])
                    if t < TT - 1:
                        do(ins)
                    else:
                        ins.then_inc(v_var, 1)

                def v_norm(t):
                    v = vT[:, :, t * P:(t + 1) * P]
                    do.then(ts(v, v, vmean[:, t, 0:1], vrstd[:, t:t + 1], ALU.subtract, ALU.mult))
                    do.then(tt(v, v, ln_g[:, :, :], ALU.mult))
                    tt(v, v, ln_b[:, :, :], ALU.add).then_inc(v_ln, 1)

                def sum_tiles(v, ready):
                    do.then(tt(zt[:, 0, :], v[:, 0, :], v[:, 1, :], ALU.add))
                    for j in range(2, KB):
                        ins = tt(zt[:, 0, :], zt[:, 0, :], v[:, j, :], ALU.add)
                        if j < KB - 1:
                            do.then(ins)
                        else:
                            ins.then_inc(ready, 1)

                done = 0
                for c in range(NIN):
                    lo(turn, c)
                    if 2 <= c <= 12 and c % 2 == 0:
                        gated_value(c // 2 - 1)
                    if c == 13:
                        dve.wait_ge(list_blank, 16)
                        dve.wait_ge(const_in, 16 * LATER)
                        with dve.If(h < 1):
                            dve.wait_ge(const_ev, 5)
                            tt(rw[:, :, :], rw[:, :, :], gcol[:, :].unsqueeze(2).to_broadcast([P, KD, G + E]),
                               ALU.mult).then_inc(dve_set, 1)
                    if 13 <= c <= 16:
                        pooled(c - 13)
                    if c == 23:
                        sum_tiles(zc, c_sum)
                    if c == 24:
                        dve.wait_ge(c_mean, h + 1)
                        for j in range(KB):
                            tt(zc[:, j, :], zc[:, j, :], ps[:, 6, :], ALU.subtract).then_inc(c_cent, 1)
                    if c == 25:
                        v_stats(0)
                        v_stats(1)
                    if c == 25:
                        dve.wait_ge(c_sq, h * KB + KB)
                        sum_tiles(zt, c_sqsum)
                    if c == 26:
                        v_stats(2)
                        v_stats(3)
                    if c == 27:
                        dve.wait_ge(c_std, h + 1)
                        do.then(nc.vector.reciprocal(zt[:, 1, :], zt[:, 0, :]))
                        for j in range(KB):
                            tt(zc[:, j, :], zc[:, j, :], zt[:, 1, :], ALU.mult).then_inc(c_norm, 1)
                    if c == 27:
                        dve.wait_ge(v_std, h + 1)
                        do.then(nc.vector.reciprocal(vrstd[:, :], vstd[:, :]))
                        v_norm(0)
                    if 4 <= c <= 22:
                        last = min(KB * TAPS, done + (6 if 13 <= c <= 16 else 10 if c < 13 else 12))
                        taps(done, last)
                        done = last
                    if c == 22:
                        assert done == KB * TAPS
                        dve.wait_ge(tap, h * (KB * TAPS) + KB * TAPS)
                        do.then(nc.vector.tensor_copy(halo_z[:, :, :], z[:, :, 2 + HALF:]))

                def y_rest(k, source):
                    dve.wait_ge(y_hi, h * KD + split_place(k) + 1)
                    tt(act_lo[:, :, k, :], source.rearrange("p (t n) -> p t n", t=TT),
                       act_hi[:, :, k, :].bitcast(F32), ALU.subtract).then_inc(y_lo, 1)

                def gate(j):
                    dve.wait_ge(gate_mm, h * KB + j + 1)
                    g = ps[:, GATEB[j], :].rearrange("p (n t) -> p n t", n=TT)
                    do.then(tt(g, g, gate_b[:, j:j + 1, :].to_broadcast([P, TT, P]), ALU.add))
                    tt(uT[:, j, :], ps[:, GATEB[j], :], uT[:, j, :], ALU.mult).then_inc(gated, 1)

                for j in range(KB):
                    dve.wait_ge(zc_round, h * KB + j + 1)
                    tt(zc_lo[:, j, :], zc[:, j, :], zc_hi[:, j, :].bitcast(F32), ALU.subtract).then_inc(zc_rest, 1)
                lo(turn + OUT_TURN, 0)
                for n in range(KB):
                    dve.wait_ge(pw_round, h * KB + n + 1)
                    tt(act_lo[:, n % TT, POOLS:POOLS + KB, :], pw[:, n % 2, :, :],
                       act_hi[:, n % TT, POOLS:POOLS + KB, :].bitcast(F32), ALU.subtract).then_inc(pw_rest, 1)
                    if 1 <= n <= 3:
                        v_norm(n)
                for g in range(POOLS):
                    y_rest(g, xa[:, g, :])
                lo(turn + OUT_TURN, 1)
                for n in range(KB):
                    y_rest(POOLS + KB + n, ps[:, PWB[n], :])
                gate(0)
                for j in range(KB):
                    if j < KB - 1:
                        gate(j + 1)
                    y_rest(POOLS + j, uT[:, j, :])

                def add_rows(n, sub):
                    dve.wait_ge(unit_done, multiplied(turn + OUT_TURN + n, RAW))
                    for t in range(TT):
                        to = xt[t][:, bass.ds(n * BANK, BANK)]
                        if n == 0:
                            dve.wait_ge(xres_landed, h * 16 + 16)
                        tt(to, to, ps[:, (4 if sub == 0 else 0) + t, :], ALU.add).then_inc(x1_part, 1)

                def add_logits(n):
                    dve.wait_ge(r_lg, h * 4 + n + 1)
                    part_ = ps[:, 4 if n % 2 == 0 else 0, 0:TT * (G + E)].rearrange("p (t n) -> p t n", t=TT)
                    if n == 0:
                        ins = nc.vector.tensor_copy(acc[:, :, :], part_)
                    else:
                        dve.wait_ge(r_acc, h * 4 + n + FREE_BANK)
                        ins = tt(acc[:, :, :], acc[:, :, :], part_, ALU.add)
                    ins.then_inc(r_acc, 1)

                for n in range(4):
                    lo(turn + OUT_TURN + n, 2)
                    lo(turn + OUT_TURN + n, 3)
                    if n:
                        add_logits(n - 1)
                    if n < 3:
                        lo(turn + OUT_TURN + n + 1, 0)
                    add_rows(n, n % 2)
                    if n < 3:
                        lo(turn + OUT_TURN + n + 1, 1)

                dve.wait_ge(r_ss, h * 16 + 16)
                do.then(nc.vector.tensor_reduce(ms[:, 0:4], ss2[:, :, :], AX.X, ALU.add))
                ts(ms[:, 4:8], ms[:, 0:4], 1.0 / D, EPS, ALU.mult, ALU.add).then_inc(r_ms, 1)
                dve.wait_ge(r_std, h + 1)
                nc.vector.reciprocal(rstd[:, 4:8], std[:, 4:8]).then_inc(r_rstd, 1)
                dve.wait_ge(r_rstd, h + 1)
                dve.wait_ge(gain_landed, h * 16 + 16)

                def second_norm(t):
                    stt(h2_rows[t], xt[t], rstd[:, 4 + t:5 + t], gain, ALU.mult, ALU.mult).then_inc(r_h2, 1)

                second_norm(0)
                second_norm(1)
                add_logits(3)
                dve.wait_ge(r_acc, h * 4 + 4 + FREE_BANK)
                do(tt(lg_all[:, bass.ds(before, TT), :], acc[:, :, :],
                      rstd[:, 4:8].unsqueeze(2).to_broadcast([P, TT, G + E]), ALU.mult))
                dve.wait_ge(x1_free, h + 1 + FREE_ROWS)
                second_norm(2)
                second_norm(3)
                do.wait()
                assert do.n == STEPS, f"STEPS = {do.n}"

            do = Steps(SET + HALVES * STEPS)
            dve.wait_ge(r_h2, NT)

            def over_tiles(v, n):
                return v.unsqueeze(1).to_broadcast([P, NT, n])

            def over_last(v, n):
                return v.unsqueeze(2).to_broadcast([P, NT, n])

            do(nc.vector.memset(slot_f, float(PADS)))
            do(nc.vector.memset(lg[:, :, G:], -3.0e38))
            do(tt(lg[:, :, 0:G], lg_all[:, :, 0:G], over_tiles(rb[:, 0:G], G), ALU.add))
            do.then(tt(le, lg_all[:, :, G:], over_tiles(rb[:, G:], E), ALU.add))
            for t in range(NT):
                do(nc.vector.max(top_g[:, t, :], lg[:, t, :]))
            do.wait()
            tt(sh_g, lg[:, :, 0:G], top_g[:, :, 0:1].to_broadcast([P, NT, G]), ALU.subtract).then_inc(r_shift, 1)
            for t in range(NT):
                do(nc.vector.max_index(idx_g.bitcast(U32)[:, t, :], top_g[:, t, :], lg[:, t, :]))
            do.wait()
            do.then(nc.vector.tensor_copy(gf, idx_g.bitcast(U32)[:, :, 0]))
            do.then(tt(onehot_g, over_tiles(iota_p[:, 0:G], G), over_last(gf, G), ALU.is_equal))
            for g in range(G):
                one = onehot_g[:, :, g:g + 1].to_broadcast([P, NT, EG])
                if g == 0:
                    do.then(tt(le8, le[:, :, 0:EG], one, ALU.mult))
                else:
                    do.then(tt(prod8, le[:, :, g * EG:(g + 1) * EG], one, ALU.mult))
                    do.then(tt(le8, le8, prod8, ALU.add))
            for t in range(NT):
                do(nc.vector.max(top_e[:, t, :], le8[:, t, :]))
            do.wait()
            tt(sh_e, le8, top_e[:, :, 0:1].to_broadcast([P, NT, EG]), ALU.subtract).then_inc(r_shift, 1)
            for t in range(NT):
                do(nc.vector.max_index(idx_e.bitcast(U32)[:, t, :], top_e[:, t, :], le8[:, t, :]))
            do(ts(ge, gf, float(EG), None, ALU.mult))
            do.wait()
            do.then(nc.vector.tensor_copy(wk, idx_e.bitcast(U32)[:, :, 0:2]))
            do.then(tt(ef, wk, ge.unsqueeze(2).to_broadcast([P, NT, 2]), ALU.add))
            for k in range(2):
                do(tt(hot[:, :, k, :], over_tiles(iota_p[:, 0:E], E), over_last(ef[:, :, k], E), ALU.is_equal))
            do.wait()
            do(nc.vector.memset(earlier[:, 0, :], 0.0))
            do.then(tt(both, hot[:, :, 0, :], hot[:, :, 1, :], ALU.add))
            for t in range(NT):
                do.then(tt(earlier[:, t + 1, :], earlier[:, t, :], both[:, t, :], ALU.add))
            nc.vector.sem_inc(r_hot, 1)
            do(tt(hot_asg, hot, asg_m[:, :, :].unsqueeze(3).to_broadcast([P, NT, 2, E]), ALU.mult))
            dve.wait_ge(r_rank, 1)
            counted = ps[:, 7, 0:NT * E].rearrange("p (t o e) -> p t o e", t=NT, o=1)
            do.then(tt(hot_rank, hot, counted.to_broadcast([P, NT, 2, E]), ALU.mult))
            do.then(nc.vector.tensor_reduce(rank, hot_rank, AX.X, ALU.add))
            tt(at_slot, iota_p[:, :].unsqueeze(1).unsqueeze(1).to_broadcast([P, NT, 2, P]),
               rank.unsqueeze(3).to_broadcast([P, NT, 2, P]), ALU.is_equal).then_inc(r_slot, 1)
            do(nc.vector.tensor_copy(carry[:, :], ps[:, 7, NT * E:(NT + 1) * E]))
            do(nc.vector.tensor_copy(count_i[:, :], ps[:, 7, NT * E:(NT + 1) * E]))
            do.then(stt(dest_f, ef, float(LISTED), rank, ALU.mult, ALU.add))
            nc.vector.tensor_copy(dest_i[:, :, :], dest_f).then_inc(r_dest, 1)
            dve.wait_ge(r_table, 1)
            for b, (start, n) in enumerate(PIECE):
                do(ts(slot_f[0:n, b, :], ps[start:start + n, 6, 0:E], float(PADS), None, ALU.add))
            do.wait()
            do.then(nc.vector.tensor_copy(slot_i[:, :, :], slot_f))
            do.then(ts(tok_i[:, :, :], slot_i[:, :, :], 1, None, ALU.logical_shift_right))
            nc.vector.sem_inc(slots, 1)
            dve.wait_ge(r_exp, 2)
            for k in range(2):
                do.then(tt(prod8, over_tiles(iota_p[:, 0:EG], EG), over_last(wk[:, :, k], EG), ALU.is_equal))
                do.then(tt(prod8, prod8, ex_e, ALU.mult))
                do.then(nc.vector.tensor_reduce(wk[:, :, k:k + 1], prod8, AX.X, ALU.add))
            do(nc.vector.tensor_reduce(sum_g, ex_g, AX.X, ALU.add))
            do(nc.vector.tensor_reduce(sum_e, ex_e, AX.X, ALU.add))
            do.wait()
            do(nc.vector.reciprocal(sum_g, sum_g))
            do(nc.vector.reciprocal(sum_e, sum_e))
            do.wait()
            do.then(tt(wk, wk, sum_e.unsqueeze(2).to_broadcast([P, NT, 2]), ALU.mult))
            do.then(tt(sum_p, wk[:, :, 0], wk[:, :, 1], ALU.add))
            do(nc.vector.reciprocal(sum_p, sum_p))
            do.then(tt(wk, wk, sum_g.unsqueeze(2).to_broadcast([P, NT, 2]), ALU.mult))
            do.then(tt(wts[:, :, :], wk, sum_p.unsqueeze(2).to_broadcast([P, NT, 2]), ALU.mult))
            nc.vector.sem_inc(slots, 1)

            def rest_of_x(i, q):
                dve.wait_ge(m_xhi, 4 * i + q + 1)
                tt(xT_lo[:, 4 * q:4 * q + 4, :], ps[:, 2 + q % 2, :].rearrange("p (k n) -> p k n", k=4),
                   xT_hi[:, 4 * q:4 * q + 4, :].bitcast(F32), ALU.subtract).then_inc(m_xlo, 1)

            def hidden(i, turn, first=False):
                dve.wait_ge(m_silu, i + 1)
                dve.wait_ge(unit_done, multiplied(turn, NW))
                if not first:
                    dve.wait_ge(m_htr, i)
                tt(hid[:, :], ps[:, 1, :], silu[:, :], ALU.mult).then_inc(m_hid, 1)

            def rest_of_h(i):
                dve.wait_ge(m_hhi, i + 1)
                tt(hT_lo[:, :, :].rearrange("p k n -> p (k n)"), ps[:, 1, :],
                   hT_hi[:, :, :].rearrange("p k n -> p (k n)").bitcast(F32), ALU.subtract).then_inc(m_hlo, 1)

            def chunks(place, first, last):
                for c in range(first, last):
                    for j in range(2):
                        s = (2 * c + j) % SPLIT
                        dve.wait_ge(hi_ready, 8 * place.turn + 2 * c + j + 1)
                        tt(w_lo[:, s, :], place.slot(c)[:, j * UNIT:(j + 1) * UNIT], w_hi[:, s, :].bitcast(F32),
                           ALU.subtract).then_inc(lo_ready, 1)

            for q in range(4):
                rest_of_x(0, q)

            dve.wait_ge(m_zero, 5)
            for b in range(7):
                do(ts(over[:, b, :], carry[:, :], float(P * (b + 1)), None, ALU.is_gt))
            do.wait()
            flat = over[:, :, :].rearrange("p b e -> p (b e)")
            flat_cum = cum[:, :, :].rearrange("p b e -> p (b e)")
            do.then(nc.vector.tensor_tensor_scan(flat_cum, allone[:, :], flat, 0.0, ALU.mult, ALU.add))
            nc.vector.tensor_copy(n_extra[:, :], cum[:, 6, E - 1:E]).then_inc(count_ready, 1)
            dve.wait_ge(count_ready, 1)
            do.then(tt(flat_cum, flat_cum, flat, ALU.mult))
            for r in range(2):
                do.then(stt(flat, flat_cum, iota_1[:, 0:1], code[:, r, :, :].rearrange("p b e -> p (b e)"),
                            ALU.is_equal, ALU.mult, accum_out=tab_f[:, r:r + 1]))
            nc.vector.tensor_copy(tab_i[:, :], tab_f[:, :]).then_inc(tab_ready, 1)

            chunks(first_place(), 0, 9)
            hidden(0, EXP_TURN, first=True)
            for q in range(4):
                rest_of_x(1, q)
            chunks(first_place(), 9, 10)

            def expert(i, more):
                turn, place = LOOP_TURN + 3 * i, item_place(i)
                chunks(place, 2, 3)
                rest_of_h(i)
                chunks(place, 3, 10)
                hidden(i + 1, turn)
                if more:
                    rest_of_x(i + 2, 0)
                    rest_of_x(i + 2, 1)
                chunks(place, 10, 11)
                if more:
                    rest_of_x(i + 2, 2)
                chunks(place, 11, 12)
                if more:
                    rest_of_x(i + 2, 3)
                chunks(place, 12, 14)

            with dve.Fori(0, E - 2) as i:
                expert(i, True)
            expert(E - 2, False)
            rest_of_h(E - 1)
            chunks(last_place(), 2, 4)
            n = dve.value_load(n_extra[0:1, 0:1], min_val=0, max_val=EXTRA)
            with dve.Fori(0, EXTRA) as i:
                with dve.If(i < n):
                    turn, place = EXTRA_TURN + 3 * i, extra_place(i)
                    dve.wait_ge(e_list, 16 * i + 16)
                    ts(ix_new[:, :], ix_more[:, :], 1, None, ALU.logical_shift_right).then_inc(e_tok, 1)
                    for q in range(4):
                        rest_of_x(i + E, q)
                    chunks(place, 0, 8)
                    hidden(i + E, turn)
                    chunks(place, 8, 9)
                    rest_of_h(i + E)
                    chunks(place, 9, 12)

            dve.wait_ge(f_gain, 16)

            def add_pair(t, a):
                if a:
                    dve.wait_ge(f_sum, 2 * t + 1)
                stt(x1_rows[t], ye[t % FB][:, a, :], wts[:, t, a:a + 1], x1_rows[t], ALU.mult, ALU.add)\
                    .then_inc(f_sum, 1)

            for t in range(NT + 1):
                if t < NT:
                    dve.wait_ge(f_x[t], 16)
                    dve.wait_ge(f_y[t], 16)
                    add_pair(t, 0)
                if t:
                    dve.wait_ge(f_sq, t)
                    ts(fst[:, t - 1, 1:2], fst[:, t - 1, 0:1], 1.0 / D, EPS, ALU.mult, ALU.add).then_inc(f_ms, 1)
                if t < NT:
                    add_pair(t, 1)
                if t:
                    dve.wait_ge(f_std, t)
                    nc.vector.reciprocal(fst[:, t - 1, 3:4], fst[:, t - 1, 2:3]).then_inc(f_rstd, 1)
                    dve.wait_ge(f_rstd, t)
                    stt(ye[(t - 1) % FB][:, 1, :], x1_rows[t - 1], fst[:, t - 1, 3:4], gfin[:, :], ALU.mult, ALU.mult)\
                        .then_inc(f_out, 1)

        @block.tensor
        def _(pe):
            pe.sem_inc(unit_done, FREE_UNITS)
            mm = nc.tensor.matmul

            def transposes(source, bank, count, done, n=P):
                for a in range(count):
                    last = nc.tensor.transpose(ps[:, bank, a * P:(a + 1) * P], source(a), ident[:, :])
                last.then_inc(done, 1)

            def three(out_, s_hi, s_lo, m_hi, m_lo, start, stop):
                mm(out_, s_hi, m_hi, start=start, stop=False)
                mm(out_, s_hi, m_lo, start=False, stop=False)
                return mm(out_, s_lo, m_hi, start=False, stop=stop)

            pe.wait_ge(const_set, 10)
            NC = TAPS + 3
            for j in range(KB):
                nc.tensor.transpose(ps[:, 0, j * NC:(j + 1) * NC], zv[0:NC, j * P:(j + 1) * P], ident[0:NC, 0:NC])\
                    .then_inc(const_tr, 1)
            nc.tensor.transpose(ps[:, 0, KB * NC:KB * NC + POOLS], zv[0:POOLS, DC:DC + P], ident[0:POOLS, 0:POOLS])\
                .then_inc(const_tr, 1)
            at_ = KB * NC + POOLS
            nc.tensor.transpose(ps[:, 0, at_:at_ + KD], zv[0:KD, DC + P:DC + 2 * P], ident[0:KD, 0:KD])\
                .then_inc(const_tr, 1)
            for j in range(KB):
                nc.tensor.transpose(ps[:, 1 + j // 4, (j % 4) * P:(j % 4 + 1) * P],
                                    zv[:, 1024 + j * P:1024 + (j + 1) * P], ident[:, :]).then_inc(const_tr, 1)
            pe.wait_ge(const_ev, 5)
            pe.wait_ge(dve_set, 1)

            with pe.Fori(0, HALVES) as h:
                turn = half_turn(h)
                before = h * TT

                pe.wait_ge(r_acc, h * 4 + FREE_BANK)
                for t in range(TT):
                    pe.wait_ge(a_xn, before + t + 1)
                    pe.wait_ge(a_lo, h * 16 + 4 * t + 4)
                    for q in range(4):
                        transposes(lambda a: x_in[:, t, (4 * q + a) * P:(4 * q + a + 1) * P], INB[t] + q, 4, a_tr)
                pe.wait_ge(a_lo, h * 16 + 16 + FREE_TILES)

                def product(unit, m, reads):
                    pe.wait_ge(bank_read[m], h * 14 + reads + FREE_BANK)
                    for j in range(2):
                        s = 2 * m + j
                        pe.wait_ge(lo_ready, unit + s + 1 + FREE_RAW)
                        for k in range(8):
                            cols = slice(k * P, (k + 1) * P)
                            last = three(ps[:, m, :].rearrange("p (t n) -> p t n", t=TT), w_hi[:, s, cols], w_lo[:, s, cols],
                                         act_hi[:, :, 8 * j + k, :], act_lo[:, :, 8 * j + k, :],
                                         j == 0 and k == 0, j == 1 and k == 7)
                        last.then_inc(unit_done, 1)

                def pairs(first, last):
                    with pe.Fori(first, last) as i:
                        for m in range(2):
                            product(h * UH + 4 * i, m, i)

                def v_transposes(t):
                    b = 2 + 2 * (t % 2)
                    for a in range(KB):
                        last = nc.tensor.transpose(ps[:, b + a // 4, (a % 4) * P:(a % 4 + 1) * P],
                                                   vT[:, a, t * P:(t + 1) * P], ident[:, :])
                    last.then_inc(v_tr, 1)

                apart(pe)
                pairs(0, 9)
                pe.wait_ge(pool_d, h * POOLS + POOLS)
                pe.wait_ge(const_in, 16 * LATER)
                pe.wait_ge(dve_set, 2)
                for g in range(POOLS):
                    mm(ps[:, 2 + g, :], pool_wt[:, g, :], xa[:, g, :], start=True, stop=True).then_inc(pool_mm, 1)
                pairs(9, 11)
                product(h * UH + 44, 0, 11)
                pe.wait_ge(bank_read[1], h * 14 + 11 + FREE_BANK)
                pe.wait_ge(pool_y, h * POOLS + POOLS)
                v_transposes(0)
                v_transposes(1)
                product(h * UH + 44, 1, 11)
                pe.wait_ge(v_tok, 2 * before + 4)
                v_transposes(2)
                v_transposes(3)
                pe.wait_ge(c_sum, h + 1)
                mm(ps[:, 6, :], mean1[:, :], zt[:, 0, :], start=True, stop=True).then_inc(c_mean, 1)
                product(h * UH + 48, 0, 12)
                product(h * UH + 48, 1, 12)
                pe.wait_ge(c_sqsum, h + 1)
                mm(ps[:, 7, :], mean1[:, :], zt[:, 0, :], start=True, stop=True).then_inc(c_var, 1)
                apart(pe)
                pairs(13, 14)
                pe.wait_ge(c_act, h * KB + KB)
                pe.wait_ge(v_tok, 2 * before + 2 * TT)
                for n in range(KB):
                    pe.wait_ge(pw_rest, h * KB + n + 1)
                    for k in range(KB):
                        if n == 0:
                            pe.wait_ge(zc_rest, h * KB + k + 1)
                        w = (n % TT, POOLS + k)
                        last = three(ps[:, PWB[n], :], act_hi[:, w[0], w[1], :], act_lo[:, w[0], w[1], :],
                                     zc_hi[:, k, :], zc_lo[:, k, :], k == 0, k == KB - 1)
                    last.then_inc(pw_mm, 1)

                pe.wait_ge(v_ln, before + TT)

                def gates(j):
                    if j < 2:
                        pe.wait_ge(bank_read[j], h * 14 + 14 + FREE_BANK)
                    if j in (2, 3):
                        pe.wait_ge(y_lo, h * KD + POOLS + j + 1)
                    if j >= 4:
                        pe.wait_ge(gated, h * KB + j - 3)
                    for t in range(TT):
                        cols = slice(t * P, (t + 1) * P)
                        last = mm(ps[:, GATEB[j], cols], vT[:, j, cols], wmT[:, j, :], start=True, stop=True)
                    last.then_inc(gate_mm, 1)

                for j in range(4):
                    gates(j)

                def columns(n):
                    for t in range(TT):
                        pe.wait_ge(x1_part, h * 16 + 4 * n + t + 1 + FREE_BLOCKS)
                        transposes(lambda a: xt[t][:, (4 * n + a) * P:(4 * n + a + 1) * P],
                                   (4 if n % 2 == 0 else 0) + t, 4, r_tr)

                def logits(n):
                    pe.wait_ge(r_cols, h * 16 + 4 * n + 4)
                    for t in range(TT):
                        for a in range(4):
                            last = mm(ps[:, 4 if n % 2 == 0 else 0, t * (G + E):(t + 1) * (G + E)],
                                      tgrp[t][:, a * P:(a + 1) * P], rw[:, 4 * n + a, :],
                                      start=a == 0, stop=a == 3)
                    last.then_inc(r_lg, 1)

                for n in range(D // BANK):
                    if n >= 2:
                        pe.wait_ge(r_acc, h * 4 + n - 1 + FREE_BANK)
                    for g in range(4):
                        for j in range(2):
                            s = (2 * g + j) % SPLIT
                            pe.wait_ge(lo_ready, split_of(turn + OUT_TURN + n, g, j))
                            for a in range(2):
                                k = 4 * g + 2 * j + a
                                cols = slice(a * BANK, (a + 1) * BANK)
                                if n == 0:
                                    pe.wait_ge(y_lo, h * KD + max(split_place(k) + 1, POOLS + KB))
                                for t in range(TT):
                                    last = three(ps[:, (4 if n % 2 == 0 else 0) + t, :],
                                                 act_hi[:, t, k, :], act_lo[:, t, k, :],
                                                 w_hi[:, s, cols], w_lo[:, s, cols], k == 0, k == KD - 1)
                            last.then_inc(unit_done, 1)
                        if n == 0 and g == 0:
                            gates(4)
                            gates(5)
                        if n and g == 0:
                            columns(n - 1)
                        if n and g == 1:
                            logits(n - 1)
                columns(3)
                logits(3)

            pe.wait_ge(r_hot, 1)
            mm(ps[:, 7, 0:(NT + 1) * E], ones[:, :], earlier.rearrange("p t e -> p (t e)"), start=True, stop=False)
            mm(ps[:, 7, 0:NT * E], tri[:, :], both.rearrange("p t e -> p (t e)"), start=False, stop=True)\
                .then_inc(r_rank, 1)
            pe.wait_ge(r_slot, 1)
            for t in range(NT):
                for k in range(2):
                    last = mm(ps[:, 6, 0:E], at_slot[:, t, k, :], hot_asg[:, t, k, :],
                              start=t == 0 and k == 0, stop=t == NT - 1 and k == 1)
            last.then_inc(r_table, 1)


            def x_columns(i, q):
                if q == 0:
                    pe.wait_ge(m_rows, i + 1)
                if q >= 2:
                    pe.wait_ge(m_xlo, 4 * i + q - 1)
                transposes(lambda a: xg[:, (4 * q + a) * P:(4 * q + a + 1) * P], 2 + q % 2, 4, m_xtr)

            def h_columns(i):
                pe.wait_ge(m_hid, i + 1)
                transposes(lambda a: hid[:, a * P:(a + 1) * P], 1, KF, m_htr)

            def up(turn_, c):
                for j in range(2):
                    s = (2 * c + j) % SPLIT
                    pe.wait_ge(lo_ready, split_of(turn_, c, j))
                    for a in range(2):
                        k = 4 * (c % 4) + 2 * j + a
                        cols = slice(a * BANK, (a + 1) * BANK)
                        last = three(ps[:, c // 4, :], xT_hi[:, k, :], xT_lo[:, k, :],
                                     w_hi[:, s, cols], w_lo[:, s, cols], k == 0, k == KD - 1)
                    last.then_inc(unit_done, 1)

            def down(turn_, c, f):
                for j in range(2):
                    s = (2 * c + j) % SPLIT
                    pe.wait_ge(lo_ready, split_of(turn_, c, j))
                    for a in range(2):
                        cols = slice(a * BANK, (a + 1) * BANK)
                        last = three(ps[:, 4 + 2 * j + a, :], hT_hi[:, f, :], hT_lo[:, f, :],
                                     w_hi[:, s, cols], w_lo[:, s, cols], f == 0, f == KF - 1)
                    last.then_inc(unit_done, 1)

            for q in range(4):
                x_columns(0, q)
            pe.wait_ge(m_xlo, 4)
            for c in range(NW):
                up(EXP_TURN, c)
            for q in range(4):
                x_columns(1, q)

            def expert(i, more):
                turn_ = LOOP_TURN + 3 * i
                pe.wait_ge(m_xlo, 4 * i + 8)
                pe.wait_ge(m_silu, i + 1)
                up(turn_, 0)
                h_columns(i)
                for c in range(1, 4):
                    up(turn_, c)
                pe.wait_ge(m_hlo, i + 1)
                for c in range(4, NW):
                    up(turn_, c)
                    if more and c >= 6:
                        x_columns(i + 2, c - 6)
                pe.wait_ge(m_y, 4 * i + FREE_BANK)
                for f in range(KF):
                    down(turn_, NW + f, f)
                    if more and f < 2:
                        x_columns(i + 2, f + 2)

            with pe.Fori(0, E - 2) as i:
                expert(i, True)
            expert(E - 2, False)
            h_columns(E - 1)
            pe.wait_ge(m_hlo, E)
            pe.wait_ge(m_y, 4 * (E - 1) + FREE_BANK)
            for f in range(KF):
                down(LAST_TURN, f, f)
            pe.wait_ge(count_ready, 1)
            n = pe.value_load(n_extra[0:1, 0:1], min_val=0, max_val=EXTRA)
            with pe.Fori(0, EXTRA) as i:
                with pe.If(i < n):
                    turn_ = EXTRA_TURN + 3 * i
                    for q in range(4):
                        x_columns(i + E, q)
                    pe.wait_ge(m_xlo, 4 * i + (4 * E + 4))
                    pe.wait_ge(m_silu, i + E)
                    for c in range(4):
                        up(turn_, c)
                    pe.wait_ge(m_hlo, i + E)
                    for c in range(4, NW):
                        up(turn_, c)
                    h_columns(i + E)
                    pe.wait_ge(m_hlo, i + E + 1)
                    pe.wait_ge(m_y, 4 * i + (4 * E + FREE_BANK))
                    for f in range(KF):
                        down(turn_, NW + f, f)


INPUTS = ["x", "norm_mix", "w_in", "pool_w", "pool_scale", "sgu_ln_g", "sgu_ln_b", "sgu_w", "sgu_b",
          "conv_dw_w", "conv_dw_b", "conv_ln_g", "conv_ln_b", "conv_pw", "w_out", "norm_ffn",
          "router_g_w", "router_g_b", "router_e_w", "router_e_b", "exp_w1", "exp_w3", "exp_w2",
          "norm_final"]


def kernel(**inputs):
    import numpy as np
    from concourse import bacc
    from concourse.bass_utils import run_bass_kernel_spmd

    nc = bacc.Bacc("TRN2", target_bir_lowering=False, num_devices=1, dynamic_dma_scratch_size=8192)
    arrays, args = {}, []
    for name in INPUTS:
        a = np.ascontiguousarray(inputs[name])
        arrays[f"in_{name}"] = a
        args.append(nc.dram_tensor(f"in_{name}", a.shape, mybir.dt.from_np(a.dtype), kind="ExternalInput").ap())
    result = nc.dram_tensor("result", (1, S, D), F32, kind="ExternalOutput").ap()
    build(nc, *args, result)
    ran = run_bass_kernel_spmd(nc, [arrays], core_ids=[0])
    return ran.results[0]["result"]
```
